# Optimizing a Trainium2 kernel written in Bass

```python
import jax, jax.numpy as jnp
from jax import lax
import numpy as np

D_MODEL = 1024
BATCH = 1
SEQ = 256
DEPTH = 2

HEAD_DIM = 64
NSA_HEADS = 8
NSA_KV_HEADS = 2
NSA_GROUP = NSA_HEADS // NSA_KV_HEADS
MOBA_HEADS = 8
MIX_WIDTH = (NSA_HEADS + MOBA_HEADS) * HEAD_DIM
ROT_DIM = HEAD_DIM // 4
ROPE_THETA = 500000.0
CMP_LEN = 32
CMP_STRIDE = 16
CMP_HIDDEN = 256
SLC_BLOCK = 64
SLC_TOPN = 16
WINDOW = 512
MOBA_BLOCK = 256
MOBA_TOPK = 3
Q_BLOCK = 128
SLC_CHUNK = 128
MOBA_CHUNK = 32
D_FF = 2816
EPS = 1e-6
NEG = -1e30
FORCE_BONUS = 1e4

NSA_Q_COLS = NSA_HEADS * HEAD_DIM
NSA_KV_COLS = 3 * 2 * NSA_KV_HEADS * HEAD_DIM
NSA_GATE_COLS = NSA_HEADS * 3
MOBA_COLS = 3 * MOBA_HEADS * HEAD_DIM
IN_COLS = NSA_Q_COLS + NSA_KV_COLS + NSA_GATE_COLS + MOBA_COLS


def rms_norm(x, g):
    xf = x.astype(jnp.float32)
    y = xf * lax.rsqrt(jnp.mean(xf * xf, axis=-1, keepdims=True) + EPS)
    return (y * g.astype(jnp.float32)).astype(x.dtype)

def swiglu(x, w_gate, w_up, w_down):
    return (jax.nn.silu(x @ w_gate) * (x @ w_up)) @ w_down

def rope_tables(S):
    inv_freq = jnp.power(ROPE_THETA, -(jnp.arange(0, ROT_DIM, 2, dtype=jnp.float32) / ROT_DIM))
    ang = jnp.arange(S, dtype=jnp.float32)[:, None] * inv_freq[None, :]
    return jnp.cos(ang), jnp.sin(ang)

def apply_partial_rope(x, cos, sin):
    half = ROT_DIM // 2
    cos = cos.astype(x.dtype)
    sin = sin.astype(x.dtype)
    x1 = x[..., :half]
    x2 = x[..., half:ROT_DIM]
    return jnp.concatenate([x1 * cos - x2 * sin, x2 * cos + x1 * sin, x[..., ROT_DIM:]], axis=-1)

def masked_softmax(s, valid):
    s = jnp.where(valid, s.astype(jnp.float32), NEG)
    m = jnp.max(s, axis=-1, keepdims=True)
    p = jnp.where(valid, jnp.exp(s - m), 0.0)
    return p / jnp.maximum(jnp.sum(p, axis=-1, keepdims=True), 1.0)

def nsa_mixer(q, k_cmp, v_cmp, k_slc, v_slc, k_win, v_win, gates,
              pos_ck, w_ck1, w_ck2, pos_cv, w_cv1, w_cv2, cos, sin):
    B, G, R, S, Dh = q.shape
    scale = Dh ** -0.5
    t = jnp.arange(S)
    q_rot = apply_partial_rope(q, cos, sin)
    k_slc = apply_partial_rope(k_slc, cos, sin)
    k_win = apply_partial_rope(k_win, cos, sin)

    n_cmp = (S - CMP_LEN) // CMP_STRIDE + 1
    starts = jnp.arange(n_cmp) * CMP_STRIDE
    cidx = starts[:, None] + jnp.arange(CMP_LEN)[None, :]

    def compress(k, pos, w1, w2):
        blocks = k[:, :, cidx, :] + pos
        flat = blocks.reshape(B, G, n_cmp, CMP_LEN * Dh)
        return jax.nn.gelu(flat @ w1) @ w2

    kc = compress(k_cmp, pos_ck, w_ck1, w_ck2)
    vc = compress(v_cmp, pos_cv, w_cv1, w_cv2)
    s_c = jnp.einsum('bgrqd,bgnd->bgrqn', q, kc) * scale
    valid_c = (starts + CMP_LEN - 1)[None, :] <= t[:, None]
    p_c = masked_softmax(s_c, valid_c)
    o_cmp = jnp.einsum('bgrqn,bgnd->bgrqd', p_c.astype(vc.dtype), vc)

    n_slc = S // SLC_BLOCK
    top_n = min(SLC_TOPN, n_slc)
    sb = jnp.arange(n_slc) * SLC_BLOCK
    overlap = ((starts[:, None] < (sb + SLC_BLOCK)[None, :]) &
               ((starts + CMP_LEN)[:, None] > sb[None, :])).astype(jnp.float32)
    imp = jnp.einsum('bgrqn,nj->bgqj', p_c, overlap)
    qblk = t // SLC_BLOCK
    j = jnp.arange(n_slc)
    forced = (j[None, :] == 0) | (j[None, :] == qblk[:, None]) | (j[None, :] == qblk[:, None] - 1)
    visible = sb[None, :] <= t[:, None]
    score = jnp.where(visible, jnp.where(forced, FORCE_BONUS, imp), NEG)
    sel_idx = lax.top_k(score, top_n)[1]

    ks_blocks = k_slc.reshape(B, G, n_slc, SLC_BLOCK, Dh)
    vs_blocks = v_slc.reshape(B, G, n_slc, SLC_BLOCK, Dh)
    bi = jnp.arange(B)[:, None, None, None]
    gi = jnp.arange(G)[None, :, None, None]

    def slc_chunk(c):
        q0 = c * SLC_CHUNK
        qc = lax.dynamic_slice_in_dim(q_rot, q0, SLC_CHUNK, axis=3)
        ic = lax.dynamic_slice_in_dim(sel_idx, q0, SLC_CHUNK, axis=2)
        kg = ks_blocks[bi, gi, ic]
        vg = vs_blocks[bi, gi, ic]
        s = jnp.einsum('bgrqd,bgqnld->bgrqnl', qc, kg) * scale
        kpos = ic[..., None] * SLC_BLOCK + jnp.arange(SLC_BLOCK)
        tq = q0 + jnp.arange(SLC_CHUNK)
        valid = (kpos <= tq[None, None, :, None, None]).reshape(B, G, 1, SLC_CHUNK, top_n * SLC_BLOCK)
        p = masked_softmax(s.reshape(B, G, R, SLC_CHUNK, top_n * SLC_BLOCK), valid)
        p = p.reshape(B, G, R, SLC_CHUNK, top_n, SLC_BLOCK).astype(vg.dtype)
        return jnp.einsum('bgrqnl,bgqnld->bgrqd', p, vg)

    o_slc = lax.map(slc_chunk, jnp.arange(S // SLC_CHUNK))
    o_slc = jnp.moveaxis(o_slc, 0, 3).reshape(B, G, R, S, Dh)

    n_qb = S // Q_BLOCK
    kw_pad = jnp.pad(k_win, ((0, 0), (0, 0), (WINDOW, 0), (0, 0)))
    vw_pad = jnp.pad(v_win, ((0, 0), (0, 0), (WINDOW, 0), (0, 0)))
    widx = jnp.arange(n_qb)[:, None] * Q_BLOCK + jnp.arange(WINDOW + Q_BLOCK)[None, :]
    kw = kw_pad[:, :, widx]
    vw = vw_pad[:, :, widx]
    qw = q_rot.reshape(B, G, R, n_qb, Q_BLOCK, Dh)
    s_w = jnp.einsum('bgrcqd,bgckd->bgrcqk', qw, kw) * scale
    kpos = widx - WINDOW
    tq = jnp.arange(n_qb)[:, None] * Q_BLOCK + jnp.arange(Q_BLOCK)[None, :]
    diff = tq[:, :, None] - kpos[:, None, :]
    valid_w = (diff >= 0) & (diff < WINDOW) & (kpos[:, None, :] >= 0)
    p_w = masked_softmax(s_w, valid_w).astype(vw.dtype)
    o_win = jnp.einsum('bgrcqk,bgckd->bgrcqd', p_w, vw).reshape(B, G, R, S, Dh)

    g = jax.nn.sigmoid(gates)
    return g[..., 0:1] * o_cmp + g[..., 1:2] * o_slc + g[..., 2:3] * o_win

def moba_mixer(q, k, v, cos, sin):
    B, H, S, Dh = q.shape
    scale = Dh ** -0.5
    q = apply_partial_rope(q, cos, sin)
    k = apply_partial_rope(k, cos, sin)
    n_blk = -(-S // MOBA_BLOCK)
    pad = n_blk * MOBA_BLOCK - S
    kb = jnp.pad(k, ((0, 0), (0, 0), (0, pad), (0, 0))).reshape(B, H, n_blk, MOBA_BLOCK, Dh)
    vb = jnp.pad(v, ((0, 0), (0, 0), (0, pad), (0, 0))).reshape(B, H, n_blk, MOBA_BLOCK, Dh)
    k_mean = jnp.mean(kb.astype(jnp.float32), axis=3)
    t = jnp.arange(S)
    qblk = t // MOBA_BLOCK
    past = jnp.arange(n_blk)[None, :] < qblk[:, None]
    gate = jnp.einsum('bhqd,bhnd->bhqn', q.astype(jnp.float32), k_mean)
    gate = jnp.where(past, gate, NEG)
    kk = max(min(MOBA_TOPK, n_blk - 1), 1)
    idx = lax.top_k(gate, kk)[1]
    sel_valid = idx < qblk[None, None, :, None]
    bi = jnp.arange(B)[:, None, None, None]
    hi = jnp.arange(H)[None, :, None, None]

    def chunk(c):
        q0 = c * MOBA_CHUNK
        qc = lax.dynamic_slice_in_dim(q, q0, MOBA_CHUNK, axis=2)
        ic = lax.dynamic_slice_in_dim(idx, q0, MOBA_CHUNK, axis=2)
        vc_ = lax.dynamic_slice_in_dim(sel_valid, q0, MOBA_CHUNK, axis=2)
        kg = kb[bi, hi, ic]
        vg = vb[bi, hi, ic]
        s_past = jnp.einsum('bhqd,bhqnld->bhqnl', qc, kg).reshape(B, H, MOBA_CHUNK, kk * MOBA_BLOCK)
        own = q0 // MOBA_BLOCK
        ko = lax.dynamic_index_in_dim(kb, own, axis=2, keepdims=False)
        vo = lax.dynamic_index_in_dim(vb, own, axis=2, keepdims=False)
        s_own = jnp.einsum('bhqd,bhld->bhql', qc, ko)
        tq = q0 + jnp.arange(MOBA_CHUNK)
        own_valid = (own * MOBA_BLOCK + jnp.arange(MOBA_BLOCK))[None, :] <= tq[:, None]
        valid = jnp.concatenate([
            jnp.broadcast_to(vc_[..., None], (B, H, MOBA_CHUNK, kk, MOBA_BLOCK)).reshape(B, H, MOBA_CHUNK, kk * MOBA_BLOCK),
            jnp.broadcast_to(own_valid, (B, H, MOBA_CHUNK, MOBA_BLOCK))], axis=-1)
        s = jnp.concatenate([s_past, s_own], axis=-1) * scale
        p = masked_softmax(s, valid).astype(vg.dtype)
        p_past = p[..., :kk * MOBA_BLOCK].reshape(B, H, MOBA_CHUNK, kk, MOBA_BLOCK)
        p_own = p[..., kk * MOBA_BLOCK:]
        return (jnp.einsum('bhqnl,bhqnld->bhqd', p_past, vg) +
                jnp.einsum('bhql,bhld->bhqd', p_own, vo))

    o = lax.map(chunk, jnp.arange(S // MOBA_CHUNK))
    return jnp.moveaxis(o, 0, 2).reshape(B, H, S, Dh)

def hybrid_mixer(h, w_in, pos_ck, w_ck1, w_ck2, pos_cv, w_cv1, w_cv2, w_out, cos, sin):
    B, S, _ = h.shape
    G, R, Dh = NSA_KV_HEADS, NSA_GROUP, HEAD_DIM
    proj = h @ w_in
    q_n, kv_n, gate_n, moba = jnp.split(
        proj, [NSA_Q_COLS, NSA_Q_COLS + NSA_KV_COLS, NSA_Q_COLS + NSA_KV_COLS + NSA_GATE_COLS], axis=-1)
    q_n = q_n.reshape(B, S, G, R, Dh).transpose(0, 2, 3, 1, 4)
    kv_n = kv_n.reshape(B, S, 6, G, Dh).transpose(2, 0, 3, 1, 4)
    gate_n = gate_n.reshape(B, S, G, R, 3).transpose(0, 2, 3, 1, 4)
    o_nsa = nsa_mixer(q_n, kv_n[0], kv_n[1], kv_n[2], kv_n[3], kv_n[4], kv_n[5], gate_n,
                      pos_ck, w_ck1, w_ck2, pos_cv, w_cv1, w_cv2, cos, sin)
    o_nsa = o_nsa.transpose(0, 3, 1, 2, 4).reshape(B, S, NSA_HEADS * Dh)
    qkv_m = moba.reshape(B, S, 3, MOBA_HEADS, Dh).transpose(2, 0, 3, 1, 4)
    o_moba = moba_mixer(qkv_m[0], qkv_m[1], qkv_m[2], cos, sin)
    o_moba = o_moba.transpose(0, 2, 1, 3).reshape(B, S, MOBA_HEADS * Dh)
    return jnp.concatenate([o_nsa, o_moba], axis=-1) @ w_out

def first_inputs(seed: int = 0) -> dict:
    key = jax.random.key(seed)
    ks = jax.random.split(key, 19)

    def w(k, shape, fan_in):
        return jax.random.normal(k, shape, jnp.float32) * fan_in ** -0.5

    def gain(k, shape):
        return 1.0 + 0.02 * jax.random.normal(k, shape, jnp.float32)

    return {
        "x": jax.random.normal(ks[0], (BATCH, SEQ, D_MODEL), jnp.float32),
        "norm_ffn1": gain(ks[1], (DEPTH, D_MODEL)),
        "w_ffn1_gate": w(ks[2], (DEPTH, D_MODEL, D_FF), D_MODEL),
        "w_ffn1_up": w(ks[3], (DEPTH, D_MODEL, D_FF), D_MODEL),
        "w_ffn1_down": w(ks[4], (DEPTH, D_FF, D_MODEL), D_FF),
        "norm_mix": gain(ks[5], (DEPTH, D_MODEL)),
        "w_in": w(ks[6], (DEPTH, D_MODEL, IN_COLS), D_MODEL),
        "pos_ck": 0.1 * jax.random.normal(ks[7], (DEPTH, CMP_LEN, HEAD_DIM), jnp.float32),
        "w_ck1": w(ks[8], (DEPTH, CMP_LEN * HEAD_DIM, CMP_HIDDEN), CMP_LEN * HEAD_DIM),
        "w_ck2": w(ks[9], (DEPTH, CMP_HIDDEN, HEAD_DIM), CMP_HIDDEN),
        "pos_cv": 0.1 * jax.random.normal(ks[10], (DEPTH, CMP_LEN, HEAD_DIM), jnp.float32),
        "w_cv1": w(ks[11], (DEPTH, CMP_LEN * HEAD_DIM, CMP_HIDDEN), CMP_LEN * HEAD_DIM),
        "w_cv2": w(ks[12], (DEPTH, CMP_HIDDEN, HEAD_DIM), CMP_HIDDEN),
        "w_out": w(ks[13], (DEPTH, MIX_WIDTH, D_MODEL), MIX_WIDTH),
        "norm_ffn2": gain(ks[14], (DEPTH, D_MODEL)),
        "w_ffn2_gate": w(ks[15], (DEPTH, D_MODEL, D_FF), D_MODEL),
        "w_ffn2_up": w(ks[16], (DEPTH, D_MODEL, D_FF), D_MODEL),
        "w_ffn2_down": w(ks[17], (DEPTH, D_FF, D_MODEL), D_FF),
        "norm_final": gain(ks[18], (D_MODEL,)),
    }

def first_block(x, norm_ffn1, w_ffn1_gate, w_ffn1_up, w_ffn1_down, norm_mix, w_in,
              pos_ck, w_ck1, w_ck2, pos_cv, w_cv1, w_cv2, w_out,
              norm_ffn2, w_ffn2_gate, w_ffn2_up, w_ffn2_down, norm_final):
    cos, sin = rope_tables(x.shape[1])
    for l in range(DEPTH):
        x = x + 0.5 * swiglu(rms_norm(x, norm_ffn1[l]), w_ffn1_gate[l], w_ffn1_up[l], w_ffn1_down[l])
        x = x + hybrid_mixer(rms_norm(x, norm_mix[l]), w_in[l], pos_ck[l], w_ck1[l], w_ck2[l],
                             pos_cv[l], w_cv1[l], w_cv2[l], w_out[l], cos, sin)
        x = x + 0.5 * swiglu(rms_norm(x, norm_ffn2[l]), w_ffn2_gate[l], w_ffn2_up[l], w_ffn2_down[l])
    return rms_norm(x, norm_final)


RW_HEADS = 8
RW_HEAD_DIM = 64
RW_WIDTH = RW_HEADS * RW_HEAD_DIM
RW_DECAY_RANK = 64
RW_ICLR_RANK = 64
RW_GATE_RANK = 128
RW_COLS = 3 * RW_WIDTH + RW_DECAY_RANK + RW_ICLR_RANK + RW_GATE_RANK
RW_GN_EPS = 64e-5
RET_HEADS = 4
RET_QK_DIM = 64
RET_V_DIM = 128
RET_QK_WIDTH = RET_HEADS * RET_QK_DIM
RET_V_WIDTH = RET_HEADS * RET_V_DIM
RET_COLS = 2 * RET_QK_WIDTH + 2 * RET_V_WIDTH
RET_CHUNK = 128
ROPE_BASE = 10000.0
SG_GROUPS = 4
SG_CHUNK = 128
SG_WIDTH = 512
SG_GROUP_DIM = SG_WIDTH // SG_GROUPS
SG_COLS = 2 * SG_WIDTH
N_BRANCH = 3
BRANCH_WIDTH = 512
GATE_COLS = N_BRANCH * D_MODEL
IN_COLS_2 = RW_COLS + RET_COLS + SG_COLS + GATE_COLS
CONV_WIDTH = 3


def rmsnorm(x, g):
    xf = x.astype(jnp.float32)
    y = xf * lax.rsqrt(jnp.mean(xf * xf, axis=-1, keepdims=True) + EPS) * g.astype(jnp.float32)
    return y.astype(x.dtype)

def rwkv7_scan(r, w, k, v, kk, a):
    B, S, H, N = r.shape

    def step(state, inp):
        r_t, w_t, k_t, v_t, kk_t, a_t = inp
        sa = jnp.einsum('bhvk,bhk->bhv', state, -kk_t)
        state = (state * w_t[:, :, None, :]
                 + sa[..., None] * (kk_t * a_t)[:, :, None, :]
                 + v_t[..., None] * k_t[:, :, None, :])
        y = jnp.einsum('bhvk,bhk->bhv', state, r_t)
        return state, y

    xs = tuple(jnp.moveaxis(t.astype(jnp.float32), 1, 0) for t in (r, w, k, v, kk, a))
    s0 = jnp.zeros((B, H, N, N), jnp.float32)
    _, ys = lax.scan(step, s0, xs)
    return jnp.moveaxis(ys, 0, 1)

def rwkv7_branch(p, mu, w0, w_up, a0, a_up, g_up, k_k, k_a, r_k, lnx_g, lnx_b):
    B, S, _ = p.shape
    p_prev = jnp.pad(p, ((0, 0), (1, 0), (0, 0)))[:, :S]
    p = p + mu * (p_prev - p)
    cuts = [RW_WIDTH, 2 * RW_WIDTH, 3 * RW_WIDTH, 3 * RW_WIDTH + RW_DECAY_RANK,
            3 * RW_WIDTH + RW_DECAY_RANK + RW_ICLR_RANK]
    r, k, v, wd, ad, gd = jnp.split(p, cuts, axis=-1)
    w = -jax.nn.softplus(-(w0 + jnp.tanh(wd) @ w_up)) - 0.5
    decay = jnp.exp(-jnp.exp(w.astype(jnp.float32)))
    a = jax.nn.sigmoid(a0 + ad @ a_up)
    g = jax.nn.sigmoid(gd) @ g_up
    kk = (k * k_k).astype(jnp.float32)
    k = k * (1.0 + (a - 1.0) * k_a)

    def heads(t):
        return t.reshape(B, S, RW_HEADS, RW_HEAD_DIM)

    r, k, v, decay, a, kk = map(heads, (r, k, v, decay, a, kk))
    kk = kk / jnp.maximum(jnp.sqrt(jnp.sum(kk * kk, axis=-1, keepdims=True)), 1e-12)
    y = rwkv7_scan(r, decay, k, v, kk, a)
    mean = jnp.mean(y, axis=-1, keepdims=True)
    var = jnp.mean(jnp.square(y - mean), axis=-1, keepdims=True)
    y = (y - mean) * lax.rsqrt(var + RW_GN_EPS) * lnx_g + lnx_b
    y = y + jnp.sum(r * k * r_k, axis=-1, keepdims=True) * v
    return (y.reshape(B, S, RW_WIDTH) * g).astype(p.dtype)

def rotary(t, cos, sin):
    t1, t2 = jnp.split(t, 2, axis=-1)
    c = cos[None, :, None, :]
    s = sin[None, :, None, :]
    return jnp.concatenate([t1 * c - t2 * s, t2 * c + t1 * s], axis=-1)

def retention_branch(p, cos, sin):
    B, S, _ = p.shape
    nC = S // RET_CHUNK
    q, k, v, g = jnp.split(p, [RET_QK_WIDTH, 2 * RET_QK_WIDTH, 2 * RET_QK_WIDTH + RET_V_WIDTH], axis=-1)
    q = rotary(q.reshape(B, S, RET_HEADS, RET_QK_DIM), cos, sin)
    k = rotary(k.reshape(B, S, RET_HEADS, RET_QK_DIM), cos, sin) * (RET_QK_DIM ** -0.5)
    v = v.reshape(B, S, RET_HEADS, RET_V_DIM)

    def chunks(t):
        return t.reshape(B, nC, RET_CHUNK, RET_HEADS, t.shape[-1]).transpose(0, 3, 1, 2, 4)

    qc, kc, vc = chunks(q), chunks(k), chunks(v)
    log_gamma = jnp.log(1.0 - 2.0 ** (-5.0 - jnp.arange(RET_HEADS, dtype=jnp.float32)))
    pos = jnp.arange(RET_CHUNK, dtype=jnp.float32)
    diff = pos[:, None] - pos[None, :]
    decay_in = jnp.where(diff[None] >= 0,
                         jnp.exp(jnp.maximum(diff, 0.0)[None] * log_gamma[:, None, None]), 0.0)
    scores = jnp.einsum('bhnid,bhnjd->bhnij', qc, kc) * decay_in[:, None]
    inner = jnp.einsum('bhnij,bhnje->bhnie', scores, vc)
    k_dec = jnp.exp((RET_CHUNK - 1.0 - pos)[None] * log_gamma[:, None])
    kv = jnp.einsum('bhnjd,bhnje,hj->nbhde', kc, vc, k_dec).astype(jnp.float32)
    chunk_decay = jnp.exp(RET_CHUNK * log_gamma)[None, :, None, None]

    def step(R, kv_n):
        return R * chunk_decay + kv_n, R

    _, R_prev = lax.scan(step, jnp.zeros((B, RET_HEADS, RET_QK_DIM, RET_V_DIM), jnp.float32), kv)
    q_dec = jnp.exp((pos + 1.0)[None] * log_gamma[:, None])
    cross = jnp.einsum('bhnid,nbhde,hi->bhnie', qc, R_prev, q_dec)
    y = (inner + cross).transpose(0, 2, 3, 1, 4).reshape(B, S, RET_HEADS, RET_V_DIM)
    y = y * lax.rsqrt(jnp.mean(y * y, axis=-1, keepdims=True) + EPS)
    return (y.reshape(B, S, RET_V_WIDTH) * jax.nn.silu(g)).astype(p.dtype)

def sgu_branch(p, ln_g, ln_b, w_s, b_s):
    B, S, _ = p.shape
    nC = S // SG_CHUNK
    z = jax.nn.gelu(p, approximate=False)
    u, v = jnp.split(z, 2, axis=-1)
    vf = v.astype(jnp.float32)
    mean = jnp.mean(vf, axis=-1, keepdims=True)
    var = jnp.mean(jnp.square(vf - mean), axis=-1, keepdims=True)
    v = ((vf - mean) * lax.rsqrt(var + EPS) * ln_g + ln_b).astype(p.dtype)
    vc = v.reshape(B, nC, SG_CHUNK, SG_GROUPS, SG_GROUP_DIM)
    causal = jnp.tril(jnp.ones((SG_CHUNK, SG_CHUNK), dtype=bool))
    w = jnp.where(causal[None], w_s, 0.0)
    mixed = jnp.einsum('gij,bnjgd->bnigd', w, vc) + b_s.T[:, :, None]
    return u * mixed.reshape(B, S, SG_WIDTH)

def conv_ffn(h, w_up, conv_w, conv_b, w_down):
    S = h.shape[1]
    u = h @ w_up
    up = jnp.pad(u, ((0, 0), (CONV_WIDTH - 1, 0), (0, 0)))
    c = conv_b
    for j in range(CONV_WIDTH):
        c = c + conv_w[j] * up[:, j:j + S]
    gate, val = jnp.split(c, 2, axis=-1)
    return (jax.nn.silu(gate) * val) @ w_down

def _normal(k, shape, scale):
    return scale * jax.random.normal(k, shape, jnp.float32)

def second_inputs(seed: int = 0) -> dict:
    key = jax.random.key(seed)
    ks = jax.random.split(key, 32)
    L = DEPTH
    f32 = jnp.float32
    return {
        "x": jax.random.normal(ks[0], (BATCH, SEQ, D_MODEL), f32),
        "norm1_g": 1.0 + _normal(ks[1], (L, D_MODEL), 0.05),
        "w_in": _normal(ks[2], (L, D_MODEL, IN_COLS_2), D_MODEL ** -0.5),
        "rw_mu": jax.random.uniform(ks[3], (L, RW_COLS), f32),
        "rw_w0": jax.random.uniform(ks[4], (L, RW_WIDTH), f32, -6.0, 1.0),
        "rw_w_up": _normal(ks[5], (L, RW_DECAY_RANK, RW_WIDTH), 0.1 * RW_DECAY_RANK ** -0.5),
        "rw_a0": _normal(ks[6], (L, RW_WIDTH), 0.1),
        "rw_a_up": _normal(ks[7], (L, RW_ICLR_RANK, RW_WIDTH), 0.3 * RW_ICLR_RANK ** -0.5),
        "rw_g_up": _normal(ks[8], (L, RW_GATE_RANK, RW_WIDTH), RW_GATE_RANK ** -0.5),
        "rw_k_k": 0.85 + _normal(ks[9], (L, RW_WIDTH), 0.05),
        "rw_k_a": 1.0 + _normal(ks[10], (L, RW_WIDTH), 0.05),
        "rw_r_k": _normal(ks[11], (L, RW_HEADS, RW_HEAD_DIM), 0.1),
        "rw_lnx_g": 1.0 + _normal(ks[12], (L, RW_HEADS, RW_HEAD_DIM), 0.05),
        "rw_lnx_b": _normal(ks[13], (L, RW_HEADS, RW_HEAD_DIM), 0.02),
        "sg_ln_g": 1.0 + _normal(ks[14], (L, SG_WIDTH), 0.05),
        "sg_ln_b": _normal(ks[15], (L, SG_WIDTH), 0.02),
        "sg_w_s": _normal(ks[16], (L, SG_GROUPS, SG_CHUNK, SG_CHUNK), SG_CHUNK ** -0.5),
        "sg_b": 1.0 + _normal(ks[17], (L, SG_GROUPS, SG_CHUNK), 0.1),
        "w_branch": _normal(ks[18], (L, N_BRANCH, BRANCH_WIDTH, D_MODEL), BRANCH_WIDTH ** -0.5),
        "w_out": _normal(ks[19], (L, D_MODEL, D_MODEL), 0.5 * D_MODEL ** -0.5),
        "norm2_g": 1.0 + _normal(ks[20], (L, D_MODEL), 0.05),
        "ffn_w_up": _normal(ks[21], (L, D_MODEL, 2 * D_FF), D_MODEL ** -0.5),
        "ffn_conv_w": _normal(ks[22], (L, CONV_WIDTH, 2 * D_FF), CONV_WIDTH ** -0.5),
        "ffn_conv_b": _normal(ks[23], (L, 2 * D_FF), 0.02),
        "ffn_w_down": _normal(ks[24], (L, D_FF, D_MODEL), 0.5 * D_FF ** -0.5),
        "final_g": 1.0 + _normal(ks[25], (D_MODEL,), 0.05),
    }

def second_block(x, norm1_g, w_in, rw_mu, rw_w0, rw_w_up, rw_a0, rw_a_up, rw_g_up, rw_k_k, rw_k_a,
              rw_r_k, rw_lnx_g, rw_lnx_b, sg_ln_g, sg_ln_b, sg_w_s, sg_b, w_branch, w_out,
              norm2_g, ffn_w_up, ffn_conv_w, ffn_conv_b, ffn_w_down, final_g):
    B, S, _ = x.shape
    inv_freq = 1.0 / (ROPE_BASE ** jnp.linspace(0.0, 1.0, RET_QK_DIM // 2, dtype=jnp.float32))
    ang = jnp.arange(S, dtype=jnp.float32)[:, None] * inv_freq[None, :]
    cos, sin = jnp.cos(ang), jnp.sin(ang)
    in_cuts = [RW_COLS, RW_COLS + RET_COLS, RW_COLS + RET_COLS + SG_COLS]
    for l in range(DEPTH):
        h = rmsnorm(x, norm1_g[l])
        p = h @ w_in[l]
        p_rw, p_ret, p_sg, gate_logits = jnp.split(p, in_cuts, axis=-1)
        y_rw = rwkv7_branch(p_rw, rw_mu[l], rw_w0[l], rw_w_up[l], rw_a0[l], rw_a_up[l], rw_g_up[l],
                            rw_k_k[l], rw_k_a[l], rw_r_k[l], rw_lnx_g[l], rw_lnx_b[l])
        y_ret = retention_branch(p_ret, cos, sin)
        y_sg = sgu_branch(p_sg, sg_ln_g[l], sg_ln_b[l], sg_w_s[l], sg_b[l])
        branches = jnp.stack([y_rw, y_ret, y_sg], axis=2)
        proj = jnp.einsum('bsgc,gcd->bsgd', branches, w_branch[l])
        gates = jax.nn.sigmoid(gate_logits.reshape(B, S, N_BRANCH, D_MODEL))
        x = x + jnp.sum(gates * proj, axis=2) @ w_out[l]
        x = x + conv_ffn(rmsnorm(x, norm2_g[l]), ffn_w_up[l], ffn_conv_w[l], ffn_conv_b[l], ffn_w_down[l])
    return rmsnorm(x, final_g)


def setup_inputs(seed=0):
    out = dict(first_inputs(seed))
    for name, value in second_inputs(seed + 1).items():
        if name != "x":
            out[name + "_2"] = value
    return out


def reference(
    x, norm_ffn1, w_ffn1_gate, w_ffn1_up, w_ffn1_down, norm_mix, w_in, pos_ck, w_ck1, w_ck2,
    pos_cv, w_cv1, w_cv2, w_out, norm_ffn2, w_ffn2_gate, w_ffn2_up, w_ffn2_down, norm_final,
    norm1_g_2, w_in_2, rw_mu_2, rw_w0_2, rw_w_up_2, rw_a0_2, rw_a_up_2, rw_g_up_2, rw_k_k_2,
    rw_k_a_2, rw_r_k_2, rw_lnx_g_2, rw_lnx_b_2, sg_ln_g_2, sg_ln_b_2, sg_w_s_2, sg_b_2,
    w_branch_2, w_out_2, norm2_g_2, ffn_w_up_2, ffn_conv_w_2, ffn_conv_b_2, ffn_w_down_2,
    final_g_2,
):
    x = first_block(
        x, norm_ffn1, w_ffn1_gate, w_ffn1_up, w_ffn1_down, norm_mix, w_in, pos_ck, w_ck1, w_ck2,
        pos_cv, w_cv1, w_cv2, w_out, norm_ffn2, w_ffn2_gate, w_ffn2_up, w_ffn2_down, norm_final,
    )
    return second_block(
        x, norm1_g_2, w_in_2, rw_mu_2, rw_w0_2, rw_w_up_2, rw_a0_2, rw_a_up_2, rw_g_up_2,
        rw_k_k_2, rw_k_a_2, rw_r_k_2, rw_lnx_g_2, rw_lnx_b_2, sg_ln_g_2, sg_ln_b_2, sg_w_s_2,
        sg_b_2, w_branch_2, w_out_2, norm2_g_2, ffn_w_up_2, ffn_conv_w_2, ffn_conv_b_2,
        ffn_w_down_2, final_g_2,
    )


_drawn_inputs = setup_inputs


def setup_inputs(seed=0):
    import zlib

    import numpy as np

    out = dict(_drawn_inputs(seed))
    spreads = {}
    factors = {'norm_ffn1': 3.579,
     'norm_mix': 4.318,
     'pos_ck': 8.0,
     'norm_ffn2': 4.128,
     'rw_w_up_2': 8.0,
     'rw_a0_2': 6.018,
     'rw_k_k_2': 4.867,
     'rw_k_a_2': 4.236,
     'rw_lnx_g_2': 5.402,
     'rw_lnx_b_2': 8.0,
     'sg_ln_g_2': 6.443,
     'sg_ln_b_2': 23.897,
     'ffn_conv_b_2': 4.942,
     'sg_b_2': 3.03}
    for name, (base, spread) in spreads.items():
        noise = np.random.default_rng([zlib.crc32(name.encode()), seed]).standard_normal(out[name].shape)
        drawn = base * np.exp(spread * noise) if base else spread * noise
        out[name] = __import__('jax').numpy.asarray(drawn.astype(out[name].dtype))
    for name, factor in factors.items():
        out[name] = (out[name] * factor).astype(out[name].dtype)
    return out
```

```python
from contextlib import ExitStack

import concourse.bass as bass
import numpy as np
from concourse import mybir

F32 = mybir.dt.float32
ALU = mybir.AluOpType
ACT = mybir.ActivationFunctionType
AX = mybir.AxisListType.X

P = 128
D = 1024
KT = D // P
S = 256
NT = S // P
DEPTH = 2
D_FF = 2816
EPS = 1e-6
NEG = -1e30

DH = 64
NH = 8
GROUPS = 2
REP = NH // GROUPS
SCALE = DH**-0.5
Q_COLS = NH * DH
KV_COLS = 6 * GROUPS * DH
GATE_COLS = NH * 3
IN_COLS = Q_COLS + KV_COLS + GATE_COLS + 3 * Q_COLS
MOBA_OFF = Q_COLS + KV_COLS + GATE_COLS
ROT = DH // 4
CMP_LEN, CMP_STRIDE, CMP_HID = 32, 16, 256
N_CMP = (S - CMP_LEN) // CMP_STRIDE + 1
CJ = CMP_LEN * DH // P
FF_W = 2 * P
N_CHUNK = D_FF // FF_W


def constants():
    c = {}
    c["ident"] = np.eye(P, dtype=np.float32)
    half = ROT // 2
    inv = np.power(np.float32(500000.0), -(np.arange(0, ROT, 2, dtype=np.float32) / np.float32(ROT)))
    ang = np.arange(S, dtype=np.float32)[:, None] * inv.astype(np.float32)[None, :]
    cos, sin = np.ones((P, S), np.float32), np.zeros((P, S), np.float32)
    swap = np.zeros((P, P), np.float32)
    for base in (0, DH):
        for i in range(half):
            for d, src, sign in ((base + i, base + i + half, -1), (base + i + half, base + i, 1)):
                cos[d], sin[d] = np.cos(ang[:, i]), sign * np.sin(ang[:, i])
                swap[src, d] = 1
    c["swap"], c["cos"], c["sin"] = swap, cos, sin
    q, k = np.arange(P)[:, None], np.arange(S)[None, :]
    c["causal"] = np.where(k - P <= q, 0, NEG).astype(np.float32)
    t = (np.arange(NT)[None, :, None] * P + np.arange(P)[:, None, None])
    n = np.arange(16)[None, None, :]
    ok = (n < N_CMP) & (n * CMP_STRIDE + CMP_LEN - 1 <= t)
    c["cmp_neg"] = np.where(ok, 0, NEG).astype(np.float32).reshape(P, NT * 16)
    c["cmp_one"] = ok.astype(np.float32).reshape(P, NT * 16)
    c["head_of_row"] = (np.arange(P)[:, None] // 16 == np.arange(NH)[None, :]).astype(np.float32)
    c["eps"] = np.full((P, 1), EPS, np.float32)
    return c


def layout(c):
    at, place = 0, {}
    for name, a in c.items():
        place[name] = (at, a.shape[1])
        at += a.shape[1]
    return place, at


F32R = mybir.dt.float32r


def plain(ap):
    return ap.bitcast(F32)


def matmul3(pe, out, lhs, rhs, start, stop):
    pe.matmul(out, lhs[0], rhs[0], start=start, stop=False)
    pe.matmul(out, lhs[0], rhs[1], start=False, stop=False)
    return pe.matmul(out, lhs[1], rhs[0], start=False, stop=stop)


class Chip:
    pass


def norm_scalar(act, c, sumsq_ready, root_ready):
    for t in range(NT):
        act.activation(c.h[:, t, :], c.x[:, t, :], ACT.Square, accum_out=c.stat[:, t:t + 1]).then_inc(sumsq_ready, 1)
    act.wait_ge(sumsq_ready, NT)
    act.activation(c.stat[:, 2:4], c.stat[:, 0:2], ACT.Sqrt, bias=c.eps, scale=1.0 / D).then_inc(root_ready, 1)


def norm_vector(dve, c, root_ready, rstd_ready, h_ready):
    dve.wait_ge(root_ready, 1)
    dve.reciprocal(c.stat[:, 4:6], c.stat[:, 2:4]).then_inc(rstd_ready, 1)
    dve.wait_ge(rstd_ready, 1)
    for t in range(NT):
        dve.tensor_scalar(c.h[:, t, :], c.x[:, t, :], c.stat[:, 4 + t:5 + t], None, ALU.mult).then_inc(h_ready, 1)


def turn_tensor(pe, c, src, src_ready, turned):
    for t in range(NT):
        pe.wait_ge(src_ready, t + 1)
        for k in range(KT):
            bank = c.ps[2 * t + k // 4]
            last = pe.transpose(bank[:, (k % 4) * P:(k % 4 + 1) * P], src[:, t, k * P:(k + 1) * P], c.ident)
            if k % 4 == 3:
                last.then_inc(turned, 1)


def turn_vector(dve, c, dst, gain, turned, turned_copied):
    for b in range(2 * NT):
        t, k = b // 2, (b % 2) * 4
        dve.wait_ge(turned, b + 1)
        src = c.ps[b][:].rearrange("p (k n) -> p k n", k=4)
        out = dst[:, k:k + 4, t * P:(t + 1) * P]
        if gain is None:
            dve.tensor_copy(out, src).then_inc(turned_copied, 1)
        else:
            g = gain[:, k:k + 4].unsqueeze(2).to_broadcast([P, 4, P])
            dve.tensor_tensor(out, src, g, ALU.mult).then_inc(turned_copied, 1)


def semaphores(nc, phase, names):
    stack = ExitStack()
    sems = {n: stack.enter_context(nc.semaphore(f"{phase}_{n}")) for n in names.split()}
    nums = [x.num for x in sems.values()]

    def end_phase():
        nc.all_engine_barrier(sems_to_clear=range(min(nums), max(nums) + 1))
        stack.close()

    return sems, end_phase


def turned_high_scalar(act, c, high, gain, gain_loaded, turned, high_ready):
    act.wait_ge(gain_loaded, 16)
    for b in range(2 * NT):
        t, k0 = b // 2, (b % 2) * 4
        act.wait_ge(turned, b + 1)
        for k in range(k0, k0 + 4):
            last = act.activation(high[:, k, t * P:(t + 1) * P], c.ps[b][:, (k - k0) * P:(k - k0 + 1) * P], ACT.Copy,
                                  scale=gain[:, k:k + 1])
        last.then_inc(high_ready, 1)


def turned_low_vector(dve, c, high, low, gain, high_ready, ready):
    for b in range(2 * NT):
        t, k0 = b // 2, (b % 2) * 4
        dve.wait_ge(high_ready, b + 1)
        for k in range(k0, k0 + 4):
            toks = slice(t * P, (t + 1) * P)
            last = dve.scalar_tensor_tensor(low[:, k, toks], c.ps[b][:, (k - k0) * P:(k - k0 + 1) * P], gain[:, k:k + 1],
                                            plain(high[:, k, toks]), ALU.mult, ALU.subtract)
        last.then_inc(ready, 1)


def ffn_phase(nc, c, phase, gain, weights, factor=0.5, conv=None):
    s, end_phase = semaphores(nc, phase, "gain_loaded sumsq_ready root_ready rstd_ready h_ready turned hT_high hT_ready "
                                         "gate0 gate1 up0 up1 down taps0 taps1 first_high gu_high gu_split "
                                         "down_high down_split hidden_ready started tap_step tapped silu_ready "
                                         "product_ready act_high act_ready down_done residual_done")
    gu_loaded = ((s["gate0"], s["gate1"]), (s["up0"], s["up1"]))
    taps_loaded = (s["taps0"], s["taps1"])
    PART = KT * FF_W
    ctx = ExitStack()

    def sb(name, shape, dtype=F32):
        return ctx.enter_context(nc.sbuf_tensor(f"{phase}_{name}", shape, dtype))

    arrived_gu = sb("arrived_gate_up", [P, 2, 2, PART])
    arrived_down = sb("arrived_down", [P, PART])
    parts = sb("split_weights", [P, 2, 3, 2, PART], F32R)
    hT_parts = sb("hT_split", [P, 2, KT, S], F32R)
    act_parts = sb("act_split", [P, 2, 2, 2, S], F32R)
    w = [[tuple(parts[:, lo, part, slot, :].rearrange("p (k n) -> p k n", k=2 if part == 2 else KT) for lo in range(2))
          for slot in range(2)] for part in range(3)]
    hT = (hT_parts[:, 0], hT_parts[:, 1])
    act_high, act_low = act_parts[:, 0], act_parts[:, 1]
    acts = c.work[:, 0:4 * S].rearrange("p (s f n) -> p s f n", s=2, f=2)
    if conv is not None:
        conv_buf = c.h[:].rearrange("p t (a b n) -> p t a b n", a=2, b=2)
        taps = sb("taps", [P, 2, CONV_W])
    acc = [[c.ps[4 + 2 * t + half] for half in range(2)] for t in range(NT)]
    LOOP0 = 3
    LOOPS = (N_CHUNK - LOOP0) // 2
    assert LOOP0 + 2 * LOOPS == N_CHUNK

    def tap(slot, which, f, j):
        at = (which * 2 + f) * 4 + j
        return taps[:, slot, at:at + 1]

    def arrived(part, slot):
        return arrived_down[:] if part == 2 else arrived_gu[:, part, slot]

    def flat(a):
        return a.rearrange("p k n -> p (k n)")

    with nc.Block() as block:
        @block.sync
        def _(sp):
            def load_gu(i, slot, reuse):
                for part in range(2):
                    if reuse:
                        sp.wait_ge(s["gu_split"], i * 2 - 3 + part)
                    sp.dma_start(arrived(part, slot), weights[bass.ds(i * (3 * P) + part * P, P), :]
                                 ).then_inc(gu_loaded[part][slot], 16)

            def load_down(i, slot, reuse):
                if reuse:
                    sp.wait_ge(s["down_split"], i)
                sp.dma_start(arrived(2, slot), weights[bass.ds(i * (3 * P) + 2 * P, P), :]).then_inc(s["down"], 16)

            def load_taps(i, slot, reuse):
                if conv is not None:
                    if reuse:
                        sp.wait_ge(s["act_ready"], i * 2 - 2)
                    sp.dma_start(taps[:, slot], conv[bass.ds(i * P, P), :]).then_inc(taps_loaded[slot], 16)

            sp.dma_start(c.gain[:, 0:KT], gain, allow_slow_non_contiguous=True).then_inc(s["gain_loaded"], 16)
            load_gu(0, 0, False)
            load_gu(1, 1, False)
            load_down(0, 0, False)
            load_taps(0, 0, False)
            load_taps(1, 1, False)
            load_gu(2, 0, True)
            load_down(1, 1, True)
            with sp.Fori(0, LOOPS) as i:
                for d, slot in ((0, 1), (1, 0)):
                    load_gu(i * 2 + LOOP0 + d, slot, True)
                    load_down(i * 2 + LOOP0 - 1 + d, 1 - slot, True)
                    load_taps(i * 2 + LOOP0 - 1 + d, 1 - slot, True)
            load_down(N_CHUNK - 1, 0, True)
            load_taps(N_CHUNK - 1, 0, True)

        @block.scalar
        def _(act):
            def high_gu(i, slot, n_loads, reuse):
                for part in range(2):
                    act.wait_ge(gu_loaded[part][slot], n_loads)
                    if reuse:
                        act.wait_ge(s["hidden_ready"], i * 2 - 2)
                    act.activation(flat(w[part][slot][0]), arrived(part, slot), ACT.Copy).then_inc(s["gu_high"], 1)

            def high_down(i, slot, reuse):
                act.wait_ge(s["down"], i * 16 + 16)
                if reuse:
                    act.wait_ge(s["down_done"], i - 1)
                act.activation(flat(w[2][slot][0]), arrived(2, slot), ACT.Copy).then_inc(s["down_high"], 1)

            def silu(i, slot):
                for f in range(2):
                    act.wait_ge(s["hidden_ready"], i * 2 + f + 1)
                    act.activation(acts[:, slot, f], c.ps[2 * slot + f][:, 0:S], ACT.Silu).then_inc(s["silu_ready"], 1)

            def newest_tap(i, slot, n_loads):
                act.wait_ge(taps_loaded[slot], n_loads)
                for f in range(2):
                    act.wait_ge(s["hidden_ready"], i * 2 + f + 1)
                    for which in range(2):
                        last = act.activation(conv_buf[:, slot, f, which], c.ps[2 * slot + f][:, which * S:(which + 1) * S],
                                              ACT.Identity, bias=tap(slot, which, f, 3), scale=tap(slot, which, f, 2))
                    last.then_inc(s["started"], 1)

            def silu_tapped(i, slot):
                for f in range(2):
                    act.wait_ge(s["tapped"], i * 2 + f + 1)
                    act.activation(acts[:, slot, f], conv_buf[:, slot, f, 0], ACT.Silu).then_inc(s["silu_ready"], 1)

            def step(i, slot, n_loads, reuse_down):
                if conv is None:
                    silu(i - 2, slot)
                    high_gu(i, slot, n_loads, True)
                    high_down(i - 1, 1 - slot, reuse_down)
                else:
                    newest_tap(i - 2, slot, n_loads - 16)
                    high_down(i - 1, 1 - slot, reuse_down)
                    silu_tapped(i - 2, slot)
                    high_gu(i, slot, n_loads, True)

            norm_scalar(act, c, s["sumsq_ready"], s["root_ready"])
            turned_high_scalar(act, c, hT[0], c.gain, s["gain_loaded"], s["turned"], s["hT_high"])
            act.wait_ge(s["up0"], 16)
            act.activation(flat(w[1][0][0]), arrived(1, 0), ACT.Copy).then_inc(s["gu_high"], 1)
            high_gu(1, 1, 16, False)
            high_down(0, 0, False)
            step(2, 0, 32, False)
            with act.Fori(0, LOOPS) as i:
                step(i * 2 + LOOP0, 1, i * 16 + 32, True)
                step(i * 2 + LOOP0 + 1, 0, i * 16 + 48, True)
            last_load = 16 * (N_CHUNK // 2)
            if conv is None:
                high_down(N_CHUNK - 1, 0, True)
                silu(N_CHUNK - 2, 1)
                silu(N_CHUNK - 1, 0)
            else:
                newest_tap(N_CHUNK - 2, 1, last_load)
                high_down(N_CHUNK - 1, 0, True)
                silu_tapped(N_CHUNK - 2, 1)
                newest_tap(N_CHUNK - 1, 0, last_load + 16)
                silu_tapped(N_CHUNK - 1, 0)

        @block.vector
        def _(dve):
            def low_part(i, slot, part):
                dve.wait_ge(s["gu_high"], i * 2 + part)
                high, low = w[part][slot]
                dve.tensor_tensor(flat(low), arrived(part, slot), plain(flat(high)), ALU.subtract).then_inc(s["gu_split"], 1)

            def low_gu(i, slot):
                for part in range(2):
                    low_part(i, slot, part)

            def low_down(i, slot):
                dve.wait_ge(s["down_high"], i + 1)
                high, low = w[2][slot]
                dve.tensor_tensor(flat(low), arrived(2, slot), plain(flat(high)), ALU.subtract).then_inc(s["down_split"], 1)

            def older_taps(i, slot):
                for f in range(2):
                    dve.wait_ge(s["started"], i * 2 + f + 1)
                    for shift in (1, 2):
                        if shift == 2:
                            dve.wait_ge(s["tap_step"], i * 2 + f + 1)
                        for which in range(2):
                            buf = conv_buf[:, slot, f, which, shift:]
                            last = dve.scalar_tensor_tensor(buf, c.ps[2 * slot + f][:, which * S:(which + 1) * S - shift],
                                                            tap(slot, which, f, 2 - shift), buf, ALU.mult, ALU.add)
                        last.then_inc(s["tap_step"] if shift == 1 else s["tapped"], 1)

            def product(i, slot):
                for f in range(2):
                    dve.wait_ge(s["silu_ready"], i * 2 + f + 1)
                    value, out = acts[:, slot, f], act_high[:, slot, f]
                    up = c.ps[2 * slot + f][:, S:2 * S] if conv is None else conv_buf[:, slot, f, 1]
                    dve.tensor_tensor(value, up, value, ALU.mult).then_inc(s["product_ready"], 1)
                    dve.wait_ge(s["product_ready"], i * 2 + f + 1)
                    dve.tensor_copy(out, value).then_inc(s["act_high"], 1)
                    dve.wait_ge(s["act_high"], i * 2 + f + 1)
                    dve.tensor_tensor(act_low[:, slot, f], value, plain(out), ALU.subtract).then_inc(s["act_ready"], 1)

            def step(i, slot):
                if conv is None:
                    product(i - 2, slot)
                    low_gu(i, slot)
                    low_down(i - 1, 1 - slot)
                else:
                    older_taps(i - 2, slot)
                    low_down(i - 1, 1 - slot)
                    product(i - 2, slot)
                    low_gu(i, slot)

            norm_vector(dve, c, s["root_ready"], s["rstd_ready"], s["h_ready"])
            dve.wait_ge(s["gate0"], 16)
            high, low = w[0][0]
            dve.tensor_copy(flat(high), arrived(0, 0)).then_inc(s["first_high"], 1)
            dve.wait_ge(s["first_high"], 1)
            dve.tensor_tensor(flat(low), arrived(0, 0), plain(flat(high)), ALU.subtract).then_inc(s["gu_split"], 1)
            turned_low_vector(dve, c, hT[0], hT[1], c.gain, s["hT_high"], s["hT_ready"])
            low_part(0, 0, 1)
            low_gu(1, 1)
            low_down(0, 0)
            step(2, 0)
            with dve.Fori(0, LOOPS) as i:
                step(i * 2 + LOOP0, 1)
                step(i * 2 + LOOP0 + 1, 0)
            if conv is None:
                low_down(N_CHUNK - 1, 0)
                product(N_CHUNK - 2, 1)
            else:
                older_taps(N_CHUNK - 2, 1)
                low_down(N_CHUNK - 1, 0)
                product(N_CHUNK - 2, 1)
                older_taps(N_CHUNK - 1, 0)
            product(N_CHUNK - 1, 0)
            dve.wait_ge(s["down_done"], N_CHUNK)
            for t in range(NT):
                for half in range(2):
                    cols = slice(half * 512, half * 512 + 512)
                    dve.scalar_tensor_tensor(c.x[:, t, cols], acc[t][half][:], factor, c.x[:, t, cols],
                                             ALU.mult, ALU.add).then_inc(s["residual_done"], 1)

        @block.tensor
        def _(pe):
            turn_tensor(pe, c, c.h, s["h_ready"], s["turned"])
            pe.wait_ge(s["hT_ready"], 2 * NT)

            def hidden(i, slot):
                for f in range(2):
                    bank = c.ps[2 * slot + f]
                    for part in range(2):
                        pe.wait_ge(s["gu_split"], i * 2 + part + 1)
                        high, low = w[part][slot]
                        for k in range(KT):
                            last = matmul3(pe, bank[:, part * S:(part + 1) * S],
                                           (high[:, k, f * P:(f + 1) * P], low[:, k, f * P:(f + 1) * P]),
                                           (hT[0][:, k, :], hT[1][:, k, :]), k == 0, k == KT - 1)
                    last.then_inc(s["hidden_ready"], 1)

            def down(i, slot, first=False, final=False):
                pe.wait_ge(s["down_split"], i + 1)
                high, low = w[2][slot]
                for f in range(2):
                    pe.wait_ge(s["act_ready"], i * 2 + f + 1)
                    for t in range(NT):
                        toks = slice(t * P, (t + 1) * P)
                        for half in range(2):
                            cols = slice(half * 512, half * 512 + 512)
                            last = matmul3(pe, acc[t][half][:], (act_high[:, slot, f, toks], act_low[:, slot, f, toks]),
                                           (high[:, f, cols], low[:, f, cols]), first and f == 0, final and f == 1)
                last.then_inc(s["down_done"], 1)

            hidden(0, 0)
            hidden(1, 1)
            down(0, 0, first=True)
            hidden(2, 0)
            down(1, 1)
            with pe.Fori(0, LOOPS) as i:
                hidden(i * 2 + LOOP0, 1)
                down(i * 2 + LOOP0 - 1, 0)
                hidden(i * 2 + LOOP0 + 1, 0)
                down(i * 2 + LOOP0, 1)
            down(N_CHUNK - 1, 0, final=True)
    end_phase()
    ctx.close()


def mixer_buffers(nc, ctx, c):
    def sb(name, shape):
        return ctx.enter_context(nc.sbuf_tensor(name, shape, F32))

    c.wc1 = sb("w_cmp1", [P, 2, CJ, CMP_HID])
    c.wc2 = sb("w_cmp2", [P, 2, 2, 2, DH])
    c.pos = sb("pos", [P, 2, CJ])
    c.raw = sb("raw", [P, N_TURNED, S])
    c.rot = sb("rot", [P, N_ROT, S])
    c.vtok = sb("v_tokens", [P, NT, 2 * P + Q_COLS])
    c.gates = sb("gates", [P, NT, GATE_COLS])
    c.kcols = c.h[:].rearrange("p t d -> p (t d)")[:, 0:2 * GROUPS * CJ * N_CMP].rearrange(
        "p (v g j n) -> p v g j n", v=2, g=GROUPS, j=CJ)
    hid_w = 2 * 2 * GROUPS * 16
    c.hid = c.work[:, 2 * S:2 * S + hid_w].rearrange("p (v f g n) -> p v f g n", v=2, f=2, g=GROUPS)
    c.hid_v = c.work[:, 2 * S + hid_w:2 * S + hid_w + 2 * NH * 16].rearrange("p (f g r n) -> p f g r n", f=2, g=GROUPS, r=REP)
    c.kc = sb("k_cmp", [P, GROUPS, 16])
    c.vc = sb("v_cmp_by_head", [P, NH, DH])


Q_T, KS_T, KW_T, MQ_T, MK_T = 0, 4, 5, 6, 10
N_ROT = 14
CMP_T = N_ROT
N_TURNED = N_ROT + 4

WI_CMP = 4 * P
WI_KEYS = WI_CMP + 4 * P
WI_VALUES = WI_KEYS + 2 * P
WI_MOBA = WI_VALUES + 2 * P + GATE_COLS
WI_MOBA_V = WI_MOBA + 2 * Q_COLS
W_IN = WI_MOBA_V + Q_COLS


def w_in_columns():
    def head(first, n):
        return list(range(first + n * DH, first + (n + 1) * DH))

    def kv(which):
        return Q_COLS + which * GROUPS * DH

    order = []
    for j in range(REP):
        order += head(0, j) + head(0, REP + j)
    for which in (0, 1):
        for g in range(GROUPS):
            order += head(kv(which), g) * 2
    for which in (2, 4, 3, 5):
        order += head(kv(which), 0) + head(kv(which), 1)
    order += range(kv(6), IN_COLS)
    assert len(order) == W_IN
    return order


def project_phase(nc, c, gain, w_in, pos, w_c1, w_c2):
    s, end_phase = semaphores(nc, "project", "gain_loaded w0 w1 w2 w3 pos_loaded wc1_loaded wc2_loaded sumsq_ready root_ready "
                            "rstd_ready h_ready turned hT_ready projected copied swapped swap_used cos_done "
                            "sin_done rotated kcols_ready pad_ready hid_ready gelu_ready repeated kv_ready kv_copied")
    w = c.arena[:, 0:KT * W_IN].rearrange("p (k n) -> p k n", k=KT)
    edges = [0, WI_CMP, WI_MOBA, WI_MOBA_V, W_IN]
    w_loaded = (s["w0"], s["w1"], s["w2"], s["w3"])

    jobs = [(0, "rotate", Q_T + j, j * P) for j in range(4)]
    jobs += [(1, "plain", CMP_T + j, WI_CMP + j * P) for j in range(4)]
    jobs += [(1, "rotate", KS_T, WI_KEYS), (1, "rotate", KW_T, WI_KEYS + P)]
    jobs += [(1, "tokens", t, WI_VALUES) for t in range(NT)]
    jobs += [(2, "rotate", MQ_T + j, WI_MOBA + j * P) for j in range(8)]
    jobs += [(3, "values", t, WI_MOBA_V) for t in range(NT)]
    rotated_jobs = [i for i, j in enumerate(jobs) if j[1] == "rotate"]
    cmp_done = max(i for i, j in enumerate(jobs) if j[1] == "plain") + 1
    hid_bank, kv_bank = c.ps[4], c.ps[5]

    with nc.Block() as block:
        @block.sync
        def _(sp):
            sp.dma_start(c.gain[:, 0:KT], gain, allow_slow_non_contiguous=True).then_inc(s["gain_loaded"], 16)
            for g in range(4):
                sp.dma_start(w[:, :, edges[g]:edges[g + 1]],
                             w_in[:, edges[g]:edges[g + 1]].rearrange("(k p) n -> p k n", p=P)).then_inc(w_loaded[g], 16)
                if g == 1:
                    for kv in range(2):
                        sp.dma_start(c.pos[:, kv, :], pos[kv].rearrange("(j u) d -> (u d) j", u=2),
                                     allow_slow_non_contiguous=True).then_inc(s["pos_loaded"], 16)
                        sp.dma_start(c.wc1[:, kv], w_c1[kv].rearrange("(j p) n -> p j n", p=P)).then_inc(s["wc1_loaded"], 16)
                        for u in range(2):
                            sp.dma_start(c.wc2[:, kv, :, u], w_c2[kv].rearrange("(j p) n -> p j n", p=P)).then_inc(s["wc2_loaded"], 16)

        @block.scalar
        def _(act):
            norm_scalar(act, c, s["sumsq_ready"], s["root_ready"])
            for i, (_, kind, to, _) in enumerate(jobs):
                bank = c.ps[i % 2]
                act.wait_ge(s["projected"], i + 1)
                if kind in ("rotate", "plain"):
                    last = act.activation(c.raw[:, to, :], bank[:, 0:S], ACT.Copy)
                elif kind == "tokens":
                    act.activation(c.gates[:, to, :], bank[:, 2 * P:2 * P + GATE_COLS], ACT.Sigmoid)
                    last = act.activation(c.vtok[:, to, 0:2 * P], bank[:, 0:2 * P], ACT.Copy)
                else:
                    last = act.activation(c.vtok[:, to, 2 * P:], bank[:, 0:Q_COLS], ACT.Copy)
                last.then_inc(s["copied"], 1)
            act.wait_ge(s["hid_ready"], 1)
            act.wait_ge(s["pad_ready"], 1)
            hid = hid_bank[:, 0:4 * GROUPS * 16].rearrange("p (v f g n) -> p (v f) g n", v=2, f=2, n=16)
            act.activation(c.hid.rearrange("p v f g n -> p (v f) g n")[:, :, :, 0:N_CMP], hid[:, :, :, 0:N_CMP],
                           ACT.Gelu_apprx_tanh).then_inc(s["gelu_ready"], 1)

        @block.gpsimd
        def _(pool):
            pool.memset(c.hid, 0.0).then_inc(s["pad_ready"], 1)
            for n, i in enumerate(rotated_jobs):
                to = jobs[i][2]
                pool.wait_ge(s["copied"], i + 1)
                if n >= 2:
                    pool.wait_ge(s["rotated"], n - 1)
                pool.tensor_tensor(c.work[:, (n % 2) * S:(n % 2 + 1) * S], c.raw[:, to, :], c.cos,
                                   ALU.mult).then_inc(s["cos_done"], 1)
                pool.wait_ge(s["cos_done"], n + 1)
                pool.wait_ge(s["sin_done"], n + 1)
                pool.tensor_tensor(c.rot[:, to, :], c.rot[:, to, :], c.work[:, (n % 2) * S:(n % 2 + 1) * S],
                                   ALU.add).then_inc(s["rotated"], 1)
            pool.wait_ge(s["gelu_ready"], 1)
            pool.tensor_copy(c.hid_v.rearrange("p f g r n -> p (f g) r n"),
                             c.hid[:, 1].rearrange("p f g n -> p (f g) n").unsqueeze(2).to_broadcast([P, 4, REP, 16])
                             ).then_inc(s["repeated"], 1)

        @block.vector
        def _(dve):
            norm_vector(dve, c, s["root_ready"], s["rstd_ready"], s["h_ready"])
            dve.wait_ge(s["gain_loaded"], 16)
            turn_vector(dve, c, c.hT, c.gain, s["turned"], s["hT_ready"])
            n = 0
            for i, (_, kind, to, _) in enumerate(jobs):
                if kind == "rotate":
                    dve.wait_ge(s["swapped"], n + 1)
                    dve.tensor_tensor(c.rot[:, to, :], c.ps[2 + n % 2][:, 0:S], c.sin, ALU.mult).then_inc(s["sin_done"], 1)
                    n += 1
                if i + 1 == cmp_done:
                    dve.wait_ge(s["copied"], cmp_done)
                    dve.wait_ge(s["pos_loaded"], 32)
                    for v in range(2):
                        for g in range(GROUPS):
                            raw = c.raw[:, CMP_T + 2 * v + g, :].rearrange("p (m j r) -> p r j m", r=2, j=8)
                            for half in range(2):
                                rows = slice(half * DH, (half + 1) * DH)
                                for jh in range(2):
                                    js = slice(8 * jh, 8 * jh + 8)
                                    add = c.pos[rows, v, js].unsqueeze(2).to_broadcast([DH, 8, N_CMP])
                                    last = dve.tensor_tensor(c.kcols[rows, v, g, js, :],
                                                             raw[rows, half, :, jh:jh + N_CMP], add, ALU.add)
                    last.then_inc(s["kcols_ready"], 1)
            dve.wait_ge(s["kv_ready"], 1)
            dve.tensor_copy(c.kc[:], kv_bank[:, 0:GROUPS * 16].rearrange("p (g n) -> p g n", n=16)).then_inc(s["kv_copied"], 1)
            vc = kv_bank[:, 64:64 + DH].unsqueeze(1).to_broadcast([P, NH, DH])
            own = c.head_of_row.unsqueeze(2).to_broadcast([P, NH, DH])
            dve.tensor_tensor(c.vc[:], vc, own, ALU.mult).then_inc(s["kv_copied"], 1)

        @block.tensor
        def _(pe):
            turn_tensor(pe, c, c.h, s["h_ready"], s["turned"])
            pe.wait_ge(s["hT_ready"], 2 * NT)

            def swap(n, i):
                pe.wait_ge(s["copied"], i + 1)
                if n >= 2:
                    pe.wait_ge(s["sin_done"], n - 1)
                pe.matmul(c.ps[2 + n % 2][:, 0:S], c.swap, c.raw[:, jobs[i][2], :], start=True, stop=True).then_inc(s["swapped"], 1)

            waiting, n = [], 0
            for i, (group, kind, to, col) in enumerate(jobs):
                bank = c.ps[i % 2]
                pe.wait_ge(w_loaded[group], 16)
                if i >= 2:
                    pe.wait_ge(s["copied"], i - 1)
                if kind in ("rotate", "plain"):
                    for k in range(KT):
                        last = pe.matmul(bank[:, 0:S], w[:, k, col:col + P], c.hT[:, k, :], start=(k == 0), stop=(k == KT - 1))
                else:
                    n_cols = 2 * P + GATE_COLS if kind == "tokens" else Q_COLS
                    for k in range(KT):
                        last = pe.matmul(bank[:, 0:n_cols], c.hT[:, k, to * P:(to + 1) * P],
                                         w[:, k, col:col + n_cols], start=(k == 0), stop=(k == KT - 1))
                last.then_inc(s["projected"], 1)
                if waiting:
                    swap(n, waiting.pop())
                    n += 1
                if kind == "rotate":
                    waiting.append(i)
            assert not waiting
            pe.wait_ge(s["kcols_ready"], 1)
            pe.wait_ge(s["wc1_loaded"], 32)
            for v in range(2):
                for f in range(2):
                    at = (2 * v + f) * GROUPS * 16
                    out = hid_bank[:, at:at + GROUPS * 16].rearrange("p (g n) -> p g n", n=16)[:, :, 0:N_CMP]
                    for j in range(CJ):
                        last = pe.matmul(out, c.wc1[:, v, j, f * P:(f + 1) * P], c.kcols[:, v, :, j, :],
                                         start=(j == 0), stop=(j == CJ - 1))
            last.then_inc(s["hid_ready"], 1)
            pe.wait_ge(s["gelu_ready"], 1)
            pe.wait_ge(s["wc2_loaded"], 64)
            pe.wait_ge(s["repeated"], 1)
            for f in range(2):
                pe.matmul(kv_bank[:, 0:GROUPS * 16], c.wc2[:, 0, f].rearrange("p u d -> p (u d)"),
                          c.hid[:, 0, f], start=(f == 0), stop=(f == 1))
            for f in range(2):
                last = pe.matmul(kv_bank[:, 64:64 + DH], c.hid_v[:, f].rearrange("p g r n -> p (g r n)"),
                                 c.wc2[:, 1, f, 0, :], start=(f == 0), stop=(f == 1))
            last.then_inc(s["kv_ready"], 1)
    end_phase()


def attend_phase(nc, c, w_out):
    s, end_phase = semaphores(nc, "attend", "w_loaded cmp_scored cmp_masked cmp_max_ready cmp_shifted cmp_exp cmp_kept cmp_sum_ready "
                           "cmp_turned cmp_pT_ready scored masked exp_ready turned pT_ready added "
                           "norm_step combined o_turned oT_ready out_ready residual_done")
    w = c.arena[:, 0:KT * D].rearrange("p (k n) -> p k n", k=KT)
    at = KT * D

    def scratch(n):
        nonlocal at
        at += n
        return c.arena[:, at - n:at]

    scores = [scratch(S) for _ in range(3)]
    probs = [scratch(S) for _ in range(3)]
    probsT = [scratch(S) for _ in range(3)]
    low = scratch(NT * 4 * NH)
    total = scratch(NT * 4 * NH)
    weight = scratch(NT * 4 * NH)
    cs, cp, cpT = scratch(P), scratch(P), scratch(P)
    c_low = scratch(NH)
    parts = [scratch(Q_COLS) for _ in range(3)]
    o = c.h
    units = []
    for t in range(NT):
        units += [(t, b, h) for h in range(NH) for b in (1, 2)]
        units += [(t, 3, h) for h in range(NH)]
    PER_T = len(units) // NT

    def column(t, b, h):
        return (t * 4 + b) * NH + h

    def operands(t, b, h):
        if b == 3:
            rows = slice((h % 2) * DH, (h % 2 + 1) * DH)
            return rows, MQ_T + h // 2, MK_T + h // 2, 2 * P + h * DH
        g = h // REP
        return slice(g * DH, (g + 1) * DH), Q_T + h % REP, (KS_T, KW_T)[b - 1], (b - 1) * P + g * DH

    with nc.Block() as block:
        @block.sync
        def _(sp):
            sp.dma_start(w, w_out.rearrange("(k p) n -> p k n", p=P)).then_inc(s["w_loaded"], 16)

        @block.scalar
        def _(act):
            def copy_probs(act, u):
                keys = (units[u][0] + 1) * P
                act.wait_ge(s["turned"], u + 1)
                if u >= 3:
                    act.wait_ge(s["added"], u - 2)
                act.activation(probsT[u % 3][:, 0:keys], c.ps[2 + u % 2][:, 0:keys], ACT.Copy).then_inc(s["pT_ready"], 1)

            for t in range(NT):
                act.wait_ge(s["cmp_shifted"], t + 1)
                act.activation(cp, cs, ACT.Exp).then_inc(s["cmp_exp"], 1)
                for n in range(PER_T):
                    u = t * PER_T + n
                    keys = (t + 1) * P
                    col = column(*units[u])
                    act.wait_ge(s["masked"], u + 1)
                    if u >= 3:
                        act.wait_ge(s["turned"], u - 2)
                    act.activation(probs[u % 3][:, 0:keys], scores[u % 3][:, 0:keys], ACT.Exp, scale=-1.0,
                                   bias=low[:, col:col + 1], accum_out=total[:, col:col + 1]).then_inc(s["exp_ready"], 1)
                    if n >= 1:
                        copy_probs(act, u - 1)
                copy_probs(act, (t + 1) * PER_T - 1)

        @block.vector
        def _(dve):
            def compressed(t):
                sc = c.ps[7][:, 0:P].rearrange("p (h n) -> p h n", n=16)
                cs3, cp3 = (a.rearrange("p (h n) -> p h n", n=16) for a in (cs, cp))
                neg = c.cmp_neg[:, t * 16:(t + 1) * 16].unsqueeze(1).to_broadcast([P, NH, 16])
                one = c.cmp_one[:, t * 16:(t + 1) * 16].unsqueeze(1).to_broadcast([P, NH, 16])
                dve.wait_ge(s["cmp_scored"], GROUPS * (t + 1))
                if t:
                    dve.wait_ge(s["cmp_exp"], t)
                dve.scalar_tensor_tensor(cs3, sc, SCALE, neg, ALU.mult, ALU.add).then_inc(s["cmp_masked"], 1)
                dve.wait_ge(s["cmp_masked"], t + 1)
                dve.tensor_reduce(c_low, cs3, AX, ALU.max).then_inc(s["cmp_max_ready"], 1)
                dve.wait_ge(s["cmp_max_ready"], t + 1)
                if t:
                    dve.wait_ge(s["cmp_turned"], t)
                dve.tensor_tensor(cs3, cs3, c_low.unsqueeze(2).to_broadcast([P, NH, 16]),
                                  ALU.subtract).then_inc(s["cmp_shifted"], 1)
                dve.wait_ge(s["cmp_exp"], t + 1)
                dve.tensor_tensor(cp3, cp3, one, ALU.mult).then_inc(s["cmp_kept"], 1)
                dve.wait_ge(s["cmp_kept"], t + 1)
                col = column(t, 0, 0)
                dve.tensor_reduce(total[:, col:col + NH], cp3, AX, ALU.add).then_inc(s["cmp_sum_ready"], 1)
                dve.wait_ge(s["cmp_turned"], t + 1)
                dve.tensor_copy(cpT, c.ps[7][:, P:2 * P]).then_inc(s["cmp_pT_ready"], 1)

            steps = 0

            def step(ins):
                nonlocal steps
                steps += 1
                ins.then_inc(s["norm_step"], 1)
                dve.wait_ge(s["norm_step"], steps)

            def weights(t, b, n_b):
                lo = column(t, b, 0)
                cols = slice(lo, lo + n_b * NH)
                step(dve.tensor_scalar(weight[:, cols], total[:, cols], 1.0, None, ALU.max))
                step(dve.reciprocal(weight[:, cols], weight[:, cols]))

            def nsa(t):
                dve.wait_ge(s["added"], t * PER_T + 2 * NH)
                dve.wait_ge(s["cmp_sum_ready"], t + 1)
                dve.wait_ge(s["exp_ready"], t * PER_T + 2 * NH)
                weights(t, 0, 3)
                gate = c.gates[:, t, :].rearrange("p (h b) -> p b h", b=3)
                wts = weight[:, column(t, 0, 0):column(t, 3, 0)].rearrange("p (b h) -> p b h", b=3)
                step(dve.tensor_tensor(wts, wts, gate, ALU.mult))
                for b in range(3):
                    last = dve.tensor_tensor(parts[b].rearrange("p (h d) -> p h d", d=DH),
                                             c.ps[4 + b][:].rearrange("p (h d) -> p h d", d=DH),
                                             wts[:, b, :].unsqueeze(2).to_broadcast([P, NH, DH]), ALU.mult)
                step(last)
                step(dve.tensor_tensor(parts[0], parts[0], parts[1], ALU.add))
                dve.tensor_tensor(o[:, t, 0:Q_COLS], parts[0], parts[2], ALU.add).then_inc(s["combined"], 1)

            def moba(t):
                dve.wait_ge(s["added"], (t + 1) * PER_T)
                dve.wait_ge(s["exp_ready"], (t + 1) * PER_T)
                weights(t, 3, 1)
                wts = weight[:, column(t, 3, 0):column(t, 3, 0) + NH].unsqueeze(2).to_broadcast([P, NH, DH])
                dve.tensor_tensor(o[:, t, Q_COLS:].rearrange("p (h d) -> p h d", d=DH),
                                  c.ps[7][:].rearrange("p (h d) -> p h d", d=DH), wts, ALU.mult).then_inc(s["combined"], 1)

            def mask(u):
                t, b, h = units[u]
                keys = (t + 1) * P
                col = column(t, b, h)
                dve.wait_ge(s["scored"], u + 1)
                if u >= 3:
                    dve.wait_ge(s["exp_ready"], u - 2)
                dve.tensor_tensor_reduce(scores[u % 3][:, 0:keys], c.ps[u % 2][:, 0:keys], c.causal[:, S - keys:S],
                                         -SCALE, 3e38, ALU.add, ALU.min, low[:, col:col + 1]).then_inc(s["masked"], 1)

            for t in range(NT):
                compressed(t)
                for n in range(PER_T):
                    mask(t * PER_T + n)
                    if n == 2 * NH + 2:
                        nsa(t)
                moba(t)

            for b in range(2 * NT):
                t, k = b // 2, (b % 2) * 4
                dve.wait_ge(s["o_turned"], b + 1)
                dve.tensor_copy(c.hT[:, k:k + 4, t * P:(t + 1) * P],
                                c.ps[b][:].rearrange("p (k n) -> p k n", k=4)).then_inc(s["oT_ready"], 1)
            for b in range(2 * NT):
                t, half = b // 2, b % 2
                dve.wait_ge(s["out_ready"], b + 1)
                cols = slice(half * 512, half * 512 + 512)
                dve.tensor_tensor(c.x[:, t, cols], c.ps[4 + b][:], c.x[:, t, cols], ALU.add).then_inc(s["residual_done"], 1)

        @block.tensor
        def _(pe):
            def compressed_scores(t):
                if t:
                    pe.wait_ge(s["combined"], 2 * t)
                for h in range(NH):
                    g = h // REP
                    rows = slice(g * DH, (g + 1) * DH)
                    last = pe.matmul(c.ps[7][:, h * 16:(h + 1) * 16], c.raw[rows, Q_T + h % REP, t * P:(t + 1) * P],
                                     c.kc[rows, g, :], start=True, stop=True)
                    if h % REP == REP - 1:
                        last.then_inc(s["cmp_scored"], 1)
                        if g == 0:
                            pe.wait_ge(s["cmp_scored"], 2 * t + 1)

            def compressed_sum(t):
                pe.wait_ge(s["cmp_kept"], t + 1)
                pe.transpose(c.ps[7][:, P:2 * P], cp, c.ident).then_inc(s["cmp_turned"], 1)
                pe.wait_ge(s["cmp_pT_ready"], t + 1)
                if t:
                    pe.wait_ge(s["combined"], 2 * t)
                pe.matmul(c.ps[4][:], cpT, c.vc[:].rearrange("p h d -> p (h d)"), start=True, stop=True)

            def score(u):
                t, b, h = units[u]
                rows, q, k, _ = operands(t, b, h)
                if u >= 2:
                    pe.wait_ge(s["masked"], u - 1)
                pe.matmul(c.ps[u % 2][:, 0:(t + 1) * P], c.rot[rows, q, t * P:(t + 1) * P],
                          c.rot[rows, k, 0:(t + 1) * P], start=True, stop=True).then_inc(s["scored"], 1)

            def turn(u):
                t = units[u][0]
                pe.wait_ge(s["exp_ready"], u + 1)
                if u >= 2:
                    pe.wait_ge(s["pT_ready"], u - 1)
                for kt in range(t + 1):
                    last = pe.transpose(c.ps[2 + u % 2][:, kt * P:(kt + 1) * P], probs[u % 3][:, kt * P:(kt + 1) * P], c.ident)
                last.then_inc(s["turned"], 1)

            def add(u):
                t, b, h = units[u]
                v = operands(t, b, h)[3]
                pe.wait_ge(s["pT_ready"], u + 1)
                if t:
                    pe.wait_ge(s["combined"], 2 * t - 1 if b < 3 else 2 * t)
                for kt in range(t + 1):
                    last = pe.matmul(c.ps[4 + b][:, h * DH:(h + 1) * DH], probsT[u % 3][:, kt * P:(kt + 1) * P],
                                     c.vtok[:, kt, v:v + DH], start=(kt == 0), stop=(kt == t))
                last.then_inc(s["added"], 1)

            for t in range(NT):
                compressed_scores(t)
                compressed_sum(t)
                first = t * PER_T
                for n in range(PER_T + 2):
                    if n < PER_T:
                        score(first + n)
                    if 1 <= n <= PER_T:
                        turn(first + n - 1)
                    if n >= 2:
                        add(first + n - 2)
            for t in range(NT):
                pe.wait_ge(s["combined"], 2 * NT)
                for k in range(KT):
                    last = pe.transpose(c.ps[2 * t + k // 4][:, (k % 4) * P:(k % 4 + 1) * P], o[:, t, k * P:(k + 1) * P], c.ident)
                    if k % 4 == 3:
                        last.then_inc(s["o_turned"], 1)
            pe.wait_ge(s["oT_ready"], 2 * NT)
            pe.wait_ge(s["w_loaded"], 16)
            for b in range(2 * NT):
                t, half = b // 2, b % 2
                for k in range(KT):
                    last = pe.matmul(c.ps[4 + b][:], c.hT[:, k, t * P:(t + 1) * P], w[:, k, half * 512:half * 512 + 512],
                                     start=(k == 0), stop=(k == KT - 1))
                last.then_inc(s["out_ready"], 1)
    end_phase()


SHARED = ("ident", "eps")


def load_tables(nc, c, ctx, name, tables, dram, x=None):
    place, width = layout(tables)
    sb = ctx.enter_context(nc.sbuf_tensor(f"{name}_tables", [P, width], F32))
    s, end_phase = semaphores(nc, f"{name}_tables", "loaded")
    with nc.Block() as block:
        @block.sync
        def _(sp):
            sp.dma_start(sb[:], dram).then_inc(s["loaded"], 16)
            if x is not None:
                sp.dma_start(c.x[:], x.rearrange("b (t p) d -> p (b t) d", p=P)).then_inc(s["loaded"], 16)
            sp.wait_ge(s["loaded"], 16 if x is None else 32)
    end_phase()
    return {key: sb[:, at:at + n] for key, (at, n) in place.items()}


def build(nc, a, out):
    with ExitStack() as ctx:
        def sb(name, shape, stack=ctx):
            return stack.enter_context(nc.sbuf_tensor(name, shape, F32))

        c = Chip()
        c.x = sb("residual", [P, NT, D])
        c.h = sb("normed", [P, NT, D])
        c.stat = sb("norm_stats", [P, 8])
        c.gain = sb("gain", [P, KT])
        c.work = sb("work", [P, 8 * S])
        c.ps = [ctx.enter_context(nc.psum_tensor(f"bank{i}", [P, 512], F32)) for i in range(8)]

        t = load_tables(nc, c, ctx, "shared", {k: v for k, v in constants().items() if k in SHARED},
                        a["constants_shared"], a["x"])
        c.ident, c.eps = t["ident"], t["eps"]
        with ExitStack() as first:
            t = load_tables(nc, c, first, "first", {k: v for k, v in constants().items() if k not in SHARED},
                            a["constants"])
            c.swap, c.cos, c.sin, c.causal = t["swap"], t["cos"], t["sin"], t["causal"]
            c.cmp_neg, c.cmp_one, c.head_of_row = t["cmp_neg"], t["cmp_one"], t["head_of_row"]

            def gain(name, l):
                return a[name][l].rearrange("(k p) -> p k", p=P)

            with nc.Fori(0, DEPTH) as l:
                ffn_phase(nc, c, "ffn1", gain("norm_ffn1", l), a["ffn1"][l])
                with ExitStack() as mixer:
                    c.hT = sb("normed_T", [P, KT, S], mixer)
                    c.arena = sb("weights", [P, KT * W_IN], mixer)
                    mixer_buffers(nc, mixer, c)
                    project_phase(nc, c, gain("norm_mix", l), a["w_in"][l], (a["pos_ck"][l], a["pos_cv"][l]),
                                  (a["w_ck1"][l], a["w_cv1"][l]), (a["w_ck2"][l], a["w_cv2"][l]))
                    attend_phase(nc, c, a["w_out"][l])
                ffn_phase(nc, c, "ffn2", gain("norm_ffn2", l), a["ffn2"][l])
            final_norm_phase(nc, c, "norm_final", a["norm_final"])

        second_block(nc, c, ctx, a, out)


def final_norm_phase(nc, c, name, gain, out=None):
    s, end_phase = semaphores(nc, name, "gain_loaded sumsq_ready root_ready rstd_ready scaled stored")
    rows = c.work[:, 0:D]
    with nc.Block() as block:
        @block.sync
        def _(sp):
            sp.dma_start(rows, gain.unsqueeze(0).to_broadcast([P, D])).then_inc(s["gain_loaded"], 16)
            if out is not None:
                for t in range(NT):
                    sp.wait_ge(s["scaled"], t + 1)
                    sp.dma_start(out[0, t * P:(t + 1) * P, :], c.x[:, t, :]).then_inc(s["stored"], 16)
                sp.wait_ge(s["stored"], 16 * NT)

        @block.scalar
        def _(act):
            norm_scalar(act, c, s["sumsq_ready"], s["root_ready"])

        @block.vector
        def _(dve):
            dve.wait_ge(s["root_ready"], 1)
            dve.reciprocal(c.stat[:, 4:6], c.stat[:, 2:4]).then_inc(s["rstd_ready"], 1)
            dve.wait_ge(s["rstd_ready"], 1)
            dve.wait_ge(s["gain_loaded"], 16)
            for t in range(NT):
                dve.scalar_tensor_tensor(c.x[:, t, :], c.x[:, t, :], c.stat[:, 4 + t:5 + t], rows,
                                         ALU.mult, ALU.mult).then_inc(s["scaled"], 1)
    end_phase()


RW_W, RW_GATE = 512, 128
HALF = RW_W // NT
RW_T = 14
PAIRS = 4
RW_COLS = RW_T * P
RET_H, RET_V = 4, 128
RET_OFF = RW_COLS
SG_OFF = RET_OFF + 2 * RET_H * DH + 2 * RET_H * RET_V
SG_W = 512
GATE_OFF = SG_OFF + 2 * SG_W
BR_W, N_BRANCH = 512, 3
DECAY = float(np.exp(-0.5))
LEVELS = 7
UNITS = 2 * NH
MIX_COLS = KT * N_BRANCH * P + 4 * N_BRANCH * P
CONV_W = 16


def second_constants():
    c = {}
    half = DH // 2
    inv = (1.0 / (np.float32(10000.0) ** np.linspace(0.0, 1.0, half, dtype=np.float32))).astype(np.float32)
    ang = np.arange(S, dtype=np.float32)[:, None] * inv[None, :]
    cos, sin, swap = np.ones((P, S), np.float32), np.zeros((P, S), np.float32), np.zeros((P, P), np.float32)
    for base in (0, DH):
        for i in range(half):
            for d, src, sign in ((base + i, base + i + half, -1), (base + i + half, base + i, 1)):
                cos[d], sin[d] = np.cos(ang[:, i]), sign * np.sin(ang[:, i])
                swap[src, d] = 1
    c["ret_swap"], c["ret_cos"], c["ret_sin"] = swap, cos, sin
    gamma = 1.0 - 2.0 ** (-5.0 - np.arange(RET_H))
    j, i = np.arange(P)[:, None], np.arange(S)[None, :]
    for h in range(RET_H):
        first = np.where(i >= j, gamma[h] ** np.maximum(i - j, 0), 0)
        c[f"ret_decay{h}"] = np.concatenate([first, first[:, :P]], 1).astype(np.float32)
    s, t = np.arange(P)[:, None], np.arange(P)[None, :]
    before, until = (s < t).astype(np.float32), (s <= t).astype(np.float32)
    c["rw_mask"] = np.concatenate([before, until, before, until], 1)
    c["rw_mask_t"] = np.ascontiguousarray(before.T)
    for level in range(LEVELS):
        b = 2**level
        low = ((s // (2 * b) == t // (2 * b)) & (s % (2 * b) >= b) & (t % (2 * b) < b)).astype(np.float32)
        c[f"level{level}"] = low
    c["minus_level0_t"] = -np.ascontiguousarray(c["level0"].T)
    c["same_head"] = (s // DH == t // DH).astype(np.float32)
    c["head_pair"] = (s // DH == np.arange(2)[None, :]).astype(np.float32)
    c["rw_eps"] = np.full((P, 1), 64e-5, np.float32)
    c["ones"] = np.ones((P, P), np.float32)
    return c


def second_buffers(nc, ctx, c):
    def sb(name, shape):
        return ctx.enter_context(nc.sbuf_tensor(name, shape, F32))

    c.hT = sb("normed_T2", [P, KT, S])
    c.arena = sb("weights2", [P, 4 * KT * 512])
    c.vecs = sb("vectors", [P, 40])
    c.mu, c.w0, c.a0, c.k_k, c.k_a, c.r_k = (c.vecs[:, a:b] for a, b in
                                             ((0, 14), (14, 18), (18, 22), (22, 26), (26, 30), (30, 34)))
    c.low_rank = sb("low_rank", [P, 2 * RW_W])
    c.rw = sb("rw", [P, 12, PAIRS * S])
    c.raw2 = sb("raw2", [P, 2, S + 1])
    c.diff = sb("diff", [P, 2, S])
    c.thin = sb("thin", [P, 2, S])
    c.vt = sb("rw_v_tokens", [P, NT, RW_W])
    c.gt = sb("rw_g_tokens", [P, NT, RW_W])
    c.bonus = sb("rw_bonus", [P, NT, NH])
    c.rw_small = sb("rw_small", [P, 3, PAIRS, NT])
    c.ret_rot = sb("ret_rot", [P, 4, S])
    c.ret_v = sb("ret_v", [P, NT, RET_H * RET_V])
    c.ret_g = sb("ret_g", [P, NT, RET_H * RET_V])
    c.y_rw = sb("y_rw_T", [P, 4, S])
    c.st = sb("row_stats", [P, 64])


R_, K_, V_, A_, LW, KK, BH, KH, KR, KR2, E1, E2 = range(12)


def rw_project_phase(nc, c, gain, w_in, vecs, w_up, a_up, g_up):
    s, end_phase = semaphores(nc, "rw_project", "gain_loaded slot0 slot1 slot2 slot3 vecs_loaded low_loaded sumsq_ready root_ready "
                               "rstd_ready h_ready turned hT_ready projected copied zeroed diffed mixed "
                               "thin_ready small_ready z_ready act_step kk_ready heads_summed norm_ready "
                               "swapped cos_done sin_done rotated v_turned v_copied rk_ready bonus_ready g_ready "
                               "dve_step centred kk_normed exps_ready")
    slot_loaded = (s["slot0"], s["slot1"], s["slot2"], s["slot3"])
    slots = [c.arena[:, i * KT * 512:(i + 1) * KT * 512].rearrange("p (k n) -> p k n", k=KT) for i in range(4)]
    groups = [(512, 512), (1536, 256), (0, 512), (1024, 512), (RET_OFF, 512), (RET_OFF + 512, 512),
              (RET_OFF + 1024, 512), (SG_OFF, 512), (SG_OFF + 512, 512)]
    jobs = [(0, j * P, "rw", (K_, j)) for j in range(4)] + [(1, j * P, "rw", ("thin", j)) for j in range(2)]
    jobs += [(2, j * P, "rw", (R_, j)) for j in range(4)] + [(3, j * P, "rw", (V_, j)) for j in range(4)]
    jobs += [(4, j * P, "ret", j) for j in range(4)]
    jobs += [(5, 0, "ret_v", t) for t in range(NT)] + [(6, 0, "ret_g", t) for t in range(NT)]
    jobs += [(7, 0, "sg_u", t) for t in range(NT)] + [(8, 0, "sg_v", t) for t in range(NT)]
    mu_of = {K_: 4, R_: 0, V_: 8, "thin": 12}
    N_RW = 14
    rw = c.rw[:]
    rw3 = rw.rearrange("p b (j n) -> p b j n", j=PAIRS)
    rw4 = rw.rearrange("p b (j c n) -> p b j c n", j=PAIRS, c=NT)
    kr = rw[:, KR:KR + 2, :].rearrange("p a n -> p (a n)").rearrange("p (j c x n) -> p j c x n", j=PAIRS, c=NT, x=2)
    sg = c.h[:].rearrange("p t (x n) -> p t x n", x=2)
    ret_raw = rw3[:, KR]

    def mixed_place(to):
        which, j = to
        return c.thin[:, j, :] if which == "thin" else rw3[:, which, j]

    with nc.Block() as block:
        @block.sync
        def _(sp):
            sp.dma_start(c.gain[:, 0:KT], gain, allow_slow_non_contiguous=True).then_inc(s["gain_loaded"], 16)
            sp.dma_start(c.vecs[:, 0:34], vecs).then_inc(s["vecs_loaded"], 16)
            for g, (col, n) in enumerate(groups):
                if g >= 4:
                    sp.wait_ge(s["projected"], max(i for i, job in enumerate(jobs) if job[0] == g - 4) + 1)
                sp.dma_start(slots[g % 4][:, :, 0:n], w_in[:, col:col + n].rearrange("(k p) n -> p k n", p=P)
                             ).then_inc(slot_loaded[g % 4], 16)
                if g == 1:
                    sp.dma_start(c.low_rank[0:DH, 0:RW_W], w_up).then_inc(s["low_loaded"], 16)
                    sp.dma_start(c.low_rank[DH:P, 0:RW_W], a_up).then_inc(s["low_loaded"], 16)
                    sp.dma_start(c.low_rank[:, RW_W:], g_up).then_inc(s["low_loaded"], 16)

        @block.scalar
        def _(act):
            norm_scalar(act, c, s["sumsq_ready"], s["root_ready"])

            def copies(lo, hi):
                for i in range(lo, hi):
                    _, _, kind, to = jobs[i]
                    act.wait_ge(s["projected"], i + 1)
                    bank = c.ps[i % 2]
                    if kind == "rw":
                        if i >= 2:
                            act.wait_ge(s["mixed"], i - 1)
                        last = act.activation(c.raw2[:, i % 2, 1:], bank[:, 0:S], ACT.Copy)
                    elif kind == "ret":
                        last = act.activation(ret_raw[:, to], bank[:, 0:S], ACT.Copy, scale=1.0 if to < 2 else DH**-0.5)
                    elif kind == "ret_v":
                        last = act.activation(c.ret_v[:, to], bank[:], ACT.Copy)
                    elif kind == "ret_g":
                        last = act.activation(c.ret_g[:, to], bank[:], ACT.Silu)
                    else:
                        last = act.activation(sg[:, to, int(kind == "sg_v")], bank[:], ACT.Gelu)
                    last.then_inc(s["copied"], 1)

            copies(0, N_RW)
            act.wait_ge(s["mixed"], 6)
            act.activation(c.thin[0:DH, 0, :], c.thin[0:DH, 0, :], ACT.Tanh).then_inc(s["thin_ready"], 1)
            act.activation(c.thin[:, 1, :], c.thin[:, 1, :], ACT.Sigmoid).then_inc(s["thin_ready"], 1)
            act.wait_ge(s["vecs_loaded"], 16)
            for which, bias in ((LW, c.w0), (A_, c.a0)):
                for j in range(PAIRS):
                    bank = c.ps[(4 if which == LW else 6) + j // 2]
                    act.wait_ge(s["small_ready"], 1 if which == LW else 2)
                    act.activation(rw3[:, which, j], bank[:, (j % 2) * S:(j % 2 + 1) * S], ACT.Sigmoid,
                                   bias=bias[:, j:j + 1]).then_inc(s["z_ready"], 1)
            copies(N_RW, N_RW + 4)
            act.wait_ge(s["heads_summed"], 1)
            for b in range(2):
                act.activation(rw[:, E1, b * 512:(b + 1) * 512], c.ps[4 + b][:], ACT.Sqrt).then_inc(s["norm_ready"], 1)
            for t in range(NT):
                act.wait_ge(s["g_ready"], t + 1)
                last = act.activation(c.gt[:, t], c.ps[6 + t][:], ACT.Copy)
            last.then_inc(s["act_step"], 1)
            act.wait_ge(s["centred"], 1)
            act.wait_ge(s["kk_normed"], 1)
            act.activation(rw[:, E1], rw[:, LW], ACT.Exp, scale=-DECAY).then_inc(s["exps_ready"], 1)
            act.activation(rw[:, E2], rw[:, LW], ACT.Exp, scale=DECAY).then_inc(s["exps_ready"], 1)
            act.activation(c.rw_small[:, 1], c.rw_small[:, 0], ACT.Exp, scale=DECAY).then_inc(s["exps_ready"], 1)
            act.activation(c.rw_small[:, 2], c.rw_small[:, 0], ACT.Exp, scale=-DECAY).then_inc(s["exps_ready"], 1)
            copies(N_RW + 4, len(jobs))

        @block.gpsimd
        def _(pool):
            pool.memset(c.raw2[:, :, 0:1], 0.0).then_inc(s["zeroed"], 1)
            pool.wait_ge(s["zeroed"], 1)
            for i in range(N_RW):
                pool.wait_ge(s["copied"], i + 1)
                if i >= 2:
                    pool.wait_ge(s["mixed"], i - 1)
                pool.tensor_tensor(c.diff[:, i % 2], c.raw2[:, i % 2, 0:S], c.raw2[:, i % 2, 1:], ALU.subtract
                                   ).then_inc(s["diffed"], 1)
            for n in range(4):
                pool.wait_ge(s["copied"], N_RW + n + 1)
                if n >= 2:
                    pool.wait_ge(s["rotated"], n - 1)
                pool.tensor_tensor(c.work[:, (n % 2) * S:(n % 2 + 1) * S], ret_raw[:, n], c.ret_cos, ALU.mult
                                   ).then_inc(s["cos_done"], 1)
                pool.wait_ge(s["cos_done"], n + 1)
                pool.wait_ge(s["sin_done"], n + 1)
                pool.tensor_tensor(c.ret_rot[:, n], c.ret_rot[:, n], c.work[:, (n % 2) * S:(n % 2 + 1) * S], ALU.add
                                   ).then_inc(s["rotated"], 1)

        @block.vector
        def _(dve):
            norm_vector(dve, c, s["root_ready"], s["rstd_ready"], s["h_ready"])
            dve.wait_ge(s["gain_loaded"], 16)
            turn_vector(dve, c, c.hT, c.gain, s["turned"], s["hT_ready"])
            dve.wait_ge(s["vecs_loaded"], 16)
            for i in range(N_RW):
                to = jobs[i][3]
                m = mu_of[to[0]] + to[1]
                dve.wait_ge(s["diffed"], i + 1)
                dve.scalar_tensor_tensor(mixed_place(to), c.diff[:, i % 2], c.mu[:, m:m + 1], c.raw2[:, i % 2, 1:],
                                         ALU.mult, ALU.add).then_inc(s["mixed"], 1)
            steps = 0

            def step(ins):
                nonlocal steps
                steps += 1
                ins.then_inc(s["dve_step"], 1)
                dve.wait_ge(s["dve_step"], steps)

            dve.wait_ge(s["mixed"], N_RW)
            for j in range(PAIRS):
                last = dve.tensor_scalar(rw3[:, KK, j], rw3[:, K_, j], c.k_k[:, j:j + 1], None, ALU.mult)
            step(last)
            dve.tensor_tensor(rw[:, E2], rw[:, KK], rw[:, KK], ALU.mult).then_inc(s["kk_ready"], 1)
            for t in range(NT):
                dve.wait_ge(s["v_turned"], t + 1)
                dve.tensor_copy(c.vt[:, t], c.ps[2 + t][:]).then_inc(s["v_copied"], 1)
            for n in range(4):
                dve.wait_ge(s["swapped"], n + 1)
                dve.tensor_tensor(c.ret_rot[:, n], c.ps[2 + n % 2][:, 0:S], c.ret_sin, ALU.mult).then_inc(s["sin_done"], 1)
            dve.wait_ge(s["z_ready"], 2 * PAIRS)
            dve.wait_ge(s["rotated"], 4)
            for j in range(PAIRS):
                for ch in range(NT):
                    last = dve.tensor_tensor_scan(rw4[:, KR, j, ch], c.ones, rw4[:, LW, j, ch], 0.0,
                                                  ALU.mult, ALU.add)
            step(last)
            step(dve.tensor_copy(c.rw_small[:, 0], rw4[:, KR, :, :, P // 2 - 1]))
            flat = rw[:, KR].rearrange("p (a n) -> p a n", n=P)
            mid = c.rw_small[:, 0].rearrange("p j c -> p (j c)").unsqueeze(2).to_broadcast([P, PAIRS * NT, P])
            dve.tensor_tensor(rw[:, LW].rearrange("p (a n) -> p a n", n=P), flat, mid, ALU.subtract
                              ).then_inc(s["centred"], 1)
            for j in range(PAIRS):
                last = dve.tensor_scalar(rw3[:, KH, j], rw3[:, A_, j], -1.0, c.k_a[:, j:j + 1], ALU.add, ALU.mult)
            step(last)
            step(dve.scalar_tensor_tensor(rw[:, K_], rw[:, KH], 1.0, rw[:, K_], ALU.add, ALU.mult))
            step(dve.tensor_tensor(rw[:, BH], rw[:, R_], rw[:, K_], ALU.mult))
            for j in range(PAIRS):
                last = dve.tensor_scalar(rw3[:, BH, j], rw3[:, BH, j], c.r_k[:, j:j + 1], None, ALU.mult)
            last.then_inc(s["rk_ready"], 1)
            dve.wait_ge(s["norm_ready"], 2)
            step(dve.tensor_scalar(rw[:, E1], rw[:, E1], 1e-12, None, ALU.max))
            step(dve.reciprocal(rw[:, E1], rw[:, E1]))
            dve.tensor_tensor(rw[:, KK], rw[:, KK], rw[:, E1], ALU.mult).then_inc(s["kk_normed"], 1)
            dve.wait_ge(s["kk_normed"], 1)
            step(dve.tensor_tensor(rw[:, A_], rw[:, A_], rw[:, KK], ALU.mult))
            dve.wait_ge(s["bonus_ready"], 1)
            step(dve.tensor_copy(c.bonus[:].rearrange("p t h -> p (t h)"), c.ps[3][:, 0:NT * NH]))
            dve.wait_ge(s["exps_ready"], 4)
            step(dve.tensor_tensor(rw[:, BH], rw[:, A_], rw[:, E2], ALU.mult))
            step(dve.tensor_tensor(rw[:, KH], rw[:, K_], rw[:, E2], ALU.mult))
            for ch in range(NT):
                last = dve.tensor_tensor(kr[:, :, ch, 1, :], rw4[:, R_, :, ch], rw4[:, E1, :, ch], ALU.mult)
                dve.tensor_tensor(kr[:, :, ch, 0, 1:], rw4[:, KK, :, ch, 1:], rw4[:, E1, :, ch, 0:P - 1], ALU.mult)
                last = dve.tensor_tensor(kr[:, :, ch, 0, 0:1], rw4[:, KK, :, ch, 0:1],
                                         c.rw_small[:, 1, :, ch].unsqueeze(2), ALU.mult)
            step(last)
            step(dve.tensor_tensor(c.rw_small[:, 0, :, 0], rw4[:, E1, :, 0, P - 1], c.rw_small[:, 2, :, 1], ALU.mult))

        @block.tensor
        def _(pe):
            turn_tensor(pe, c, c.h, s["h_ready"], s["turned"])
            pe.wait_ge(s["hT_ready"], 2 * NT)

            def project(lo, hi, after=None):
                for i in range(lo, hi):
                    group, col, kind, to = jobs[i]
                    bank, w = c.ps[i % 2], slots[group % 4]
                    pe.wait_ge(slot_loaded[group % 4], 16 * (group // 4 + 1))
                    if i >= 2:
                        pe.wait_ge(s["copied"], i - 1)
                    for k in range(KT):
                        if kind in ("rw", "ret"):
                            last = pe.matmul(bank[:, 0:S], w[:, k, col:col + P], c.hT[:, k, :],
                                             start=(k == 0), stop=(k == KT - 1))
                        else:
                            last = pe.matmul(bank[:], c.hT[:, k, to * P:(to + 1) * P], w[:, k, :],
                                             start=(k == 0), stop=(k == KT - 1))
                    last.then_inc(s["projected"], 1)
                    if after:
                        after(i)

            project(0, N_RW)
            pe.wait_ge(s["thin_ready"], 2)
            pe.wait_ge(s["low_loaded"], 48)
            for half, first_bank in ((0, 4), (1, 6)):
                rows = slice(half * DH, (half + 1) * DH)
                for j in range(PAIRS):
                    last = pe.matmul(c.ps[first_bank + j // 2][:, (j % 2) * S:(j % 2 + 1) * S],
                                     c.low_rank[rows, j * P:(j + 1) * P], c.thin[rows, 0, :], start=True, stop=True)
                last.then_inc(s["small_ready"], 1)
            pe.wait_ge(s["mixed"], N_RW)
            for t in range(NT):
                for j in range(PAIRS):
                    last = pe.transpose(c.ps[2 + t][:, j * P:(j + 1) * P], rw3[:, V_, j, t * P:(t + 1) * P], c.ident)
                last.then_inc(s["v_turned"], 1)

            def swap(n):
                pe.wait_ge(s["copied"], N_RW + n + 1)
                pe.wait_ge(s["v_copied"], NT)
                if n >= 2:
                    pe.wait_ge(s["sin_done"], n - 1)
                pe.matmul(c.ps[2 + n % 2][:, 0:S], c.ret_swap, ret_raw[:, n], start=True, stop=True).then_inc(s["swapped"], 1)

            project(N_RW, N_RW + 4, lambda i: swap(i - N_RW - 1) if i > N_RW else None)
            swap(3)
            pe.wait_ge(s["kk_ready"], 1)
            pe.wait_ge(s["z_ready"], 2 * PAIRS)
            for j in range(PAIRS):
                last = pe.matmul(c.ps[4 + j // 2][:, (j % 2) * S:(j % 2 + 1) * S], c.same_head, rw3[:, E2, j],
                                 start=True, stop=True)
            last.then_inc(s["heads_summed"], 1)
            for t in range(NT):
                pe.matmul(c.ps[6 + t][:], c.thin[:, 1, t * P:(t + 1) * P], c.low_rank[:, RW_W:],
                          start=True, stop=True).then_inc(s["g_ready"], 1)
            project(N_RW + 4, N_RW + 6)
            pe.wait_ge(s["rk_ready"], 1)
            pe.wait_ge(s["sin_done"], 4)
            for t in range(NT):
                for j in range(PAIRS):
                    at = t * NH + 2 * j
                    last = pe.matmul(c.ps[3][:, at:at + 2], rw3[:, BH, j, t * P:(t + 1) * P], c.head_pair,
                                     start=True, stop=True)
            last.then_inc(s["bonus_ready"], 1)
            project(N_RW + 6, len(jobs))
    end_phase()


def rw_scan_phase(nc, c, lnx_g, lnx_b):
    s, end_phase = semaphores(nc, "rw_scan", "rows_loaded zeroed scored kept scored_t kept_t masked first_step inverse0 low_ready "
                            "inner_ready inner_copied outer_ready updated b_turned b_copied rhs_ready rhs_copied "
                            "w_ready w_copied state_ready state_copied y_ready post y_turned y_copied squared")
    at = 0

    def take(n):
        nonlocal at
        at += n
        return c.arena[:, at - n:at]

    pairs_of = take(UNITS * 512).rearrange("p (u n) -> p u n", u=UNITS)
    a_rows = take(UNITS * P).rearrange("p (u n) -> p u n", u=UNITS)
    z = take(UNITS * P).rearrange("p (u n) -> p u n", u=UNITS)
    x = take(UNITS * P).rearrange("p (u n) -> p u n", u=UNITS)
    assert at <= 4 * KT * 512
    rw3 = c.rw[:].rearrange("p b (j n) -> p b j n", j=PAIRS)
    rw = c.rw[:]
    kr = rw[:, KR:KR + 2, :].rearrange("p a n -> p (a n)").rearrange("p (j c n) -> p j c n", j=PAIRS, c=NT)
    low = rw[:, R_, 0:2 * 512].rearrange("p (b n) -> p b n", b=2)
    inner = rw[:, K_, 0:2 * 512].rearrange("p (b n) -> p b n", b=2)
    b_rows, h_rows = rw[:, V_, 0:512], rw[:, V_, 512:1024]
    rhs = rw[:, A_, 0:1024].rearrange("p (c n) -> p c n", c=NT)
    w_rows = rw[:, LW, 0:1024].rearrange("p (c n) -> p c n", c=NT)
    state = rw[:, KK, 0:512]
    y = rw[:, E1].rearrange("p (c n) -> p c n", c=NT)
    y2 = rw[:, E2].rearrange("p (c n) -> p c n", c=NT)
    lnx = c.work[:, 0:2 * RW_W].rearrange("p (a n) -> p a n", a=2)

    units = [(ch, e, j) for ch in range(NT) for e in range(2) for j in range(PAIRS)]
    QUADS = UNITS // 4

    def rows_of(u):
        e = units[u][1]
        return slice(e * DH, (e + 1) * DH)

    def head_cols(u):
        _, e, j = units[u]
        return slice(j * P + e * DH, j * P + (e + 1) * DH)

    def quad(buf, q):
        return buf[:, 4 * q:4 * q + 4, :]

    def bank4(b):
        return c.ps[b][:].rearrange("p (u n) -> p u n", u=4)

    with nc.Block() as block:
        @block.sync
        def _(sp):
            for i, v in enumerate((lnx_g, lnx_b)):
                sp.dma_start(lnx[:, i], v.unsqueeze(0).to_broadcast([P, RW_W])).then_inc(s["rows_loaded"], 16)

        @block.gpsimd
        def _(pool):
            pool.memset(pairs_of[:, 0:4], 0.0).then_inc(s["zeroed"], 1)
            pool.memset(a_rows, 0.0).then_inc(s["zeroed"], 1)
            for q in range(1, QUADS):
                pool.memset(pairs_of[:, 4 * q:4 * q + 4], 0.0).then_inc(s["zeroed"], 1)
            for n in range((LEVELS - 1) * QUADS):
                level, q = n // QUADS + 1, n % QUADS
                pool.wait_ge(s["kept_t"], q + 1)
                if n >= 2:
                    pool.wait_ge(s["inner_ready"], n - 1)
                m = c.levels[level].unsqueeze(1).to_broadcast([P, 4, P])
                pool.tensor_tensor(low[:, n % 2].rearrange("p (u n) -> p u n", u=4), quad(a_rows, q), m, ALU.mult
                                   ).then_inc(s["low_ready"], 1)

        @block.scalar
        def _(act):
            for n in range((LEVELS - 1) * QUADS):
                act.wait_ge(s["inner_ready"], n + 1)
                if n >= 2:
                    act.wait_ge(s["outer_ready"], n - 1)
                act.activation(inner[:, n % 2], c.ps[2 + n % 2][:], ACT.Copy).then_inc(s["inner_copied"], 1)
            for i, dst in enumerate((b_rows, h_rows)):
                act.wait_ge(s["b_turned"], i + 1)
                act.activation(dst, c.ps[2 + i][:], ACT.Copy).then_inc(s["b_copied"], 1)
            for ch in range(NT):
                act.wait_ge(s["w_ready"], ch + 1)
                act.activation(w_rows[:, ch], c.ps[1][:], ACT.Copy).then_inc(s["w_copied"], 1)
            act.wait_ge(s["post"], 1)
            act.activation(y2, y, ACT.Square).then_inc(s["squared"], 1)
            act.wait_ge(s["post"], 2)
            act.activation(c.st[:, 16:32], c.st[:, 0:16], ACT.Sqrt, bias=c.rw_eps, scale=1.0 / DH).then_inc(s["squared"], 1)

        @block.vector
        def _(dve):
            for q in range(QUADS):
                for u in range(4 * q, 4 * q + 4):
                    dve.wait_ge(s["scored"], u + 1)
                    dve.wait_ge(s["zeroed"], 1 if q == 0 else q + 2)
                    dve.copy_predicated(pairs_of[:, u], c.rw_mask.bitcast(mybir.dt.uint32), c.ps[u % 2][:]).then_inc(s["kept"], 1)
                dve.wait_ge(s["scored_t"], q + 1)
                dve.wait_ge(s["zeroed"], 2)
                mask = c.rw_mask_t.bitcast(mybir.dt.uint32).unsqueeze(1).to_broadcast([P, 4, P])
                dve.copy_predicated(quad(a_rows, q), mask, bank4(2 + q % 2)).then_inc(s["kept_t"], 1)
                dve.wait_ge(s["kept"], 4 * q + 4)
                dve.wait_ge(s["kept_t"], q + 1)
                m = c.minus_level0_t.unsqueeze(1).to_broadcast([P, 4, P])
                dve.tensor_tensor(quad(z, q), pairs_of[:, 4 * q:4 * q + 4, 0:P], m, ALU.mult).then_inc(s["first_step"], 1)
                m = c.levels[0].unsqueeze(1).to_broadcast([P, 4, P])
                dve.tensor_tensor(quad(x, q), quad(a_rows, q), m, ALU.mult).then_inc(s["first_step"], 1)
                dve.wait_ge(s["first_step"], 2 * q + 2)
                eye = c.ident.unsqueeze(1).to_broadcast([P, 4, P])
                dve.tensor_tensor(quad(z, q), quad(z, q), eye, ALU.add).then_inc(s["inverse0"], 1)
                dve.tensor_tensor(quad(x, q), eye, quad(x, q), ALU.subtract).then_inc(s["inverse0"], 1)
            for n in range((LEVELS - 1) * QUADS):
                q = n % QUADS
                dve.wait_ge(s["outer_ready"], n + 1)
                dve.tensor_tensor(quad(z, q), quad(z, q), bank4(4 + n % 2), ALU.subtract).then_inc(s["updated"], 1)
                if n < (LEVELS - 2) * QUADS:
                    dve.tensor_tensor(quad(x, q), quad(x, q), bank4(6 + n % 2), ALU.subtract).then_inc(s["updated"], 1)
            for ch in range(NT):
                dve.wait_ge(s["rhs_ready"], ch + 1)
                dve.tensor_scalar(rhs[:, ch], c.ps[0][:], -1.0, None, ALU.mult).then_inc(s["rhs_copied"], 1)
                if ch == 0:
                    dve.wait_ge(s["state_ready"], 1)
                    for j in range(PAIRS):
                        last = dve.scalar_tensor_tensor(state[:, j * P:(j + 1) * P], c.ps[6][:, j * P:(j + 1) * P],
                                                        c.rw_small[:, 0, j, 0:1], c.same_head, ALU.mult, ALU.mult)
                    last.then_inc(s["state_copied"], 1)
            steps = 0

            def step(ins):
                nonlocal steps
                steps += 1
                ins.then_inc(s["first_step"], 1)
                dve.wait_ge(s["first_step"], 2 * QUADS + steps)

            def heads(a):
                return a.rearrange("p c (h d) -> p (c h) d", d=DH)

            def wide(a):
                return a.unsqueeze(2).to_broadcast([P, NT * NH, DH])

            for ch in range(NT):
                dve.wait_ge(s["y_ready"], ch + 1)
                last = dve.tensor_copy(y[:, ch], c.ps[4 + ch][:])
            step(last)
            step(dve.tensor_reduce(c.st[:, 0:16], heads(y), AX, ALU.add))
            step(dve.tensor_scalar(c.st[:, 0:16], c.st[:, 0:16], 1.0 / DH, None, ALU.mult))
            dve.tensor_tensor(heads(y), heads(y), wide(c.st[:, 0:16]), ALU.subtract).then_inc(s["post"], 1)
            dve.wait_ge(s["squared"], 1)
            dve.tensor_reduce(c.st[:, 0:16], heads(y2), AX, ALU.add).then_inc(s["post"], 1)
            dve.wait_ge(s["squared"], 2)
            step(dve.reciprocal(c.st[:, 32:48], c.st[:, 16:32]))
            step(dve.tensor_tensor(heads(y), heads(y), wide(c.st[:, 32:48]), ALU.mult))
            dve.wait_ge(s["rows_loaded"], 32)
            step(dve.tensor_tensor(y, y, lnx[:, 0].unsqueeze(1).to_broadcast([P, NT, RW_W]), ALU.mult))
            step(dve.tensor_tensor(y, y, lnx[:, 1].unsqueeze(1).to_broadcast([P, NT, RW_W]), ALU.add))
            step(dve.tensor_tensor(heads(y2), heads(c.vt[:]), wide(c.bonus[:].rearrange("p c h -> p (c h)")), ALU.mult))
            step(dve.tensor_tensor(y, y, y2, ALU.add))
            dve.tensor_tensor(y, y, c.gt[:], ALU.mult).then_inc(s["post"], 1)
            for t in range(NT):
                dve.wait_ge(s["y_turned"], t + 1)
                dve.tensor_copy(c.y_rw[:, :, t * P:(t + 1) * P], bank4(2 + t)).then_inc(s["y_copied"], 1)

        @block.tensor
        def _(pe):
            for q in range(QUADS):
                for u in range(4 * q, 4 * q + 4):
                    ch, e, j = units[u]
                    rows, toks = rows_of(u), slice(ch * P, (ch + 1) * P)
                    if u >= 2:
                        pe.wait_ge(s["kept"], u - 1)
                    pe.matmul(c.ps[u % 2][:, 0:S], rw3[rows, BH, j, toks], kr[rows, j, ch], start=True, stop=True)
                    pe.matmul(c.ps[u % 2][:, S:2 * S], rw3[rows, KH, j, toks], kr[rows, j, ch], start=True, stop=True
                              ).then_inc(s["scored"], 1)
                if q >= 2:
                    pe.wait_ge(s["kept_t"], q - 1)
                for i, u in enumerate(range(4 * q, 4 * q + 4)):
                    ch, e, j = units[u]
                    rows, toks = rows_of(u), slice(ch * P, (ch + 1) * P)
                    last = pe.matmul(c.ps[2 + q % 2][:, i * P:(i + 1) * P], kr[rows, j, ch, 0:P], rw3[rows, BH, j, toks],
                                     start=True, stop=True)
                last.then_inc(s["scored_t"], 1)

            TOTAL = (LEVELS - 1) * QUADS

            def n_updates(n):
                both = (LEVELS - 2) * QUADS
                return 2 * (n + 1) if n < both else 2 * both + (n + 1 - both)

            def inner_product(n):
                q = n % QUADS
                pe.wait_ge(s["low_ready"], n + 1)
                if n < QUADS:
                    pe.wait_ge(s["inverse0"], 2 * q + 2)
                else:
                    pe.wait_ge(s["updated"], n_updates(n - QUADS))
                pe.wait_ge(s["kept_t"], QUADS)
                if n >= 2:
                    pe.wait_ge(s["inner_copied"], n - 1)
                for i in range(4):
                    last = pe.matmul(c.ps[2 + n % 2][:, i * P:(i + 1) * P], low[:, n % 2, i * P:(i + 1) * P],
                                     z[:, 4 * q + i], start=True, stop=True)
                last.then_inc(s["inner_ready"], 1)

            def outer_product(n):
                q = n % QUADS
                pe.wait_ge(s["inner_copied"], n + 1)
                if n >= 2:
                    pe.wait_ge(s["updated"], n_updates(n - 2))
                for i in range(4):
                    last = pe.matmul(c.ps[4 + n % 2][:, i * P:(i + 1) * P], x[:, 4 * q + i],
                                     inner[:, n % 2, i * P:(i + 1) * P], start=True, stop=True)
                if n < (LEVELS - 2) * QUADS:
                    for i in range(4):
                        last = pe.matmul(c.ps[6 + n % 2][:, i * P:(i + 1) * P], inner[:, n % 2, i * P:(i + 1) * P],
                                         x[:, 4 * q + i], start=True, stop=True)
                last.then_inc(s["outer_ready"], 1)

            inner_product(0)
            for n in range(TOTAL):
                if n + 1 < TOTAL:
                    inner_product(n + 1)
                outer_product(n)

            pe.wait_ge(s["inner_copied"], TOTAL)
            for i, which in enumerate((BH, KH)):
                for j in range(PAIRS):
                    last = pe.transpose(c.ps[2 + i][:, j * P:(j + 1) * P], rw3[:, which, j, 0:P], c.ident)
                last.then_inc(s["b_turned"], 1)
            for ch in range(NT):
                us = range(ch * NH, (ch + 1) * NH)
                if ch == 0:
                    pe.wait_ge(s["kept"], UNITS)
                else:
                    pe.wait_ge(s["rhs_copied"], ch)
                    pe.wait_ge(s["state_copied"], 1)
                    for j in range(PAIRS):
                        pe.matmul(c.ps[0][:, j * P:(j + 1) * P], kr[:, j, ch, 0:P], state[:, j * P:(j + 1) * P],
                                  start=(j == 0), stop=False, skip_group_check=True)
                for u in us:
                    last = pe.matmul(c.ps[0][:, head_cols(u)], pairs_of[:, u, S:S + P], c.vt[:, ch, head_cols(u)],
                                     start=(ch == 0), stop=True, skip_group_check=True)
                last.then_inc(s["rhs_ready"], 1)
                pe.wait_ge(s["rhs_copied"], ch + 1)
                pe.wait_ge(s["updated"], n_updates(TOTAL - 1))
                if ch:
                    pe.wait_ge(s["w_copied"], ch)
                for u in us:
                    last = pe.matmul(c.ps[1][:, head_cols(u)], z[:, u], rhs[:, ch, head_cols(u)], start=True, stop=True)
                last.then_inc(s["w_ready"], 1)
                pe.wait_ge(s["w_copied"], ch + 1)
                if ch == 0:
                    pe.wait_ge(s["b_copied"], 2)
                    for j in range(PAIRS):
                        cols = slice(j * P, (j + 1) * P)
                        pe.matmul(c.ps[6][:, cols], b_rows[:, cols], w_rows[:, 0, cols], start=True, stop=False)
                        last = pe.matmul(c.ps[6][:, cols], h_rows[:, cols], c.vt[:, 0, cols], start=False, stop=True)
                    last.then_inc(s["state_ready"], 1)
                else:
                    for j in range(PAIRS):
                        pe.matmul(c.ps[4 + ch][:, j * P:(j + 1) * P], kr[:, j, ch, P:2 * P], state[:, j * P:(j + 1) * P],
                                  start=(j == 0), stop=False, skip_group_check=True)
                for u in us:
                    pe.matmul(c.ps[4 + ch][:, head_cols(u)], pairs_of[:, u, P:2 * P], w_rows[:, ch, head_cols(u)],
                              start=(ch == 0), stop=False, skip_group_check=True)
                    last = pe.matmul(c.ps[4 + ch][:, head_cols(u)], pairs_of[:, u, S + P:2 * S],
                                     c.vt[:, ch, head_cols(u)], start=False, stop=True, skip_group_check=True)
                last.then_inc(s["y_ready"], 1)
            for t in range(NT):
                pe.wait_ge(s["post"], 3)
                for j in range(PAIRS):
                    last = pe.transpose(c.ps[2 + t][:, j * P:(j + 1) * P], y[:, t, j * P:(j + 1) * P], c.ident)
                last.then_inc(s["y_turned"], 1)
    end_phase()


def mix_phase(nc, c, sg_ln_g, sg_ln_b, sg_w, sg_b, mix_w, w_out):
    s, end_phase = semaphores(nc, "mix", "rows_loaded ws_loaded slot0 slot1 slot2 w_loaded scored decayed ret_used ret_squared "
                        "ret_done ws_turned ws_copied sg_step sg_squared sg_rooted sg_normed sg_ready sg_done y_turned "
                        "y_copied gated sig_ready multiplied dve_step merged_step out_ready residual_done")
    slot_loaded = (s["slot0"], s["slot1"], s["slot2"])
    slots = [c.arena[:, i * MIX_COLS:(i + 1) * MIX_COLS] for i in range(3)]
    rw = c.rw[:].rearrange("p b n -> p (b n)")
    at = 0

    def take(n):
        nonlocal at
        at += n
        return rw[:, at - n:at]

    w = take(KT * D).rearrange("p (k n) -> p k n", k=KT)
    y_ret, y_sg = (take(4 * S).rearrange("p (k n) -> p k n", k=4) for _ in range(2))
    merged = c.h[:].rearrange("p t (f n) -> p (t f) n", n=S)
    sg = c.h[:].rearrange("p t (x n) -> p t x n", x=2)
    sc = c.arena[:, 3 * MIX_COLS:3 * MIX_COLS + 2 * 384].rearrange("p (b n) -> p b n", b=2)
    ws = c.low_rank[:, 0:SG_W].rearrange("p (g n) -> p g n", g=4)
    wsT = c.low_rank[:, SG_W:].rearrange("p (g n) -> p g n", g=4)
    ln = c.work[:, 0:2 * SG_W].rearrange("p (a n) -> p a n", a=2)
    sig = c.work[:, SG_W * 2:SG_W * 2 + 2 * 512].rearrange("p (b n) -> p b n", b=2)
    sq = c.vt[:]
    y_branch = [c.y_rw[:], y_ret, y_sg]

    def gate_w(slot, k, b):
        return slots[slot][:, (k * N_BRANCH + b) * P:(k * N_BRANCH + b + 1) * P]

    def branch_w(slot, b, k):
        first = KT * N_BRANCH * P + (b * 4 + k) * P
        return slots[slot][:, first:first + P]

    steps_of = [(f, b) for f in range(KT) for b in range(N_BRANCH)]

    with nc.Block() as block:
        @block.sync
        def _(sp):
            sp.dma_start(ws, sg_w.rearrange("g i j -> i g j")).then_inc(s["ws_loaded"], 16)
            for i, v in enumerate((sg_ln_g, sg_ln_b)):
                sp.dma_start(ln[:, i], v.unsqueeze(0).to_broadcast([P, SG_W])).then_inc(s["rows_loaded"], 16)
            sp.dma_start(c.st[:, 48:52], sg_b.rearrange("g i -> i g"), allow_slow_non_contiguous=True
                         ).then_inc(s["rows_loaded"], 16)
            for f in range(KT):
                if f >= 3:
                    sp.wait_ge(s["gated"], N_BRANCH * (f - 2))
                sp.dma_start(slots[f % 3], mix_w[f]).then_inc(slot_loaded[f % 3], 16)
                if f == 3:
                    sp.dma_start(w, w_out.rearrange("(k p) n -> p k n", p=P)).then_inc(s["w_loaded"], 16)

        @block.scalar
        def _(act):
            for t in range(NT):
                act.wait_ge(s["sg_step"], t + 1)
                act.activation(sq[:, t], sg[:, t, 1], ACT.Square, accum_out=c.st[:, 8 + t:9 + t]).then_inc(s["sg_squared"], 1)
            act.wait_ge(s["sg_squared"], NT)
            act.activation(c.st[:, 12:14], c.st[:, 8:10], ACT.Sqrt, bias=c.eps, scale=1.0 / SG_W).then_inc(s["sg_rooted"], 1)
            for t in range(NT):
                act.wait_ge(s["ret_used"], RET_H)
                act.wait_ge(s["sg_rooted"], 1)
                act.activation(sq[:, t], c.ps[2 + t][:], ACT.Square).then_inc(s["ret_squared"], 1)
            act.wait_ge(s["ret_done"], 1)
            act.activation(c.st[:, 24:32], c.st[:, 16:24], ACT.Sqrt, bias=c.eps, scale=1.0 / RET_V).then_inc(s["ret_squared"], 1)
            for n in range(len(steps_of)):
                act.wait_ge(s["gated"], n + 1)
                if n >= 2:
                    act.wait_ge(s["multiplied"], n - 1)
                act.activation(sig[:, n % 2, 0:S], c.ps[n % 2][:, 0:S], ACT.Sigmoid).then_inc(s["sig_ready"], 1)

        @block.vector
        def _(dve):
            steps = 0

            def step(ins):
                nonlocal steps
                steps += 1
                ins.then_inc(s["dve_step"], 1)
                dve.wait_ge(s["dve_step"], steps)

            v = sg[:, :, 1]
            step(dve.tensor_reduce(c.st[:, 0:NT], v, AX, ALU.add))
            step(dve.tensor_scalar(c.st[:, 0:NT], c.st[:, 0:NT], 1.0 / SG_W, None, ALU.mult))
            for t in range(NT):
                dve.tensor_scalar(v[:, t], v[:, t], c.st[:, t:t + 1], None, ALU.subtract).then_inc(s["sg_step"], 1)
            for h in range(RET_H):
                dve.wait_ge(s["scored"], h + 1)
                if h >= 2:
                    dve.wait_ge(s["ret_used"], h - 1)
                dve.tensor_tensor(sc[:, h % 2], c.ps[h % 2][:, 0:384], c.ret_decays[h], ALU.mult).then_inc(s["decayed"], 1)
            dve.wait_ge(s["sg_rooted"], 1)
            step(dve.reciprocal(c.st[:, 14:16], c.st[:, 12:14]))
            dve.wait_ge(s["rows_loaded"], 48)
            for t in range(NT):
                step(dve.scalar_tensor_tensor(v[:, t], v[:, t], c.st[:, 14 + t:15 + t], ln[:, 0], ALU.mult, ALU.mult))
            dve.tensor_tensor(v, v, ln[:, 1].unsqueeze(1).to_broadcast([P, NT, SG_W]), ALU.add).then_inc(s["sg_normed"], 1)
            dve.wait_ge(s["ws_turned"], 1)
            dve.tensor_tensor(wsT, c.ps[6][:].rearrange("p (g n) -> p g n", g=4),
                              c.rw_mask[:, P:2 * P].unsqueeze(1).to_broadcast([P, 4, P]), ALU.mult).then_inc(s["ws_copied"], 1)
            dve.wait_ge(s["ret_squared"], NT)
            dve.tensor_reduce(c.st[:, 16:24], sq.rearrange("p t (h d) -> p (t h) d", d=RET_V), AX, ALU.add
                              ).then_inc(s["ret_done"], 1)
            dve.wait_ge(s["ret_squared"], NT + 1)
            step(dve.reciprocal(c.st[:, 32:40], c.st[:, 24:32]))
            for t in range(NT):
                wide = c.st[:, 32 + 4 * t:36 + 4 * t].unsqueeze(2).to_broadcast([P, RET_H, RET_V])
                last = dve.tensor_tensor(sq[:, t].rearrange("p (h d) -> p h d", d=RET_V),
                                         c.ps[2 + t][:].rearrange("p (h d) -> p h d", d=RET_V), wide, ALU.mult)
            step(last)
            dve.tensor_tensor(c.ret_g[:], sq, c.ret_g[:], ALU.mult).then_inc(s["ret_done"], 1)
            for t in range(NT):
                dve.wait_ge(s["sg_ready"], t + 1)
                for g in range(4):
                    cols = slice(g * P, (g + 1) * P)
                    last = dve.scalar_tensor_tensor(c.ret_v[:, t, cols], c.ps[4 + t][:, cols], c.st[:, 48 + g:49 + g],
                                                    sg[:, t, 0, cols], ALU.add, ALU.mult)
                last.then_inc(s["sg_done"], 1)
            for i in range(2 * NT):
                t = i % NT
                dve.wait_ge(s["y_turned"], i + 1)
                dst = (y_ret, y_sg)[i // NT]
                bank = c.ps[(2, 3, 6, 7)[i]][:].rearrange("p (k n) -> p k n", k=4)
                dve.tensor_copy(dst[:, :, t * P:(t + 1) * P], bank).then_inc(s["y_copied"], 1)
            for n, (f, b) in enumerate(steps_of):
                dve.wait_ge(s["sig_ready"], n + 1)
                if b == 0:
                    dve.tensor_tensor(merged[:, f], sig[:, n % 2, 0:S], c.ps[n % 2][:, S:2 * S], ALU.mult).then_inc(s["multiplied"], 1)
                else:
                    before = sum(j > 0 for _, j in steps_of[:n - 1])
                    if before:
                        dve.wait_ge(s["merged_step"], before)
                    dve.tensor_tensor(sig[:, n % 2, S:2 * S], sig[:, n % 2, 0:S], c.ps[n % 2][:, S:2 * S], ALU.mult
                                      ).then_inc(s["multiplied"], 1)
                    dve.wait_ge(s["multiplied"], n + 1)
                    if b == 2:
                        dve.wait_ge(s["merged_step"], 2 * f + 1)
                    dve.tensor_tensor(merged[:, f], merged[:, f], sig[:, n % 2, S:2 * S], ALU.add).then_inc(s["merged_step"], 1)
            for b in range(2 * NT):
                t, half = b // 2, b % 2
                dve.wait_ge(s["out_ready"], b + 1)
                cols = slice(half * 512, half * 512 + 512)
                dve.tensor_tensor(c.x[:, t, cols], c.ps[4 + b][:], c.x[:, t, cols], ALU.add).then_inc(s["residual_done"], 1)

        @block.tensor
        def _(pe):
            def ret_sum(h):
                cols = slice(h * RET_V, (h + 1) * RET_V)
                pe.wait_ge(s["decayed"], h + 1)
                pe.matmul(c.ps[2][:, cols], sc[:, h % 2, 0:P], c.ret_v[:, 0, cols], start=True, stop=True)
                pe.matmul(c.ps[3][:, cols], sc[:, h % 2, P:S], c.ret_v[:, 0, cols], start=True, stop=False)
                last = pe.matmul(c.ps[3][:, cols], sc[:, h % 2, S:384], c.ret_v[:, 1, cols], start=False, stop=True)
                last.then_inc(s["ret_used"], 1)

            for h in range(RET_H):
                rows, tile = slice((h % 2) * DH, (h % 2 + 1) * DH), h // 2
                if h >= 2:
                    pe.wait_ge(s["decayed"], h - 1)
                bank = c.ps[h % 2]
                pe.matmul(bank[:, 0:S], c.ret_rot[rows, 2 + tile, 0:P], c.ret_rot[rows, tile, :], start=True, stop=True)
                pe.matmul(bank[:, S:S + P], c.ret_rot[rows, 2 + tile, P:S], c.ret_rot[rows, tile, P:S],
                          start=True, stop=True).then_inc(s["scored"], 1)
                if h >= 1:
                    ret_sum(h - 1)
            ret_sum(RET_H - 1)
            pe.wait_ge(s["ws_loaded"], 16)
            for g in range(4):
                last = pe.transpose(c.ps[6][:, g * P:(g + 1) * P], ws[:, g], c.ident)
            last.then_inc(s["ws_turned"], 1)
            pe.wait_ge(s["ws_copied"], 1)
            pe.wait_ge(s["sg_normed"], 1)
            for t in range(NT):
                for g in range(4):
                    cols = slice(g * P, (g + 1) * P)
                    last = pe.matmul(c.ps[4 + t][:, cols], wsT[:, g], sg[:, t, 1, cols], start=True, stop=True)
                last.then_inc(s["sg_ready"], 1)
            for i in range(2 * NT):
                t = i % NT
                if i < NT:
                    pe.wait_ge(s["ret_done"], 2)
                else:
                    pe.wait_ge(s["sg_done"], t + 1)
                src = (c.ret_g, c.ret_v)[i // NT]
                for k in range(4):
                    last = pe.transpose(c.ps[(2, 3, 6, 7)[i]][:, k * P:(k + 1) * P], src[:, t, k * P:(k + 1) * P], c.ident)
                last.then_inc(s["y_turned"], 1)
            pe.wait_ge(s["decayed"], RET_H)
            for n, (f, b) in enumerate(steps_of):
                slot = f % 3
                pe.wait_ge(slot_loaded[slot], 16 * (f // 3 + 1))
                if n >= 2:
                    pe.wait_ge(s["multiplied"], n - 1)
                for k in range(KT):
                    pe.matmul(c.ps[n % 2][:, 0:S], gate_w(slot, k, b), c.hT[:, k, :], start=(k == 0), stop=(k == KT - 1))
                if n == 0:
                    pe.wait_ge(s["y_copied"], 2 * NT)
                for k in range(4):
                    last = pe.matmul(c.ps[n % 2][:, S:2 * S], branch_w(slot, b, k), y_branch[b][:, k, :],
                                     start=(k == 0), stop=(k == 3))
                last.then_inc(s["gated"], 1)
            pe.wait_ge(s["merged_step"], 2 * KT)
            pe.wait_ge(s["w_loaded"], 16)
            for b in range(2 * NT):
                t, half = b // 2, b % 2
                for k in range(KT):
                    last = pe.matmul(c.ps[4 + b][:], merged[:, k, t * P:(t + 1) * P], w[:, k, half * 512:half * 512 + 512],
                                     start=(k == 0), stop=(k == KT - 1))
                last.then_inc(s["out_ready"], 1)
    end_phase()


def second_block(nc, c, ctx, a, out):
    t = load_tables(nc, c, ctx, "second", second_constants(), a["constants2"])
    c.ret_swap, c.ret_cos, c.ret_sin = t["ret_swap"], t["ret_cos"], t["ret_sin"]
    c.ret_decays = [t[f"ret_decay{h}"] for h in range(RET_H)]
    c.rw_mask, c.rw_mask_t, c.minus_level0_t = t["rw_mask"], t["rw_mask_t"], t["minus_level0_t"]
    c.levels = [t[f"level{n}"] for n in range(LEVELS)]
    c.same_head, c.head_pair, c.rw_eps, c.ones = t["same_head"], t["head_pair"], t["rw_eps"], t["ones"]

    def gain(name, l):
        return a[name][l].rearrange("(k p) -> p k", p=P)

    with nc.Fori(0, DEPTH) as l:
        with ExitStack() as mixer:
            second_buffers(nc, mixer, c)
            rw_project_phase(nc, c, gain("norm1_g_2", l), a["w_in_2"][l], a["vectors"][l], a["rw_w_up_2"][l],
                             a["rw_a_up_2"][l], a["rw_g_up_2"][l])
            rw_scan_phase(nc, c, a["rw_lnx_g_2"][l].rearrange("h d -> (h d)"), a["rw_lnx_b_2"][l].rearrange("h d -> (h d)"))
            mix_phase(nc, c, a["sg_ln_g_2"][l], a["sg_ln_b_2"][l], a["sg_w_s_2"][l], a["sg_b_2"][l], a["mix_w"][l],
                      a["w_out_2"][l])
        ffn_phase(nc, c, "conv_ffn", gain("norm2_g_2", l), a["conv_ffn"][l], 1.0, a["conv"][l])
    final_norm_phase(nc, c, "final", a["final_g_2"], out)


def chunked(gate, up, down):
    gate, up = (x.reshape(DEPTH, KT, P, N_CHUNK, 1, FF_W).transpose(0, 3, 4, 2, 1, 5).reshape(DEPTH, N_CHUNK, 1, P, -1)
                for x in (gate, up))
    down = down.reshape(DEPTH, N_CHUNK, 1, FF_W // P, P, D).transpose(0, 1, 2, 4, 3, 5).reshape(DEPTH, N_CHUNK, 1, P, -1)
    return np.concatenate([gate, up, down], 2).reshape(DEPTH, N_CHUNK * 3 * P, -1)


def laid_out(a):
    a = {k: np.asarray(v) for k, v in a.items()}
    tables = constants()
    a["constants_shared"] = np.concatenate([tables.pop(k) for k in SHARED], 1)
    a["constants"] = np.concatenate(list(tables.values()), 1)
    a["constants2"] = np.concatenate(list(second_constants().values()), 1)
    a["w_in"] = a["w_in"][:, :, w_in_columns()]
    names = ("rw_mu_2", "rw_w0_2", "rw_a0_2", "rw_k_k_2", "rw_k_a_2", "rw_r_k_2")
    a["vectors"] = np.concatenate([a.pop(n).reshape(DEPTH, -1, P).transpose(0, 2, 1) for n in names], 2)
    gate = a["w_in_2"][:, :, GATE_OFF:].reshape(DEPTH, KT, P, N_BRANCH, KT, P).transpose(0, 4, 2, 1, 3, 5)
    branch = a.pop("w_branch_2").reshape(DEPTH, N_BRANCH, 4, P, KT, P).transpose(0, 4, 3, 1, 2, 5)
    a["mix_w"] = np.concatenate([gate.reshape(DEPTH, KT, P, -1), branch.reshape(DEPTH, KT, P, -1)], 3)
    a["w_in_2"] = a["w_in_2"][:, :, :GATE_OFF]
    conv = np.concatenate([a.pop("ffn_conv_w_2"), a.pop("ffn_conv_b_2")[:, None]], 1)
    a["conv"] = conv.reshape(DEPTH, 4, 2, N_CHUNK, 2, P).transpose(0, 3, 5, 2, 4, 1).reshape(DEPTH, N_CHUNK * P, CONV_W)
    for name in ("ffn1", "ffn2"):
        a[name] = chunked(*(a.pop(f"w_{name}_{part}") for part in ("gate", "up", "down")))
    up = a.pop("ffn_w_up_2")
    a["conv_ffn"] = chunked(up[:, :, :D_FF], up[:, :, D_FF:], a.pop("ffn_w_down_2"))
    return {k: np.ascontiguousarray(v) for k, v in a.items()}


def kernel(**inputs):
    import concourse.bacc as bacc
    from concourse.bass_utils import run_bass_kernel_spmd

    nc = bacc.Bacc("TRN2", target_bir_lowering=False, num_devices=1)
    arrays, aps = {}, {}
    for name, value in laid_out(inputs).items():
        arrays[f"in_{name}"] = value
        aps[name] = nc.dram_tensor(f"in_{name}", value.shape, mybir.dt.from_np(value.dtype), kind="ExternalInput").ap()
    out = nc.dram_tensor("out", (1, S, D), F32, kind="ExternalOutput").ap()
    build(nc, aps, out)
    result = run_bass_kernel_spmd(nc, [arrays], core_ids=[0])
    return result.results[0]["out"]
```

```python
from contextlib import ExitStack

import concourse.bass as bass
import numpy as np
from concourse import mybir

F32 = mybir.dt.float32
ALU = mybir.AluOpType
ACT = mybir.ActivationFunctionType
AX = mybir.AxisListType.X

P = 128
D = 1024
KT = D // P
S = 256
NT = S // P
DEPTH = 2
D_FF = 2816
EPS = 1e-6
NEG = -1e30

DH = 64
NH = 8
GROUPS = 2
REP = NH // GROUPS
SCALE = DH**-0.5
Q_COLS = NH * DH
KV_COLS = 6 * GROUPS * DH
GATE_COLS = NH * 3
IN_COLS = Q_COLS + KV_COLS + GATE_COLS + 3 * Q_COLS
MOBA_OFF = Q_COLS + KV_COLS + GATE_COLS
ROT = DH // 4
CMP_LEN, CMP_STRIDE, CMP_HID = 32, 16, 256
N_CMP = (S - CMP_LEN) // CMP_STRIDE + 1
CJ = CMP_LEN * DH // P
FF_W = 2 * P
N_CHUNK = D_FF // FF_W


def constants():
    c = {}
    c["ident"] = np.eye(P, dtype=np.float32)
    half = ROT // 2
    inv = np.power(np.float32(500000.0), -(np.arange(0, ROT, 2, dtype=np.float32) / np.float32(ROT)))
    ang = np.arange(S, dtype=np.float32)[:, None] * inv.astype(np.float32)[None, :]
    cos, sin = np.ones((P, S), np.float32), np.zeros((P, S), np.float32)
    swap = np.zeros((P, P), np.float32)
    for base in (0, DH):
        for i in range(half):
            for d, src, sign in ((base + i, base + i + half, -1), (base + i + half, base + i, 1)):
                cos[d], sin[d] = np.cos(ang[:, i]), sign * np.sin(ang[:, i])
                swap[src, d] = 1
    c["swap"], c["cos"], c["sin"] = swap, cos, sin
    q, k = np.arange(P)[:, None], np.arange(S)[None, :]
    c["causal"] = np.where(k - P <= q, 0, NEG).astype(np.float32)
    t = (np.arange(NT)[None, :, None] * P + np.arange(P)[:, None, None])
    n = np.arange(16)[None, None, :]
    ok = (n < N_CMP) & (n * CMP_STRIDE + CMP_LEN - 1 <= t)
    c["cmp_neg"] = np.where(ok, 0, NEG).astype(np.float32).reshape(P, NT * 16)
    c["cmp_one"] = ok.astype(np.float32).reshape(P, NT * 16)
    c["head_of_row"] = (np.arange(P)[:, None] // 16 == np.arange(NH)[None, :]).astype(np.float32)
    c["eps"] = np.full((P, 1), EPS, np.float32)
    return c


def layout(c):
    at, place = 0, {}
    for name, a in c.items():
        place[name] = (at, a.shape[1])
        at += a.shape[1]
    return place, at


F32R = mybir.dt.float32r


def plain(ap):
    return ap.bitcast(F32)


def matmul3(pe, out, lhs, rhs, start, stop):
    pe.matmul(out, lhs[0], rhs[0], start=start, stop=False)
    pe.matmul(out, lhs[0], rhs[1], start=False, stop=False)
    return pe.matmul(out, lhs[1], rhs[0], start=False, stop=stop)


class Chip:
    pass


def load_gain(sp, c, gain, gain_loaded):
    sp.dma_start(c.gain, gain.unsqueeze(0).to_broadcast([P, D])).then_inc(gain_loaded, 16)


def norm_scalar(act, c, sumsq_ready, root_ready):
    for t in range(NT):
        act.activation(c.h[:, t, :], c.x[:, t, :], ACT.Square, accum_out=c.stat[:, t:t + 1]).then_inc(sumsq_ready, 1)
        act.wait_ge(sumsq_ready, t + 1)
        act.activation(c.stat[:, 2 + t:3 + t], c.stat[:, t:t + 1], ACT.Sqrt, bias=c.eps, scale=1.0 / D).then_inc(root_ready, 1)


def norm_vector(dve, c, gain_loaded, root_ready, rstd_ready, h_ready):
    for t in range(NT):
        dve.wait_ge(root_ready, t + 1)
        dve.reciprocal(c.stat[:, 4 + t:5 + t], c.stat[:, 2 + t:3 + t]).then_inc(rstd_ready, 1)
        dve.wait_ge(rstd_ready, t + 1)
        if t == 0:
            dve.wait_ge(gain_loaded, 16)
        for half in range(2):
            cols = slice(half * D // 2, (half + 1) * D // 2)
            dve.scalar_tensor_tensor(c.h[:, t, cols], c.x[:, t, cols], c.stat[:, 4 + t:5 + t], c.gain[:, cols],
                                     ALU.mult, ALU.mult).then_inc(h_ready, 1)


def keep_clock(pe, c, out, n):
    for _ in range(n):
        pe.matmul(out, c.ident, c.ident, start=True, stop=True)


def turn_tensor(pe, c, src, src_ready, turned):
    for b in range(2 * NT):
        t, k0 = b // 2, (b % 2) * 4
        pe.wait_ge(src_ready, b + 1)
        for k in range(k0, k0 + 4):
            last = pe.transpose(c.ps[b][:, (k - k0) * P:(k - k0 + 1) * P], src[:, t, k * P:(k + 1) * P], c.ident)
        last.then_inc(turned, 1)


def semaphores(nc, phase, names):
    stack = ExitStack()
    sems = {n: stack.enter_context(nc.semaphore(f"{phase}_{n}")) for n in names.split()}
    nums = [x.num for x in sems.values()]

    def end_phase():
        nc.all_engine_barrier(sems_to_clear=range(min(nums), max(nums) + 1))
        stack.close()

    return sems, end_phase


def turned_block(c, parts_of, b):
    t, k = b // 2, (b % 2) * 4
    return c.ps[b][:].rearrange("p (k n) -> p k n", k=4), parts_of[:, k:k + 4, t * P:(t + 1) * P]


def turned_high_scalar(act, c, high, turned, high_ready):
    for b in range(2 * NT):
        act.wait_ge(turned, b + 1)
        bank, out = turned_block(c, high, b)
        act.activation(out, bank, ACT.Copy).then_inc(high_ready, 1)


def turned_low_vector(dve, c, high, low, high_ready, ready):
    for b in range(2 * NT):
        dve.wait_ge(high_ready, b + 1)
        bank, out = turned_block(c, low, b)
        dve.tensor_tensor(out, bank, plain(turned_block(c, high, b)[1]), ALU.subtract).then_inc(ready, 1)


def ffn_phase(nc, c, phase, gain, weights, factor=0.5, conv=None):
    s, end_phase = semaphores(nc, phase, "gain_loaded sumsq_ready root_ready rstd_ready h_ready turned hT_high hT_ready "
                                         "gate0 gate1 up0 up1 down taps0 taps1 first_high first_low gu_high gu_split "
                                         "down_high down_split hidden_ready started tap_step tapped silu_ready "
                                         "product_ready act_high act_ready down_done bank_done residual_done")
    gu_loaded = ((s["gate0"], s["gate1"]), (s["up0"], s["up1"]))
    taps_loaded = (s["taps0"], s["taps1"])
    PART = KT * FF_W
    ctx = ExitStack()

    def sb(name, shape, dtype=F32):
        return ctx.enter_context(nc.sbuf_tensor(f"{phase}_{name}", shape, dtype))

    arrived_gu = sb("arrived_gate_up", [P, 2, 2, PART])
    arrived_down = sb("arrived_down", [P, PART])
    parts = sb("split_weights", [P, 2, 3, 2, PART], F32R)
    hT_parts = sb("hT_split", [P, 2, KT, S], F32R)
    act_parts = sb("act_split", [P, 2, 2, 2, S], F32R)
    w = [[tuple(parts[:, lo, part, slot, :].rearrange("p (k n) -> p k n", k=2 if part == 2 else KT) for lo in range(2))
          for slot in range(2)] for part in range(3)]
    hT = (hT_parts[:, 0], hT_parts[:, 1])
    act_high, act_low = act_parts[:, 0], act_parts[:, 1]
    acts = c.work[:, 0:4 * S].rearrange("p (s f n) -> p s f n", s=2, f=2)
    if conv is not None:
        conv_buf = c.h[:].rearrange("p t (a b n) -> p t a b n", a=2, b=2)
        taps = sb("taps", [P, 2, CONV_W])
    acc = [[c.ps[4 + 2 * t + half] for half in range(2)] for t in range(NT)]
    LOOP0 = 3
    LOOPS = (N_CHUNK - LOOP0) // 2
    assert LOOP0 + 2 * LOOPS == N_CHUNK

    def tap(slot, which, f, j):
        at = (which * 2 + f) * 4 + j
        return taps[:, slot, at:at + 1]

    def arrived(part, slot):
        return arrived_down[:] if part == 2 else arrived_gu[:, part, slot]

    def flat(a):
        return a.rearrange("p k n -> p (k n)")

    with nc.Block() as block:
        @block.sync
        def _(sp):
            def load_gu(i, slot, reuse):
                if reuse:
                    sp.wait_ge(s["gu_split"], i * 2 - 2)
                for part in range(2):
                    sp.dma_start(arrived(part, slot), weights[bass.ds(i * (3 * P) + part * P, P), :]
                                 ).then_inc(gu_loaded[part][slot], 16)

            def load_down(i, slot, reuse):
                if reuse:
                    sp.wait_ge(s["down_split"], i)
                sp.dma_start(arrived(2, slot), weights[bass.ds(i * (3 * P) + 2 * P, P), :]).then_inc(s["down"], 16)

            def load_taps(i, slot, reuse):
                if conv is not None:
                    if reuse:
                        sp.wait_ge(s["act_ready"], i * 2 - 2)
                    sp.dma_start(taps[:, slot], conv[bass.ds(i * P, P), :]).then_inc(taps_loaded[slot], 16)

            load_gain(sp, c, gain, s["gain_loaded"])
            load_gu(0, 0, False)
            load_gu(1, 1, False)
            load_down(0, 0, False)
            load_taps(0, 0, False)
            load_taps(1, 1, False)
            load_gu(2, 0, True)
            load_down(1, 1, True)
            with sp.Fori(0, LOOPS) as i:
                for d, slot in ((0, 1), (1, 0)):
                    load_gu(i * 2 + LOOP0 + d, slot, True)
                    load_down(i * 2 + LOOP0 - 1 + d, 1 - slot, True)
                    load_taps(i * 2 + LOOP0 - 1 + d, 1 - slot, True)
            load_down(N_CHUNK - 1, 0, True)
            load_taps(N_CHUNK - 1, 0, True)

        @block.scalar
        def _(act):
            def high_gu(i, slot, n_loads, reuse):
                for part in range(2):
                    act.wait_ge(gu_loaded[part][slot], n_loads)
                    if reuse:
                        act.wait_ge(s["hidden_ready"], i * 2 - 2)
                    act.activation(flat(w[part][slot][0]), arrived(part, slot), ACT.Copy).then_inc(s["gu_high"], 1)

            def high_down(i, slot, reuse):
                act.wait_ge(s["down"], i * 16 + 16)
                if reuse:
                    act.wait_ge(s["down_done"], i - 1)
                act.activation(flat(w[2][slot][0]), arrived(2, slot), ACT.Copy).then_inc(s["down_high"], 1)

            def silu(i, slot):
                for f in range(2):
                    act.wait_ge(s["hidden_ready"], i * 2 + f + 1)
                    act.activation(acts[:, slot, f], c.ps[2 * slot + f][:, 0:S], ACT.Silu).then_inc(s["silu_ready"], 1)

            def newest_tap(i, slot, n_loads):
                act.wait_ge(taps_loaded[slot], n_loads)
                for f in range(2):
                    act.wait_ge(s["hidden_ready"], i * 2 + f + 1)
                    for which in range(2):
                        last = act.activation(conv_buf[:, slot, f, which], c.ps[2 * slot + f][:, which * S:(which + 1) * S],
                                              ACT.Identity, bias=tap(slot, which, f, 3), scale=tap(slot, which, f, 2))
                    last.then_inc(s["started"], 1)

            def silu_tapped(i, slot):
                for f in range(2):
                    act.wait_ge(s["tapped"], i * 2 + f + 1)
                    act.activation(acts[:, slot, f], conv_buf[:, slot, f, 0], ACT.Silu).then_inc(s["silu_ready"], 1)

            def step(i, slot, n_loads, reuse_down):
                if conv is None:
                    silu(i - 2, slot)
                    high_gu(i, slot, n_loads, True)
                    high_down(i - 1, 1 - slot, reuse_down)
                else:
                    newest_tap(i - 2, slot, n_loads - 16)
                    high_down(i - 1, 1 - slot, reuse_down)
                    silu_tapped(i - 2, slot)
                    high_gu(i, slot, n_loads, True)

            norm_scalar(act, c, s["sumsq_ready"], s["root_ready"])
            turned_high_scalar(act, c, hT[0], s["turned"], s["hT_high"])
            act.wait_ge(s["up0"], 16)
            act.activation(flat(w[1][0][0]), arrived(1, 0), ACT.Copy).then_inc(s["gu_high"], 1)
            high_gu(1, 1, 16, False)
            high_down(0, 0, False)
            step(2, 0, 32, False)
            with act.Fori(0, LOOPS) as i:
                step(i * 2 + LOOP0, 1, i * 16 + 32, True)
                step(i * 2 + LOOP0 + 1, 0, i * 16 + 48, True)
            last_load = 16 * (N_CHUNK // 2)
            if conv is None:
                high_down(N_CHUNK - 1, 0, True)
                silu(N_CHUNK - 2, 1)
                silu(N_CHUNK - 1, 0)
            else:
                newest_tap(N_CHUNK - 2, 1, last_load)
                high_down(N_CHUNK - 1, 0, True)
                silu_tapped(N_CHUNK - 2, 1)
                newest_tap(N_CHUNK - 1, 0, last_load + 16)
                silu_tapped(N_CHUNK - 1, 0)

        @block.vector
        def _(dve):
            def low_part(i, slot, part):
                dve.wait_ge(s["gu_high"], i * 2 + part)
                high, low = w[part][slot]
                dve.tensor_tensor(flat(low), arrived(part, slot), plain(flat(high)), ALU.subtract).then_inc(s["gu_split"], 1)

            def low_gu(i, slot):
                for part in range(2):
                    low_part(i, slot, part)

            def low_down(i, slot):
                dve.wait_ge(s["down_high"], i + 1)
                high, low = w[2][slot]
                dve.tensor_tensor(flat(low), arrived(2, slot), plain(flat(high)), ALU.subtract).then_inc(s["down_split"], 1)

            def older_taps(i, slot):
                for f in range(2):
                    dve.wait_ge(s["started"], i * 2 + f + 1)
                    for shift in (1, 2):
                        if shift == 2:
                            dve.wait_ge(s["tap_step"], i * 2 + f + 1)
                        for which in range(2):
                            buf = conv_buf[:, slot, f, which, shift:]
                            last = dve.scalar_tensor_tensor(buf, c.ps[2 * slot + f][:, which * S:(which + 1) * S - shift],
                                                            tap(slot, which, f, 2 - shift), buf, ALU.mult, ALU.add)
                        last.then_inc(s["tap_step"] if shift == 1 else s["tapped"], 1)

            def product(i, slot):
                for f in range(2):
                    dve.wait_ge(s["silu_ready"], i * 2 + f + 1)
                    value, out = acts[:, slot, f], act_high[:, slot, f]
                    up = c.ps[2 * slot + f][:, S:2 * S] if conv is None else conv_buf[:, slot, f, 1]
                    dve.tensor_tensor(value, up, value, ALU.mult).then_inc(s["product_ready"], 1)
                    dve.wait_ge(s["product_ready"], i * 2 + f + 1)
                    dve.tensor_copy(out, value).then_inc(s["act_high"], 1)
                    dve.wait_ge(s["act_high"], i * 2 + f + 1)
                    dve.tensor_tensor(act_low[:, slot, f], value, plain(out), ALU.subtract).then_inc(s["act_ready"], 1)

            def step(i, slot):
                if conv is None:
                    product(i - 2, slot)
                    low_gu(i, slot)
                    low_down(i - 1, 1 - slot)
                else:
                    older_taps(i - 2, slot)
                    low_down(i - 1, 1 - slot)
                    product(i - 2, slot)
                    low_gu(i, slot)

            norm_vector(dve, c, s["gain_loaded"], s["root_ready"], s["rstd_ready"], s["h_ready"])
            dve.wait_ge(s["gate0"], 16)
            def first_gate(f, low_done):
                cols = slice(f * P, (f + 1) * P)
                value = arrived(0, 0).rearrange("p (k n) -> p k n", k=KT)[:, :, cols]
                high, low = (part[:, :, cols] for part in w[0][0])
                dve.tensor_copy(high, value).then_inc(s["first_high"], 1)
                dve.wait_ge(s["first_high"], f + 1)
                dve.tensor_tensor(low, value, plain(high), ALU.subtract).then_inc(low_done, 1)

            first_gate(0, s["first_low"])
            turned_low_vector(dve, c, hT[0], hT[1], s["hT_high"], s["hT_ready"])
            low_part(0, 0, 1)
            first_gate(1, s["gu_split"])
            low_gu(1, 1)
            low_down(0, 0)
            step(2, 0)
            with dve.Fori(0, LOOPS) as i:
                step(i * 2 + LOOP0, 1)
                step(i * 2 + LOOP0 + 1, 0)
            if conv is None:
                low_down(N_CHUNK - 1, 0)
                product(N_CHUNK - 2, 1)
            else:
                older_taps(N_CHUNK - 2, 1)
                low_down(N_CHUNK - 1, 0)
                product(N_CHUNK - 2, 1)
                older_taps(N_CHUNK - 1, 0)
            product(N_CHUNK - 1, 0)
            for t in range(NT):
                for half in range(2):
                    dve.wait_ge(s["bank_done"], 2 * t + half + 1)
                    cols = slice(half * 512, half * 512 + 512)
                    dve.scalar_tensor_tensor(c.x[:, t, cols], acc[t][half][:], factor, c.x[:, t, cols],
                                             ALU.mult, ALU.add).then_inc(s["residual_done"], 1)

        @block.tensor
        def _(pe):
            turn_tensor(pe, c, c.h, s["h_ready"], s["turned"])
            pe.wait_ge(s["hT_ready"], 2 * NT)

            def hidden(i, slot, first=False):
                for f in range(2):
                    bank = c.ps[2 * slot + f]
                    for part in range(2):
                        if first and f == 0:
                            pe.wait_ge(s["gu_split"] if part else s["first_low"], 1)
                        elif first:
                            pe.wait_ge(s["gu_split"], 2)
                        else:
                            pe.wait_ge(s["gu_split"], i * 2 + part + 1)
                        high, low = w[part][slot]
                        for k in range(KT):
                            last = matmul3(pe, bank[:, part * S:(part + 1) * S],
                                           (high[:, k, f * P:(f + 1) * P], low[:, k, f * P:(f + 1) * P]),
                                           (hT[0][:, k, :], hT[1][:, k, :]), k == 0, k == KT - 1)
                    last.then_inc(s["hidden_ready"], 1)

            def down_bank(slot, f, t, half, start, stop):
                toks, cols = slice(t * P, (t + 1) * P), slice(half * 512, half * 512 + 512)
                return matmul3(pe, acc[t][half][:], (act_high[:, slot, f, toks], act_low[:, slot, f, toks]),
                               tuple(part[:, f, cols] for part in w[2][slot]), start, stop)

            def down(i, slot, first=False):
                pe.wait_ge(s["down_split"], i + 1)
                for f in range(2):
                    pe.wait_ge(s["act_ready"], i * 2 + f + 1)
                    for t in range(NT):
                        for half in range(2):
                            last = down_bank(slot, f, t, half, first and f == 0, False)
                last.then_inc(s["down_done"], 1)

            hidden(0, 0, first=True)
            hidden(1, 1)
            down(0, 0, first=True)
            hidden(2, 0)
            down(1, 1)
            with pe.Fori(0, LOOPS) as i:
                hidden(i * 2 + LOOP0, 1)
                down(i * 2 + LOOP0 - 1, 0)
                hidden(i * 2 + LOOP0 + 1, 0)
                down(i * 2 + LOOP0, 1)
            pe.wait_ge(s["down_split"], N_CHUNK)
            pe.wait_ge(s["act_ready"], 2 * N_CHUNK)
            for t in range(NT):
                for half in range(2):
                    down_bank(0, 0, t, half, False, False)
                    down_bank(0, 1, t, half, False, True).then_inc(s["bank_done"], 1)
    end_phase()
    ctx.close()


RING = 3
UNIT = KT * 2 * P


class Ring:

    def __init__(self, nc, ctx, name, s, used, use_counts, unit=UNIT):
        self.arrived = ctx.enter_context(nc.sbuf_tensor(f"{name}_arrived", [P, RING, unit], F32))
        self.parts = ctx.enter_context(nc.sbuf_tensor(f"{name}_parts", [P, 2, RING, unit], F32R))
        self.s, self.used, self.use_counts = s, used, use_counts

    def load(self, sp, n, src):
        if n >= RING:
            sp.wait_ge(self.s["unit_split"], n - RING + 1)
        width = src.shape[1]
        sp.dma_start(self.arrived[:, n % RING, 0:width], src).then_inc(self.s[f"unit{n % RING}"], 16)

    def high(self, eng, n, width=UNIT, on_pool=False):
        eng.wait_ge(self.s[f"unit{n % RING}"], 16 * (n // RING + 1))
        if n >= RING:
            eng.wait_ge(self.used, self.use_counts[n - RING])
        high, value = self.parts[:, 0, n % RING, 0:width], self.arrived[:, n % RING, 0:width]
        if on_pool:
            eng.tensor_copy(high, value).then_inc(self.s["unit_high"], 1)
        else:
            eng.activation(high, value, ACT.Copy).then_inc(self.s["unit_high"], 1)

    def low(self, eng, n, width=UNIT):
        eng.wait_ge(self.s["unit_high"], n + 1)
        slot = n % RING
        eng.tensor_tensor(self.parts[:, 1, slot, 0:width], self.arrived[:, slot, 0:width],
                          plain(self.parts[:, 0, slot, 0:width]), ALU.subtract).then_inc(self.s["unit_split"], 1)

    def operand(self, n, first, width):
        return tuple(self.parts[:, lo, n % RING, first:first + width] for lo in range(2))


RING_NAMES = " unit0 unit1 unit2 unit_high unit_split"


def both(parts, *index):
    return tuple(parts[(slice(None), lo, *index)] for lo in range(2))


def mixer_buffers(nc, ctx, c):
    def sb(name, shape, dtype=F32):
        return ctx.enter_context(nc.sbuf_tensor(name, shape, dtype))

    c.hT_parts = sb("mixer_T_parts", [P, 2, KT, S], F32R)
    c.wc1 = sb("w_cmp1", [P, 2, CJ, CMP_HID])
    c.wc2 = sb("w_cmp2", [P, 2, 2, 2, DH])
    c.pos = sb("pos", [P, 2, CJ])
    c.raw = sb("raw", [P, N_TURNED, S])
    c.rot = sb("rot", [P, N_ROT, S])
    c.vtok = sb("v_tokens", [P, NT, 2 * P + Q_COLS])
    c.gates = sb("gates", [P, NT, GATE_COLS])
    c.kcols = c.h[:].rearrange("p t d -> p (t d)")[:, 0:2 * GROUPS * CJ * N_CMP].rearrange(
        "p (v g j n) -> p v g j n", v=2, g=GROUPS, j=CJ)
    hid_w = 2 * 2 * GROUPS * 16
    c.hid = c.work[:, 2 * S:2 * S + hid_w].rearrange("p (v f g n) -> p v f g n", v=2, f=2, g=GROUPS)
    c.hid_v = c.work[:, 2 * S + hid_w:2 * S + hid_w + 2 * NH * 16].rearrange("p (f g r n) -> p f g r n", f=2, g=GROUPS, r=REP)
    c.kc = sb("k_cmp", [P, GROUPS, 16])
    c.vc = sb("v_cmp_by_head", [P, NH, DH])


Q_T, KS_T, KW_T, MQ_T, MK_T = 0, 4, 5, 6, 10
N_ROT = 14
CMP_T = N_ROT
N_TURNED = N_ROT + 4

W_IN = 4 * P + 4 * P + 2 * P + 2 * P + GATE_COLS + 3 * Q_COLS
WI_UNITS = [(n * 2 * P, 2 * P) for n in range(5)] + [(10 * P, 2 * P + GATE_COLS)]
WI_UNITS += [(12 * P + GATE_COLS + n * 2 * P, 2 * P) for n in range(6)]


def w_in_columns():
    def head(first, n):
        return list(range(first + n * DH, first + (n + 1) * DH))

    def kv(which):
        return Q_COLS + which * GROUPS * DH

    order = []
    for j in range(REP):
        order += head(0, j) + head(0, REP + j)
    for which in (0, 1):
        for g in range(GROUPS):
            order += head(kv(which), g) * 2
    for which in (2, 4, 3, 5):
        order += head(kv(which), 0) + head(kv(which), 1)
    order += range(kv(6), IN_COLS)
    assert len(order) == W_IN
    return order


def project_phase(nc, c, gain, w_in, pos, w_c1, w_c2):
    s, end_phase = semaphores(nc, "project", "gain_loaded hT_high pos_loaded wc1_loaded wc2_loaded sumsq_ready root_ready "
                            "rstd_ready h_ready turned hT_ready projected copied swapped cos_done "
                            "sin_done rotated kcols_ready pad_ready hid_ready gelu_ready repeated kv_ready kv_copied" + RING_NAMES)
    jobs = [(j // 2, j % 2 * P, "rotate", Q_T + j) for j in range(4)]
    jobs += [(2 + j // 2, j % 2 * P, "plain", CMP_T + j) for j in range(4)]
    jobs += [(4, 0, "rotate", KS_T), (4, P, "rotate", KW_T), (5, 0, "tokens", 0), (5, 0, "tokens", 1)]
    jobs += [(6 + j // 2, j % 2 * P, "rotate", MQ_T + j) for j in range(8)]
    jobs += [(10 + half, 0, "values", 1 + half) for half in range(2)]
    N_UNITS = len(WI_UNITS)
    last_job = [max(i for i, job in enumerate(jobs) if job[0] == u) for u in range(N_UNITS)]
    ctx = ExitStack()
    ring = Ring(nc, ctx, "project", s, s["projected"], [last + 1 for last in last_job],
                max(KT * n for _, n in WI_UNITS))
    rotated_jobs = [i for i, j in enumerate(jobs) if j[2] == "rotate"]
    cmp_done = max(i for i, j in enumerate(jobs) if j[2] == "plain") + 1
    hid_bank, kv_bank = c.ps[4], c.ps[5]

    def width(n):
        return KT * WI_UNITS[n][1]

    with nc.Block() as block:
        @block.sync
        def _(sp):
            load_gain(sp, c, gain, s["gain_loaded"])
            at = 0
            for n in range(N_UNITS):
                ring.load(sp, n, w_in[:, at:at + width(n)])
                at += width(n)
                if n == 2:
                    for kv in range(2):
                        sp.dma_start(c.pos[:, kv, :], pos[kv].rearrange("(j u) d -> (u d) j", u=2),
                                     allow_slow_non_contiguous=True).then_inc(s["pos_loaded"], 16)
                if n == 7:
                    for kv in range(2):
                        sp.dma_start(c.wc1[:, kv], w_c1[kv].rearrange("(j p) n -> p j n", p=P)).then_inc(s["wc1_loaded"], 16)
                        for u in range(2):
                            sp.dma_start(c.wc2[:, kv, :, u], w_c2[kv].rearrange("(j p) n -> p j n", p=P)).then_inc(s["wc2_loaded"], 16)

        @block.scalar
        def _(act):
            norm_scalar(act, c, s["sumsq_ready"], s["root_ready"])
            ring.high(act, 0, width(0))
            turned_high_scalar(act, c, c.hT_parts[:, 0], s["turned"], s["hT_high"])
            for n in range(1, RING):
                ring.high(act, n, width(n))
            for i, (unit, _, kind, to) in enumerate(jobs):
                bank = c.ps[i % 2]
                act.wait_ge(s["projected"], i + 1)
                if kind in ("rotate", "plain"):
                    last = act.activation(c.raw[:, to, :], bank[:, 0:S], ACT.Copy)
                elif kind == "tokens":
                    act.activation(c.gates[:, to], bank[:, 2 * P:2 * P + GATE_COLS], ACT.Sigmoid)
                    last = act.activation(c.vtok[:, to, 0:2 * P], bank[:, 0:2 * P], ACT.Copy)
                else:
                    last = act.activation(c.vtok[:, :, to * S:(to + 1) * S], bank[:].rearrange("p (t n) -> p t n", t=NT), ACT.Copy)
                last.then_inc(s["copied"], 1)
                if i == last_job[unit] and unit + RING < N_UNITS:
                    ring.high(act, unit + RING, width(unit + RING))
            act.wait_ge(s["hid_ready"], 1)
            act.wait_ge(s["pad_ready"], 1)
            hid = hid_bank[:, 0:4 * GROUPS * 16].rearrange("p (v f g n) -> p (v f) g n", v=2, f=2, n=16)
            act.activation(c.hid.rearrange("p v f g n -> p (v f) g n")[:, :, :, 0:N_CMP], hid[:, :, :, 0:N_CMP],
                           ACT.Gelu_apprx_tanh).then_inc(s["gelu_ready"], 1)

        @block.gpsimd
        def _(pool):
            pool.memset(c.hid, 0.0).then_inc(s["pad_ready"], 1)
            for n, i in enumerate(rotated_jobs):
                to = jobs[i][3]
                pool.wait_ge(s["copied"], i + 1)
                if n >= 2:
                    pool.wait_ge(s["rotated"], n - 1)
                pool.tensor_tensor(c.work[:, (n % 2) * S:(n % 2 + 1) * S], c.raw[:, to, :], c.cos,
                                   ALU.mult).then_inc(s["cos_done"], 1)
                pool.wait_ge(s["cos_done"], n + 1)
                pool.wait_ge(s["sin_done"], n + 1)
                pool.tensor_tensor(c.rot[:, to, :], c.rot[:, to, :], c.work[:, (n % 2) * S:(n % 2 + 1) * S],
                                   ALU.add).then_inc(s["rotated"], 1)
            pool.wait_ge(s["gelu_ready"], 1)
            pool.tensor_copy(c.hid_v.rearrange("p f g r n -> p (f g) r n"),
                             c.hid[:, 1].rearrange("p f g n -> p (f g) n").unsqueeze(2).to_broadcast([P, 4, REP, 16])
                             ).then_inc(s["repeated"], 1)

        @block.vector
        def _(dve):
            norm_vector(dve, c, s["gain_loaded"], s["root_ready"], s["rstd_ready"], s["h_ready"])
            ring.low(dve, 0, width(0))
            turned_low_vector(dve, c, c.hT_parts[:, 0], c.hT_parts[:, 1], s["hT_high"], s["hT_ready"])
            for n in range(1, RING):
                ring.low(dve, n, width(n))
            n = 0
            for i, (unit, _, kind, to) in enumerate(jobs):
                if kind == "rotate":
                    dve.wait_ge(s["swapped"], n + 1)
                    dve.tensor_tensor(c.rot[:, to, :], c.ps[2 + n % 2][:, 0:S], c.sin, ALU.mult).then_inc(s["sin_done"], 1)
                    n += 1
                if i == last_job[unit] and unit + RING < N_UNITS:
                    ring.low(dve, unit + RING, width(unit + RING))
                if i + 1 == cmp_done:
                    dve.wait_ge(s["copied"], cmp_done)
                    dve.wait_ge(s["pos_loaded"], 32)
                    for v in range(2):
                        for g in range(GROUPS):
                            raw = c.raw[:, CMP_T + 2 * v + g, :].rearrange("p (m j r) -> p r j m", r=2, j=8)
                            for half in range(2):
                                rows = slice(half * DH, (half + 1) * DH)
                                for jh in range(2):
                                    js = slice(8 * jh, 8 * jh + 8)
                                    add = c.pos[rows, v, js].unsqueeze(2).to_broadcast([DH, 8, N_CMP])
                                    last = dve.tensor_tensor(c.kcols[rows, v, g, js, :],
                                                             raw[rows, half, :, jh:jh + N_CMP], add, ALU.add)
                    last.then_inc(s["kcols_ready"], 1)
            dve.wait_ge(s["kv_ready"], 1)
            dve.tensor_copy(c.kc[:], kv_bank[:, 0:GROUPS * 16].rearrange("p (g n) -> p g n", n=16)).then_inc(s["kv_copied"], 1)
            vc = kv_bank[:, 64:64 + DH].unsqueeze(1).to_broadcast([P, NH, DH])
            own = c.head_of_row.unsqueeze(2).to_broadcast([P, NH, DH])
            dve.tensor_tensor(c.vc[:], vc, own, ALU.mult).then_inc(s["kv_copied"], 1)

        @block.tensor
        def _(pe):
            turn_tensor(pe, c, c.h, s["h_ready"], s["turned"])
            pe.wait_ge(s["hT_ready"], 2 * NT)

            def swap(n, i):
                pe.wait_ge(s["copied"], i + 1)
                if n >= 2:
                    pe.wait_ge(s["sin_done"], n - 1)
                pe.matmul(c.ps[2 + n % 2][:, 0:S], c.swap, c.raw[:, jobs[i][3], :], start=True, stop=True).then_inc(s["swapped"], 1)

            waiting, n = [], 0
            for i, (unit, col, kind, to) in enumerate(jobs):
                bank = c.ps[i % 2]
                pe.wait_ge(s["unit_split"], unit + 1)
                if i >= 2:
                    pe.wait_ge(s["copied"], i - 1)
                n_cols = WI_UNITS[unit][1]
                if kind in ("rotate", "plain"):
                    for k in range(KT):
                        last = matmul3(pe, bank[:, 0:S], ring.operand(unit, k * n_cols + col, P), both(c.hT_parts, k),
                                       k == 0, k == KT - 1)
                else:
                    for t in (to,) if kind == "tokens" else range(NT):
                        at = 0 if kind == "tokens" else t * n_cols
                        for k in range(KT):
                            last = matmul3(pe, bank[:, at:at + n_cols], both(c.hT_parts, k, slice(t * P, (t + 1) * P)),
                                           ring.operand(unit, k * n_cols, n_cols), k == 0, k == KT - 1)
                last.then_inc(s["projected"], 1)
                if waiting:
                    swap(n, waiting.pop())
                    n += 1
                if kind == "rotate":
                    waiting.append(i)
            assert not waiting
            pe.wait_ge(s["kcols_ready"], 1)
            pe.wait_ge(s["wc1_loaded"], 32)
            for v in range(2):
                for f in range(2):
                    at = (2 * v + f) * GROUPS * 16
                    out = hid_bank[:, at:at + GROUPS * 16].rearrange("p (g n) -> p g n", n=16)[:, :, 0:N_CMP]
                    for j in range(CJ):
                        last = pe.matmul(out, c.wc1[:, v, j, f * P:(f + 1) * P], c.kcols[:, v, :, j, :],
                                         start=(j == 0), stop=(j == CJ - 1))
            last.then_inc(s["hid_ready"], 1)
            pe.wait_ge(s["gelu_ready"], 1)
            pe.wait_ge(s["wc2_loaded"], 64)
            pe.wait_ge(s["repeated"], 1)
            for f in range(2):
                pe.matmul(kv_bank[:, 0:GROUPS * 16], c.wc2[:, 0, f].rearrange("p u d -> p (u d)"),
                          c.hid[:, 0, f], start=(f == 0), stop=(f == 1))
            for f in range(2):
                last = pe.matmul(kv_bank[:, 64:64 + DH], c.hid_v[:, f].rearrange("p g r n -> p (g r n)"),
                                 c.wc2[:, 1, f, 0, :], start=(f == 0), stop=(f == 1))
            last.then_inc(s["kv_ready"], 1)
    end_phase()
    ctx.close()


def attend_phase(nc, c, w_out):
    s, end_phase = semaphores(nc, "attend", "cmp_scored cmp_masked cmp_max_ready cmp_shifted cmp_exp cmp_kept cmp_sum_ready "
                           "cmp_turned cmp_pT_ready scored masked exp_ready turned pT_ready added "
                           "norm_step combined o_turned oT_high oT_ready unit_used out_ready residual_done" + RING_NAMES)
    N_UNITS = KT // 2
    ctx = ExitStack()
    ring = Ring(nc, ctx, "attend", s, s["unit_used"], [n + 1 for n in range(N_UNITS)])
    area = ctx.enter_context(nc.sbuf_tensor("attention", [P, 9 * S + 3 * NT * 4 * NH + 3 * NT * P + NT * NH], F32))
    at = 0

    def scratch(n):
        nonlocal at
        at += n
        return area[:, at - n:at]

    scores = [scratch(S) for _ in range(3)]
    probs = [scratch(S) for _ in range(3)]
    probsT = [scratch(S) for _ in range(3)]
    low = scratch(NT * 4 * NH)
    total = scratch(NT * 4 * NH)
    weight = scratch(NT * 4 * NH)
    cs, cp, cpT = scratch(NT * P), scratch(NT * P), scratch(NT * P)
    c_low = scratch(NT * NH)
    parts = [c.work[:, b * Q_COLS:(b + 1) * Q_COLS] for b in range(3)]
    o = c.h
    units = []
    for t in range(NT):
        units += [(t, b, h) for h in range(NH) for b in (1, 2)]
        units += [(t, 3, h) for h in range(NH)]
    PER_T = len(units) // NT

    def column(t, b, h):
        return (t * 4 + b) * NH + h

    def operands(t, b, h):
        if b == 3:
            rows = slice((h % 2) * DH, (h % 2 + 1) * DH)
            return rows, MQ_T + h // 2, MK_T + h // 2, 2 * P + h * DH
        g = h // REP
        return slice(g * DH, (g + 1) * DH), Q_T + h % REP, (KS_T, KW_T)[b - 1], (b - 1) * P + g * DH

    with nc.Block() as block:
        @block.sync
        def _(sp):
            for n in range(N_UNITS):
                ring.load(sp, n, w_out[n * P:(n + 1) * P, :])

        @block.gpsimd
        def _(pool):
            for n in range(RING):
                ring.high(pool, n, on_pool=True)
                ring.low(pool, n)

        @block.scalar
        def _(act):
            def copy_probs(act, u):
                keys = (units[u][0] + 1) * P
                act.wait_ge(s["turned"], u + 1)
                if u >= 3:
                    act.wait_ge(s["added"], u - 2)
                act.activation(probsT[u % 3][:, 0:keys], c.ps[2 + u % 2][:, 0:keys], ACT.Copy).then_inc(s["pT_ready"], 1)

            act.wait_ge(s["cmp_shifted"], 1)
            act.activation(cp, cs, ACT.Exp).then_inc(s["cmp_exp"], 1)
            for u in range(len(units)):
                keys = (units[u][0] + 1) * P
                col = column(*units[u])
                act.wait_ge(s["masked"], u + 1)
                if u >= 3:
                    act.wait_ge(s["turned"], u - 2)
                act.activation(probs[u % 3][:, 0:keys], scores[u % 3][:, 0:keys], ACT.Exp, scale=-1.0,
                               bias=low[:, col:col + 1], accum_out=total[:, col:col + 1]).then_inc(s["exp_ready"], 1)
                if u >= 2:
                    copy_probs(act, u - 2)
            for u in range(len(units) - 2, len(units)):
                copy_probs(act, u)
            for b in range(2 * NT):
                t, k = b // 2, (b % 2) * 4
                act.wait_ge(s["o_turned"], b + 1)
                act.activation(c.hT_parts[:, 0, k:k + 4, t * P:(t + 1) * P], c.ps[b][:].rearrange("p (k n) -> p k n", k=4),
                               ACT.Copy).then_inc(s["oT_high"], 1)
            for n in range(RING, N_UNITS):
                act.wait_ge(s["unit_split"], RING)
                ring.high(act, n)

        @block.vector
        def _(dve):
            def compressed():
                shape = [P, NT, NH, 16]
                sc, cs4, cp4 = (a.rearrange("p (t h n) -> p t h n", t=NT, h=NH) for a in (c.ps[7][:, 0:NT * P], cs, cp))
                neg, one = (a.rearrange("p (t n) -> p t n", t=NT).unsqueeze(2).to_broadcast(shape)
                            for a in (c.cmp_neg, c.cmp_one))
                dve.wait_ge(s["cmp_scored"], GROUPS * NT)
                for t in range(NT):
                    last = dve.scalar_tensor_tensor(cs4[:, t], sc[:, t], SCALE, neg[:, t], ALU.mult, ALU.add)
                last.then_inc(s["cmp_masked"], 1)
                dve.wait_ge(s["cmp_masked"], 1)
                flat = cs.rearrange("p (a n) -> p a n", n=16)
                dve.tensor_reduce(c_low, flat, AX, ALU.max).then_inc(s["cmp_max_ready"], 1)
                dve.wait_ge(s["cmp_max_ready"], 1)
                dve.tensor_tensor(flat, flat, c_low.unsqueeze(2).to_broadcast([P, NT * NH, 16]),
                                  ALU.subtract).then_inc(s["cmp_shifted"], 1)
                dve.wait_ge(s["cmp_exp"], 1)
                for t in range(NT):
                    last = dve.tensor_tensor(cp4[:, t], cp4[:, t], one[:, t], ALU.mult)
                last.then_inc(s["cmp_kept"], 1)
                dve.wait_ge(s["cmp_kept"], 1)
                for t in range(NT):
                    col = column(t, 0, 0)
                    last = dve.tensor_reduce(total[:, col:col + NH], cp4[:, t], AX, ALU.add)
                last.then_inc(s["cmp_sum_ready"], 1)
                dve.wait_ge(s["cmp_turned"], 1)
                dve.tensor_copy(cpT, c.ps[7][:, 2 * P:(2 + NT) * P]).then_inc(s["cmp_pT_ready"], 1)

            steps = 0

            def step(ins):
                nonlocal steps
                steps += 1
                ins.then_inc(s["norm_step"], 1)
                dve.wait_ge(s["norm_step"], steps)

            def weights(t, b, n_b):
                lo = column(t, b, 0)
                cols = slice(lo, lo + n_b * NH)
                step(dve.tensor_scalar(weight[:, cols], total[:, cols], 1.0, None, ALU.max))
                step(dve.reciprocal(weight[:, cols], weight[:, cols]))

            def gated(t):
                wts = weight[:, column(t, 0, 0):column(t, 3, 0)].rearrange("p (b h) -> p b h", b=3)
                return wts, c.gates[:, t, :].rearrange("p (h b) -> p b h", b=3)

            def nsa_weights(t):
                dve.wait_ge(s["added"], t * PER_T + 2 * NH)
                dve.wait_ge(s["cmp_sum_ready"], 1)
                dve.wait_ge(s["exp_ready"], t * PER_T + 2 * NH)
                weights(t, 0, 3)
                wts, gate = gated(t)
                step(dve.tensor_tensor(wts, wts, gate, ALU.mult))

            def nsa_part(t, b):
                wts = gated(t)[0]
                step(dve.tensor_tensor(parts[b].rearrange("p (h d) -> p h d", d=DH),
                                       c.ps[4 + b][:].rearrange("p (h d) -> p h d", d=DH),
                                       wts[:, b, :].unsqueeze(2).to_broadcast([P, NH, DH]), ALU.mult))

            def nsa(t, n):
                stage = n - (2 * NH + 2)
                if stage == 0:
                    nsa_weights(t)
                elif 1 <= stage <= 3:
                    nsa_part(t, stage - 1)
                elif stage == 4:
                    step(dve.tensor_tensor(parts[0], parts[0], parts[1], ALU.add))
                elif stage == 5:
                    dve.tensor_tensor(o[:, t, 0:Q_COLS], parts[0], parts[2], ALU.add).then_inc(s["combined"], 1)

            def moba(t):
                dve.wait_ge(s["added"], (t + 1) * PER_T)
                dve.wait_ge(s["exp_ready"], (t + 1) * PER_T)
                weights(t, 3, 1)
                wts = weight[:, column(t, 3, 0):column(t, 3, 0) + NH].unsqueeze(2).to_broadcast([P, NH, DH])
                dve.tensor_tensor(o[:, t, Q_COLS:].rearrange("p (h d) -> p h d", d=DH),
                                  c.ps[7][:].rearrange("p (h d) -> p h d", d=DH), wts, ALU.mult).then_inc(s["combined"], 1)

            def mask(u):
                t, b, h = units[u]
                keys = (t + 1) * P
                col = column(t, b, h)
                dve.wait_ge(s["scored"], u + 1)
                if u >= 3:
                    dve.wait_ge(s["exp_ready"], u - 2)
                dve.tensor_tensor_reduce(scores[u % 3][:, 0:keys], c.ps[u % 2][:, 0:keys], c.causal[:, S - keys:S],
                                         -SCALE, 3e38, ALU.add, ALU.min, low[:, col:col + 1]).then_inc(s["masked"], 1)

            compressed()
            for u in range(len(units)):
                t, n = u // PER_T, u % PER_T
                mask(u)
                nsa(t, n)
                if t and n == 3:
                    moba(t - 1)
            moba(NT - 1)

            for b in range(2 * NT):
                t, k = b // 2, (b % 2) * 4
                dve.wait_ge(s["oT_high"], b + 1)
                oT_high, oT_low = both(c.hT_parts, slice(k, k + 4), slice(t * P, (t + 1) * P))
                dve.tensor_tensor(oT_low, c.ps[b][:].rearrange("p (k n) -> p k n", k=4), plain(oT_high), ALU.subtract
                                  ).then_inc(s["oT_ready"], 1)
            for n in range(RING, N_UNITS):
                ring.low(dve, n)
            for b in range(2 * NT):
                t, half = b // 2, b % 2
                dve.wait_ge(s["out_ready"], b + 1)
                cols = slice(half * 512, half * 512 + 512)
                dve.tensor_tensor(c.x[:, t, cols], c.ps[4 + b][:], c.x[:, t, cols], ALU.add).then_inc(s["residual_done"], 1)

        @block.tensor
        def _(pe):
            def compressed_scores(t):
                for h in range(NH):
                    g = h // REP
                    rows = slice(g * DH, (g + 1) * DH)
                    last = pe.matmul(c.ps[7][:, t * P + h * 16:t * P + (h + 1) * 16],
                                     c.raw[rows, Q_T + h % REP, t * P:(t + 1) * P], c.kc[rows, g, :], start=True, stop=True)
                    if h % REP == REP - 1:
                        last.then_inc(s["cmp_scored"], 1)
                        pe.wait_ge(s["cmp_scored"], GROUPS * t + g + 1)

            def compressed_sum(t):
                pe.wait_ge(s["cmp_pT_ready"], 1)
                if t:
                    pe.wait_ge(s["combined"], 2 * t - 1)
                pe.matmul(c.ps[4][:], cpT[:, t * P:(t + 1) * P], c.vc[:].rearrange("p h d -> p (h d)"), start=True, stop=True)

            def score(u):
                t, b, h = units[u]
                rows, q, k, _ = operands(t, b, h)
                if u >= 2:
                    pe.wait_ge(s["masked"], u - 1)
                keep_clock(pe, c, c.ps[u % 2][:, 2 * P:3 * P], 1 - t)
                pe.matmul(c.ps[u % 2][:, 0:(t + 1) * P], c.rot[rows, q, t * P:(t + 1) * P],
                          c.rot[rows, k, 0:(t + 1) * P], start=True, stop=True).then_inc(s["scored"], 1)

            def turn(u):
                t = units[u][0]
                pe.wait_ge(s["exp_ready"], u + 1)
                if u >= 2:
                    pe.wait_ge(s["pT_ready"], u - 1)
                for kt in range(t + 1):
                    last = pe.transpose(c.ps[2 + u % 2][:, kt * P:(kt + 1) * P], probs[u % 3][:, kt * P:(kt + 1) * P], c.ident)
                last.then_inc(s["turned"], 1)

            def add(u):
                t, b, h = units[u]
                v = operands(t, b, h)[3]
                pe.wait_ge(s["pT_ready"], u + 1)
                if t:
                    pe.wait_ge(s["combined"], 2 * t - 1 if b < 3 else 2 * t)
                for kt in range(t + 1):
                    last = pe.matmul(c.ps[4 + b][:, h * DH:(h + 1) * DH], probsT[u % 3][:, kt * P:(kt + 1) * P],
                                     c.vtok[:, kt, v:v + DH], start=(kt == 0), stop=(kt == t))
                last.then_inc(s["added"], 1)

            for t in range(NT):
                compressed_scores(t)
            keep_clock(pe, c, c.ps[0][:, 0:P], 12)
            pe.wait_ge(s["cmp_kept"], 1)
            for t in range(NT):
                last = pe.transpose(c.ps[7][:, (2 + t) * P:(3 + t) * P], cp[:, t * P:(t + 1) * P], c.ident)
            last.then_inc(s["cmp_turned"], 1)
            for u in range(len(units) + 3):
                if u < len(units):
                    score(u)
                if 2 <= u < len(units) + 2:
                    turn(u - 2)
                if u >= 3:
                    if (u - 3) % PER_T == 0:
                        compressed_sum((u - 3) // PER_T)
                    add(u - 3)
            for t in range(NT):
                pe.wait_ge(s["combined"], 2 * NT)
                for k in range(KT):
                    last = pe.transpose(c.ps[2 * t + k // 4][:, (k % 4) * P:(k % 4 + 1) * P], o[:, t, k * P:(k + 1) * P], c.ident)
                    if k % 4 == 3:
                        last.then_inc(s["o_turned"], 1)
            pe.wait_ge(s["oT_ready"], 2 * NT)
            for n in range(N_UNITS):
                pe.wait_ge(s["unit_split"], n + 1)
                for b in range(2 * NT):
                    t, half = b // 2, b % 2
                    for k in range(2):
                        last = matmul3(pe, c.ps[4 + b][:], both(c.hT_parts, 2 * n + k, slice(t * P, (t + 1) * P)),
                                       ring.operand(n, k * D + half * 512, 512), n + k == 0, 2 * n + k == KT - 1)
                    if n == N_UNITS - 1:
                        last.then_inc(s["out_ready"], 1)
                if n < N_UNITS - 1:
                    last.then_inc(s["unit_used"], 1)
    end_phase()
    ctx.close()


SHARED = ("ident", "eps")


def load_tables(nc, c, ctx, name, tables, dram, x=None):
    place, width = layout(tables)
    sb = ctx.enter_context(nc.sbuf_tensor(f"{name}_tables", [P, width], F32))
    s, end_phase = semaphores(nc, f"{name}_tables", "loaded")
    with nc.Block() as block:
        @block.sync
        def _(sp):
            sp.dma_start(sb[:], dram).then_inc(s["loaded"], 16)
            if x is not None:
                sp.dma_start(c.x[:], x.rearrange("b (t p) d -> p (b t) d", p=P)).then_inc(s["loaded"], 16)
            sp.wait_ge(s["loaded"], 16 if x is None else 32)
    end_phase()
    return {key: sb[:, at:at + n] for key, (at, n) in place.items()}


def build(nc, a, out):
    with ExitStack() as ctx:
        def sb(name, shape, stack=ctx):
            return stack.enter_context(nc.sbuf_tensor(name, shape, F32))

        c = Chip()
        c.x = sb("residual", [P, NT, D])
        c.h = sb("normed", [P, NT, D])
        c.stat = sb("norm_stats", [P, 8])
        c.work = sb("work", [P, 8 * S])
        c.gain = c.work[:, D:2 * D]
        c.ps = [ctx.enter_context(nc.psum_tensor(f"bank{i}", [P, 512], F32)) for i in range(8)]

        t = load_tables(nc, c, ctx, "shared", {k: v for k, v in constants().items() if k in SHARED},
                        a["constants_shared"], a["x"])
        c.ident, c.eps = t["ident"], t["eps"]
        with ExitStack() as first:
            t = load_tables(nc, c, first, "first", {k: v for k, v in constants().items() if k not in SHARED},
                            a["constants"])
            c.swap, c.cos, c.sin, c.causal = t["swap"], t["cos"], t["sin"], t["causal"]
            c.cmp_neg, c.cmp_one, c.head_of_row = t["cmp_neg"], t["cmp_one"], t["head_of_row"]

            with nc.Fori(0, DEPTH) as l:
                ffn_phase(nc, c, "ffn1", a["norm_ffn1"][l], a["ffn1"][l])
                with ExitStack() as mixer:
                    mixer_buffers(nc, mixer, c)
                    project_phase(nc, c, a["norm_mix"][l], a["w_in"][l], (a["pos_ck"][l], a["pos_cv"][l]),
                                  (a["w_ck1"][l], a["w_cv1"][l]), (a["w_ck2"][l], a["w_cv2"][l]))
                    attend_phase(nc, c, a["w_out"][l])
                ffn_phase(nc, c, "ffn2", a["norm_ffn2"][l], a["ffn2"][l])
            final_norm_phase(nc, c, "norm_final", a["norm_final"])

        second_block(nc, c, ctx, a, out)


def final_norm_phase(nc, c, name, gain, out=None):
    s, end_phase = semaphores(nc, name, "gain_loaded sumsq_ready root_ready rstd_ready scaled stored")
    rows = c.work[:, 0:D]
    with nc.Block() as block:
        @block.sync
        def _(sp):
            sp.dma_start(rows, gain.unsqueeze(0).to_broadcast([P, D])).then_inc(s["gain_loaded"], 16)
            if out is not None:
                for t in range(NT):
                    sp.wait_ge(s["scaled"], t + 1)
                    sp.dma_start(out[0, t * P:(t + 1) * P, :], c.x[:, t, :]).then_inc(s["stored"], 16)
                sp.wait_ge(s["stored"], 16 * NT)

        @block.scalar
        def _(act):
            norm_scalar(act, c, s["sumsq_ready"], s["root_ready"])

        @block.vector
        def _(dve):
            dve.wait_ge(s["root_ready"], NT)
            dve.reciprocal(c.stat[:, 4:6], c.stat[:, 2:4]).then_inc(s["rstd_ready"], 1)
            dve.wait_ge(s["rstd_ready"], 1)
            dve.wait_ge(s["gain_loaded"], 16)
            for t in range(NT):
                dve.scalar_tensor_tensor(c.x[:, t, :], c.x[:, t, :], c.stat[:, 4 + t:5 + t], rows,
                                         ALU.mult, ALU.mult).then_inc(s["scaled"], 1)
    end_phase()


RW_W, RW_GATE = 512, 128
HALF = RW_W // NT
RW_T = 14
PAIRS = 4
RW_COLS = RW_T * P
RET_H, RET_V = 4, 128
RET_OFF = RW_COLS
SG_OFF = RET_OFF + 2 * RET_H * DH + 2 * RET_H * RET_V
SG_W = 512
GATE_OFF = SG_OFF + 2 * SG_W
BR_W, N_BRANCH = 512, 3
DECAY = float(np.exp(-0.5))
LEVELS = 7
UNITS = 2 * NH
MIX_COLS = KT * P + 4 * P
PROJECT_COLS = [512, 768, 1536, 0, 256, 1024, 1280] + list(range(RET_OFF, GATE_OFF, 2 * P))
CONV_W = 16


def second_constants():
    c = {}
    half = DH // 2
    inv = (1.0 / (np.float32(10000.0) ** np.linspace(0.0, 1.0, half, dtype=np.float32))).astype(np.float32)
    ang = np.arange(S, dtype=np.float32)[:, None] * inv[None, :]
    cos, sin, swap = np.ones((P, S), np.float32), np.zeros((P, S), np.float32), np.zeros((P, P), np.float32)
    for base in (0, DH):
        for i in range(half):
            for d, src, sign in ((base + i, base + i + half, -1), (base + i + half, base + i, 1)):
                cos[d], sin[d] = np.cos(ang[:, i]), sign * np.sin(ang[:, i])
                swap[src, d] = 1
    c["ret_swap"], c["ret_cos"], c["ret_sin"] = swap, cos, sin
    gamma = 1.0 - 2.0 ** (-5.0 - np.arange(RET_H))
    j, i = np.arange(P)[:, None], np.arange(S)[None, :]
    for h in range(RET_H):
        first = np.where(i >= j, gamma[h] ** np.maximum(i - j, 0), 0)
        c[f"ret_decay{h}"] = np.concatenate([first, first[:, :P]], 1).astype(np.float32)
    s, t = np.arange(P)[:, None], np.arange(P)[None, :]
    before, until = (s < t).astype(np.float32), (s <= t).astype(np.float32)
    c["rw_mask"] = np.concatenate([before, until, before, until], 1)
    c["rw_mask_t"] = np.ascontiguousarray(before.T)
    for level in range(LEVELS):
        b = 2**level
        low = ((s // (2 * b) == t // (2 * b)) & (s % (2 * b) >= b) & (t % (2 * b) < b)).astype(np.float32)
        c[f"level{level}"] = low
    c["minus_level0_t"] = -np.ascontiguousarray(c["level0"].T)
    c["same_head"] = (s // DH == t // DH).astype(np.float32)
    c["head_pair"] = (s // DH == np.arange(2)[None, :]).astype(np.float32)
    c["rw_eps"] = np.full((P, 1), 64e-5, np.float32)
    c["ones"] = np.ones((P, P), np.float32)
    return c


def second_buffers(nc, ctx, c):
    def sb(name, shape, dtype=F32):
        return ctx.enter_context(nc.sbuf_tensor(name, shape, dtype))

    c.hT_parts = sb("normed_T_parts", [P, 2, KT, S], F32R)
    c.vecs = sb("vectors", [P, 40])
    c.mu, c.w0, c.a0, c.k_k, c.k_a, c.r_k = (c.vecs[:, a:b] for a, b in
                                             ((0, 14), (14, 18), (18, 22), (22, 26), (26, 30), (30, 34)))
    c.low_rank = sb("low_rank", [P, 2 * RW_W])
    c.vt = sb("rw_v_tokens", [P, NT, RW_W])
    c.ret_rot = sb("ret_rot", [P, 4, S])
    c.ret_v = sb("ret_v", [P, NT, RET_H * RET_V])
    c.ret_g = sb("ret_g", [P, NT, RET_H * RET_V])
    c.y_rw = c.low_rank[:].rearrange("p (k n) -> p k n", n=S)
    c.st = sb("row_stats", [P, 64])


def recurrence_buffers(nc, ctx, c):
    def sb(name, shape):
        return ctx.enter_context(nc.sbuf_tensor(name, shape, F32))

    c.rw = sb("rw", [P, 12, PAIRS * S])
    c.raw2 = sb("raw2", [P, 2, S + 1])
    c.diff = sb("diff", [P, 2, S])
    c.thin = sb("thin", [P, 2, S])
    c.gt = sb("rw_g_tokens", [P, NT, RW_W])
    c.bonus = sb("rw_bonus", [P, NT, NH])
    c.rw_small = sb("rw_small", [P, 3, PAIRS, NT])


R_, K_, V_, A_, LW, KK, BH, KH, KR, KR2, E1, E2 = range(12)


def rw_project_phase(nc, c, gain, w_in, vecs, w_up, a_up, g_up):
    s, end_phase = semaphores(nc, "rw_project", "gain_loaded hT_high vecs_loaded low_loaded sumsq_ready root_ready "
                               "rstd_ready h_ready turned hT_ready projected copied zeroed diffed mixed "
                               "thin_ready small_ready z_ready act_step kk_ready heads_summed norm_ready "
                               "swapped cos_done sin_done rotated v_turned v_copied rk_ready bonus_ready g_ready "
                               "dve_step centred kk_normed exps_ready" + RING_NAMES)
    jobs = [(n // 2, n % 2 * P, "rw", to) for n, to in enumerate(
        [(K_, j) for j in range(4)] + [("thin", j) for j in range(2)] + [(which, j) for which in (R_, V_) for j in range(4)])]
    jobs += [(7 + j // 2, j % 2 * P, "ret", j) for j in range(4)]
    jobs += [(9 + n, 0, kind, n % 2) for n, kind in enumerate("ret_v ret_v ret_g ret_g sg_u sg_u sg_v sg_v".split())]
    N_UNITS = len(PROJECT_COLS)
    last_job = [max(i for i, job in enumerate(jobs) if job[0] == u) for u in range(N_UNITS)]
    POOL_FROM = 9
    ctx = ExitStack()
    ring = Ring(nc, ctx, "rw_project", s, s["projected"], [last + 1 for last in last_job])
    mu_of = {K_: 4, R_: 0, V_: 8, "thin": 12}
    N_RW = 14
    rw = c.rw[:]
    rw3 = rw.rearrange("p b (j n) -> p b j n", j=PAIRS)
    rw4 = rw.rearrange("p b (j c n) -> p b j c n", j=PAIRS, c=NT)
    kr = rw[:, KR:KR + 2, :].rearrange("p a n -> p (a n)").rearrange("p (j c x n) -> p j c x n", j=PAIRS, c=NT, x=2)
    sg = c.h[:].rearrange("p t (x n) -> p t x n", x=2)
    ret_raw = rw3[:, KR]

    def mixed_place(to):
        which, j = to
        return c.thin[:, j, :] if which == "thin" else rw3[:, which, j]

    with nc.Block() as block:
        @block.sync
        def _(sp):
            load_gain(sp, c, gain, s["gain_loaded"])
            sp.dma_start(c.vecs[:, 0:34], vecs).then_inc(s["vecs_loaded"], 16)
            for n in range(N_UNITS):
                ring.load(sp, n, w_in[n * P:(n + 1) * P, :])
                if n == 2:
                    sp.dma_start(c.low_rank[0:DH, 0:RW_W], w_up).then_inc(s["low_loaded"], 16)
                    sp.dma_start(c.low_rank[DH:P, 0:RW_W], a_up).then_inc(s["low_loaded"], 16)
                    sp.dma_start(c.low_rank[:, RW_W:], g_up).then_inc(s["low_loaded"], 16)

        @block.scalar
        def _(act):
            norm_scalar(act, c, s["sumsq_ready"], s["root_ready"])
            ring.high(act, 0)
            turned_high_scalar(act, c, c.hT_parts[:, 0], s["turned"], s["hT_high"])
            for n in range(1, RING):
                ring.high(act, n)

            def copies(lo, hi):
                for i in range(lo, hi):
                    unit, _, kind, to = jobs[i]
                    act.wait_ge(s["projected"], i + 1)
                    bank = c.ps[i % 2]
                    if kind == "rw":
                        if i >= 2:
                            act.wait_ge(s["mixed"], i - 1)
                        last = act.activation(c.raw2[:, i % 2, 1:], bank[:, 0:S], ACT.Copy)
                    elif kind == "ret":
                        last = act.activation(ret_raw[:, to], bank[:, 0:S], ACT.Copy, scale=1.0 if to < 2 else DH**-0.5)
                    else:
                        src, cols = bank[:].rearrange("p (t n) -> p t n", t=NT), slice(to * S, (to + 1) * S)
                        dst, func = {"ret_v": (c.ret_v, ACT.Copy), "ret_g": (c.ret_g, ACT.Silu),
                                     "sg_u": (sg[:, :, 0], ACT.Gelu), "sg_v": (sg[:, :, 1], ACT.Gelu)}[kind]
                        last = act.activation(dst[:, :, cols], src, func)
                    last.then_inc(s["copied"], 1)
                    if i == last_job[unit] and unit + RING < N_UNITS:
                        ring.high(act, unit + RING)

            copies(0, 8)
            act.wait_ge(s["mixed"], 6)
            act.activation(c.thin[0:DH, 0, :], c.thin[0:DH, 0, :], ACT.Tanh).then_inc(s["thin_ready"], 1)
            act.activation(c.thin[:, 1, :], c.thin[:, 1, :], ACT.Sigmoid).then_inc(s["thin_ready"], 1)
            copies(8, N_RW)
            act.wait_ge(s["vecs_loaded"], 16)
            for which, bias in ((LW, c.w0), (A_, c.a0)):
                for j in range(PAIRS):
                    bank = c.ps[(4 if which == LW else 6) + j // 2]
                    act.wait_ge(s["small_ready"], 1 if which == LW else 2)
                    act.activation(rw3[:, which, j], bank[:, (j % 2) * S:(j % 2 + 1) * S], ACT.Sigmoid,
                                   bias=bias[:, j:j + 1]).then_inc(s["z_ready"], 1)
            copies(N_RW, N_RW + 4)
            act.wait_ge(s["heads_summed"], 1)
            for b in range(2):
                act.activation(rw[:, E1, b * 512:(b + 1) * 512], c.ps[4 + b][:], ACT.Sqrt).then_inc(s["norm_ready"], 1)
            for t in range(NT):
                act.wait_ge(s["g_ready"], t + 1)
                last = act.activation(c.gt[:, t], c.ps[6 + t][:], ACT.Copy)
            last.then_inc(s["act_step"], 1)
            copies(N_RW + 4, N_RW + 6)
            act.wait_ge(s["centred"], 1)
            act.wait_ge(s["kk_normed"], 1)
            act.activation(rw[:, E1], rw[:, LW], ACT.Exp, scale=-DECAY).then_inc(s["exps_ready"], 1)
            act.activation(rw[:, E2], rw[:, LW], ACT.Exp, scale=DECAY).then_inc(s["exps_ready"], 1)
            act.activation(c.rw_small[:, 1], c.rw_small[:, 0], ACT.Exp, scale=DECAY).then_inc(s["exps_ready"], 1)
            act.activation(c.rw_small[:, 2], c.rw_small[:, 0], ACT.Exp, scale=-DECAY).then_inc(s["exps_ready"], 1)
            copies(N_RW + 6, len(jobs))

        @block.gpsimd
        def _(pool):
            def low(n):
                pool.wait_ge(s["unit_split"], n)
                ring.low(pool, n)

            pool.memset(c.raw2[:, :, 0:1], 0.0).then_inc(s["zeroed"], 1)
            pool.wait_ge(s["zeroed"], 1)
            for i in range(N_RW):
                pool.wait_ge(s["copied"], i + 1)
                if i >= 2:
                    pool.wait_ge(s["mixed"], i - 1)
                pool.tensor_tensor(c.diff[:, i % 2], c.raw2[:, i % 2, 0:S], c.raw2[:, i % 2, 1:], ALU.subtract
                                   ).then_inc(s["diffed"], 1)
            for n in range(4):
                if n % 2 == 0:
                    low(POOL_FROM + n // 2)
                pool.wait_ge(s["copied"], N_RW + n + 1)
                if n >= 2:
                    pool.wait_ge(s["rotated"], n - 1)
                pool.tensor_tensor(c.work[:, (n % 2) * S:(n % 2 + 1) * S], ret_raw[:, n], c.ret_cos, ALU.mult
                                   ).then_inc(s["cos_done"], 1)
                pool.wait_ge(s["cos_done"], n + 1)
                pool.wait_ge(s["sin_done"], n + 1)
                pool.tensor_tensor(c.ret_rot[:, n], c.ret_rot[:, n], c.work[:, (n % 2) * S:(n % 2 + 1) * S], ALU.add
                                   ).then_inc(s["rotated"], 1)
            for n in range(POOL_FROM + 2, N_UNITS):
                low(n)

        @block.vector
        def _(dve):
            norm_vector(dve, c, s["gain_loaded"], s["root_ready"], s["rstd_ready"], s["h_ready"])
            ring.low(dve, 0)
            turned_low_vector(dve, c, c.hT_parts[:, 0], c.hT_parts[:, 1], s["hT_high"], s["hT_ready"])
            for n in range(1, RING):
                ring.low(dve, n)
            dve.wait_ge(s["vecs_loaded"], 16)
            for i in range(N_RW):
                to = jobs[i][3]
                m = mu_of[to[0]] + to[1]
                dve.wait_ge(s["diffed"], i + 1)
                dve.scalar_tensor_tensor(mixed_place(to), c.diff[:, i % 2], c.mu[:, m:m + 1], c.raw2[:, i % 2, 1:],
                                         ALU.mult, ALU.add).then_inc(s["mixed"], 1)
                n = jobs[i][0] + RING
                if i == last_job[jobs[i][0]] and n < POOL_FROM:
                    ring.low(dve, n)
            steps = 0

            def step(ins):
                nonlocal steps
                steps += 1
                ins.then_inc(s["dve_step"], 1)
                dve.wait_ge(s["dve_step"], steps)

            dve.wait_ge(s["mixed"], N_RW)
            for j in range(PAIRS):
                last = dve.tensor_scalar(rw3[:, KK, j], rw3[:, K_, j], c.k_k[:, j:j + 1], None, ALU.mult)
            step(last)
            dve.tensor_tensor(rw[:, E2], rw[:, KK], rw[:, KK], ALU.mult).then_inc(s["kk_ready"], 1)
            for t in range(NT):
                dve.wait_ge(s["v_turned"], t + 1)
                dve.tensor_copy(c.vt[:, t], c.ps[2 + t][:]).then_inc(s["v_copied"], 1)
            for n in range(4):
                dve.wait_ge(s["swapped"], n + 1)
                dve.tensor_tensor(c.ret_rot[:, n], c.ps[2 + n % 2][:, 0:S], c.ret_sin, ALU.mult).then_inc(s["sin_done"], 1)
            dve.wait_ge(s["z_ready"], 2 * PAIRS)
            dve.wait_ge(s["rotated"], 4)
            for j in range(PAIRS):
                for ch in range(NT):
                    last = dve.tensor_tensor_scan(rw4[:, KR, j, ch], c.ones, rw4[:, LW, j, ch], 0.0,
                                                  ALU.mult, ALU.add)
            step(last)
            step(dve.tensor_copy(c.rw_small[:, 0], rw4[:, KR, :, :, P // 2 - 1]))
            flat = rw[:, KR].rearrange("p (a n) -> p a n", n=P)
            mid = c.rw_small[:, 0].rearrange("p j c -> p (j c)").unsqueeze(2).to_broadcast([P, PAIRS * NT, P])
            dve.tensor_tensor(rw[:, LW].rearrange("p (a n) -> p a n", n=P), flat, mid, ALU.subtract
                              ).then_inc(s["centred"], 1)
            for j in range(PAIRS):
                last = dve.tensor_scalar(rw3[:, KH, j], rw3[:, A_, j], -1.0, c.k_a[:, j:j + 1], ALU.add, ALU.mult)
            step(last)
            step(dve.scalar_tensor_tensor(rw[:, K_], rw[:, KH], 1.0, rw[:, K_], ALU.add, ALU.mult))
            step(dve.tensor_tensor(rw[:, BH], rw[:, R_], rw[:, K_], ALU.mult))
            for j in range(PAIRS):
                last = dve.tensor_scalar(rw3[:, BH, j], rw3[:, BH, j], c.r_k[:, j:j + 1], None, ALU.mult)
            last.then_inc(s["rk_ready"], 1)
            dve.wait_ge(s["norm_ready"], 2)
            step(dve.tensor_scalar(rw[:, E1], rw[:, E1], 1e-12, None, ALU.max))
            step(dve.reciprocal(rw[:, E1], rw[:, E1]))
            dve.tensor_tensor(rw[:, KK], rw[:, KK], rw[:, E1], ALU.mult).then_inc(s["kk_normed"], 1)
            dve.wait_ge(s["kk_normed"], 1)
            step(dve.tensor_tensor(rw[:, A_], rw[:, A_], rw[:, KK], ALU.mult))
            dve.wait_ge(s["bonus_ready"], 1)
            step(dve.tensor_copy(c.bonus[:].rearrange("p t h -> p (t h)"), c.ps[3][:, 0:NT * NH]))
            dve.wait_ge(s["exps_ready"], 4)
            step(dve.tensor_tensor(rw[:, BH], rw[:, A_], rw[:, E2], ALU.mult))
            step(dve.tensor_tensor(rw[:, KH], rw[:, K_], rw[:, E2], ALU.mult))
            for ch in range(NT):
                last = dve.tensor_tensor(kr[:, :, ch, 1, :], rw4[:, R_, :, ch], rw4[:, E1, :, ch], ALU.mult)
                dve.tensor_tensor(kr[:, :, ch, 0, 1:], rw4[:, KK, :, ch, 1:], rw4[:, E1, :, ch, 0:P - 1], ALU.mult)
                last = dve.tensor_tensor(kr[:, :, ch, 0, 0:1], rw4[:, KK, :, ch, 0:1],
                                         c.rw_small[:, 1, :, ch].unsqueeze(2), ALU.mult)
            step(last)
            step(dve.tensor_tensor(c.rw_small[:, 0, :, 0], rw4[:, E1, :, 0, P - 1], c.rw_small[:, 2, :, 1], ALU.mult))

        @block.tensor
        def _(pe):
            turn_tensor(pe, c, c.h, s["h_ready"], s["turned"])
            pe.wait_ge(s["hT_ready"], 2 * NT)

            def project(lo, hi, after=None):
                for i in range(lo, hi):
                    unit, col, kind, to = jobs[i]
                    bank = c.ps[i % 2]
                    pe.wait_ge(s["unit_split"], unit + 1)
                    if i >= 2:
                        pe.wait_ge(s["copied"], i - 1)
                    if kind in ("rw", "ret"):
                        for k in range(KT):
                            last = matmul3(pe, bank[:, 0:S], ring.operand(unit, k * S + col, P), both(c.hT_parts, k),
                                           k == 0, k == KT - 1)
                    else:
                        for t in range(NT):
                            for k in range(KT):
                                last = matmul3(pe, bank[:, t * S:(t + 1) * S], both(c.hT_parts, k, slice(t * P, (t + 1) * P)),
                                               ring.operand(unit, k * S, S), k == 0, k == KT - 1)
                    last.then_inc(s["projected"], 1)
                    if after:
                        after(i)

            project(0, N_RW)
            pe.wait_ge(s["thin_ready"], 2)
            pe.wait_ge(s["low_loaded"], 48)
            for half, first_bank in ((0, 4), (1, 6)):
                rows = slice(half * DH, (half + 1) * DH)
                for j in range(PAIRS):
                    last = pe.matmul(c.ps[first_bank + j // 2][:, (j % 2) * S:(j % 2 + 1) * S],
                                     c.low_rank[rows, j * P:(j + 1) * P], c.thin[rows, 0, :], start=True, stop=True)
                last.then_inc(s["small_ready"], 1)
            pe.wait_ge(s["mixed"], N_RW)
            for t in range(NT):
                for j in range(PAIRS):
                    last = pe.transpose(c.ps[2 + t][:, j * P:(j + 1) * P], rw3[:, V_, j, t * P:(t + 1) * P], c.ident)
                last.then_inc(s["v_turned"], 1)

            def swap(n):
                pe.wait_ge(s["copied"], N_RW + n + 1)
                pe.wait_ge(s["v_copied"], NT)
                if n >= 2:
                    pe.wait_ge(s["sin_done"], n - 1)
                pe.matmul(c.ps[2 + n % 2][:, 0:S], c.ret_swap, ret_raw[:, n], start=True, stop=True).then_inc(s["swapped"], 1)

            project(N_RW, N_RW + 4, lambda i: swap(i - N_RW - 1) if i > N_RW else None)
            swap(3)
            pe.wait_ge(s["kk_ready"], 1)
            pe.wait_ge(s["z_ready"], 2 * PAIRS)
            for j in range(PAIRS):
                last = pe.matmul(c.ps[4 + j // 2][:, (j % 2) * S:(j % 2 + 1) * S], c.same_head, rw3[:, E2, j],
                                 start=True, stop=True)
            last.then_inc(s["heads_summed"], 1)
            for t in range(NT):
                pe.matmul(c.ps[6 + t][:], c.thin[:, 1, t * P:(t + 1) * P], c.low_rank[:, RW_W:],
                          start=True, stop=True).then_inc(s["g_ready"], 1)
            project(N_RW + 4, N_RW + 6)
            pe.wait_ge(s["rk_ready"], 1)
            pe.wait_ge(s["sin_done"], 4)
            for t in range(NT):
                for j in range(PAIRS):
                    at = t * NH + 2 * j
                    last = pe.matmul(c.ps[3][:, at:at + 2], rw3[:, BH, j, t * P:(t + 1) * P], c.head_pair,
                                     start=True, stop=True)
            last.then_inc(s["bonus_ready"], 1)
            project(N_RW + 6, len(jobs))
    end_phase()
    ctx.close()


def rw_scan_phase(nc, c, lnx_g, lnx_b):
    s, end_phase = semaphores(nc, "rw_scan", "rows_loaded zeroed scored kept scored_t kept_t masked first_step inverse0 low_ready "
                            "inner_ready inner_copied outer_ready updated b_turned b_copied rhs_ready rhs_copied "
                            "w_ready w_copied state_ready state_copied y_ready centred summed y_done "
                            "y_turned y_copied squared factors_step factors_ready")
    ctx = ExitStack()
    arena = ctx.enter_context(nc.sbuf_tensor("triangles", [P, UNITS * (512 + 3 * P)], F32))
    at = 0

    def take(n):
        nonlocal at
        at += n
        return arena[:, at - n:at]

    pairs_of = take(UNITS * 512).rearrange("p (u n) -> p u n", u=UNITS)
    a_rows = take(UNITS * P).rearrange("p (u n) -> p u n", u=UNITS)
    z = take(UNITS * P).rearrange("p (u n) -> p u n", u=UNITS)
    x = take(UNITS * P).rearrange("p (u n) -> p u n", u=UNITS)
    rw3 = c.rw[:].rearrange("p b (j n) -> p b j n", j=PAIRS)
    rw = c.rw[:]
    kr = rw[:, KR:KR + 2, :].rearrange("p a n -> p (a n)").rearrange("p (j c n) -> p j c n", j=PAIRS, c=NT)
    low = rw[:, R_, 0:2 * 512].rearrange("p (b n) -> p b n", b=2)
    inner = rw[:, K_, 0:2 * 512].rearrange("p (b n) -> p b n", b=2)
    b_rows, h_rows = rw[:, V_, 0:512], rw[:, V_, 512:1024]
    rhs = rw[:, A_, 0:1024].rearrange("p (c n) -> p c n", c=NT)
    w_rows = rw[:, LW, 0:1024].rearrange("p (c n) -> p c n", c=NT)
    state = rw[:, KK, 0:512]
    y = rw[:, E1].rearrange("p (c n) -> p c n", c=NT)
    factor, addend = c.gt[:], rw[:, E2].rearrange("p (c n) -> p c n", c=NT)
    squares = c.work[:, 2 * RW_W:4 * RW_W].rearrange("p (c n) -> p c n", c=NT)
    lnx = c.work[:, 0:2 * RW_W].rearrange("p (a n) -> p a n", a=2)

    units = [(ch, e, j) for ch in range(NT) for e in range(2) for j in range(PAIRS)]
    QUADS = UNITS // 4

    def rows_of(u):
        e = units[u][1]
        return slice(e * DH, (e + 1) * DH)

    def head_cols(u):
        _, e, j = units[u]
        return slice(j * P + e * DH, j * P + (e + 1) * DH)

    def quad(buf, q):
        return buf[:, 4 * q:4 * q + 4, :]

    def bank4(b):
        return c.ps[b][:].rearrange("p (u n) -> p u n", u=4)

    with nc.Block() as block:
        @block.sync
        def _(sp):
            for i, v in enumerate((lnx_g, lnx_b)):
                sp.dma_start(lnx[:, i], v.unsqueeze(0).to_broadcast([P, RW_W])).then_inc(s["rows_loaded"], 16)

        @block.gpsimd
        def _(pool):
            pool.memset(pairs_of[:, 0:4], 0.0).then_inc(s["zeroed"], 1)
            pool.memset(a_rows, 0.0).then_inc(s["zeroed"], 1)
            for q in range(1, QUADS):
                pool.memset(pairs_of[:, 4 * q:4 * q + 4], 0.0).then_inc(s["zeroed"], 1)
            for n in range((LEVELS - 1) * QUADS):
                level, q = n // QUADS + 1, n % QUADS
                pool.wait_ge(s["kept_t"], q + 1)
                if n >= 2:
                    pool.wait_ge(s["inner_ready"], n - 1)
                m = c.levels[level].unsqueeze(1).to_broadcast([P, 4, P])
                pool.tensor_tensor(low[:, n % 2].rearrange("p (u n) -> p u n", u=4), quad(a_rows, q), m, ALU.mult
                                   ).then_inc(s["low_ready"], 1)
            pool.wait_ge(s["rows_loaded"], 32)
            for ch in range(NT):
                wide = c.bonus[:, ch].unsqueeze(2).to_broadcast([P, NH, DH])
                pool.tensor_tensor(addend[:, ch].rearrange("p (h d) -> p h d", d=DH),
                                   c.vt[:, ch].rearrange("p (h d) -> p h d", d=DH), wide, ALU.mult).then_inc(s["factors_step"], 1)
                pool.wait_ge(s["factors_step"], 3 * ch + 1)
                pool.tensor_tensor(addend[:, ch], addend[:, ch], lnx[:, 1], ALU.add).then_inc(s["factors_step"], 1)
                pool.wait_ge(s["factors_step"], 3 * ch + 2)
                pool.tensor_tensor(addend[:, ch], addend[:, ch], factor[:, ch], ALU.mult).then_inc(s["factors_step"], 1)
                pool.wait_ge(s["factors_step"], 3 * ch + 3)
                pool.tensor_tensor(factor[:, ch], factor[:, ch], lnx[:, 0], ALU.mult).then_inc(s["factors_ready"], 1)

        @block.scalar
        def _(act):
            for n in range((LEVELS - 1) * QUADS):
                act.wait_ge(s["inner_ready"], n + 1)
                if n >= 2:
                    act.wait_ge(s["outer_ready"], n - 1)
                act.activation(inner[:, n % 2], c.ps[2 + n % 2][:], ACT.Copy).then_inc(s["inner_copied"], 1)
            for i, dst in enumerate((b_rows, h_rows)):
                act.wait_ge(s["b_turned"], i + 1)
                act.activation(dst, c.ps[2 + i][:], ACT.Copy).then_inc(s["b_copied"], 1)
            for ch in range(NT):
                act.wait_ge(s["w_ready"], ch + 1)
                act.activation(w_rows[:, ch], c.ps[1][:], ACT.Copy).then_inc(s["w_copied"], 1)
            for ch in range(NT):
                act.wait_ge(s["centred"], ch + 1)
                act.activation(squares[:, ch], y[:, ch], ACT.Square).then_inc(s["squared"], 1)
                act.wait_ge(s["summed"], ch + 1)
                act.activation(c.st[:, 16 + 8 * ch:24 + 8 * ch], c.st[:, 8 * ch:8 * ch + 8], ACT.Sqrt, bias=c.rw_eps,
                               scale=1.0 / DH).then_inc(s["squared"], 1)

        @block.vector
        def _(dve):
            for q in range(QUADS):
                for u in range(4 * q, 4 * q + 4):
                    dve.wait_ge(s["scored"], u + 1)
                    dve.wait_ge(s["zeroed"], 1 if q == 0 else q + 2)
                    dve.copy_predicated(pairs_of[:, u], c.rw_mask.bitcast(mybir.dt.uint32), c.ps[u % 2][:]).then_inc(s["kept"], 1)
                dve.wait_ge(s["scored_t"], q + 1)
                dve.wait_ge(s["zeroed"], 2)
                mask = c.rw_mask_t.bitcast(mybir.dt.uint32).unsqueeze(1).to_broadcast([P, 4, P])
                dve.copy_predicated(quad(a_rows, q), mask, bank4(2 + q % 2)).then_inc(s["kept_t"], 1)
                dve.wait_ge(s["kept"], 4 * q + 4)
                dve.wait_ge(s["kept_t"], q + 1)
                m = c.minus_level0_t.unsqueeze(1).to_broadcast([P, 4, P])
                dve.tensor_tensor(quad(z, q), pairs_of[:, 4 * q:4 * q + 4, 0:P], m, ALU.mult).then_inc(s["first_step"], 1)
                m = c.levels[0].unsqueeze(1).to_broadcast([P, 4, P])
                dve.tensor_tensor(quad(x, q), quad(a_rows, q), m, ALU.mult).then_inc(s["first_step"], 1)
                dve.wait_ge(s["first_step"], 2 * q + 2)
                eye = c.ident.unsqueeze(1).to_broadcast([P, 4, P])
                dve.tensor_tensor(quad(z, q), quad(z, q), eye, ALU.add).then_inc(s["inverse0"], 1)
                dve.tensor_tensor(quad(x, q), eye, quad(x, q), ALU.subtract).then_inc(s["inverse0"], 1)
            for n in range((LEVELS - 1) * QUADS):
                q = n % QUADS
                dve.wait_ge(s["outer_ready"], n + 1)
                dve.tensor_tensor(quad(z, q), quad(z, q), bank4(4 + n % 2), ALU.subtract).then_inc(s["updated"], 1)
                if n < (LEVELS - 2) * QUADS:
                    dve.tensor_tensor(quad(x, q), quad(x, q), bank4(6 + n % 2), ALU.subtract).then_inc(s["updated"], 1)
            for ch in range(NT):
                dve.wait_ge(s["rhs_ready"], ch + 1)
                dve.tensor_scalar(rhs[:, ch], c.ps[0][:], -1.0, None, ALU.mult).then_inc(s["rhs_copied"], 1)
                if ch == 0:
                    dve.wait_ge(s["state_ready"], 1)
                    for j in range(PAIRS):
                        last = dve.scalar_tensor_tensor(state[:, j * P:(j + 1) * P], c.ps[6][:, j * P:(j + 1) * P],
                                                        c.rw_small[:, 0, j, 0:1], c.same_head, ALU.mult, ALU.mult)
                    last.then_inc(s["state_copied"], 1)
            steps = 0

            def step(ins):
                nonlocal steps
                steps += 1
                ins.then_inc(s["first_step"], 1)
                dve.wait_ge(s["first_step"], 2 * QUADS + steps)

            def heads(a):
                return a.rearrange("p (h d) -> p h d", d=DH)

            def wide(a):
                return a.unsqueeze(2).to_broadcast([P, NH, DH])

            for ch in range(NT):
                row = y[:, ch]
                sums, means, rstd = (c.st[:, at + 8 * ch:at + 8 * ch + 8] for at in (0, 48, 32))
                dve.wait_ge(s["y_ready"], ch + 1)
                step(dve.tensor_copy(row, c.ps[4 + ch][:]))
                step(dve.tensor_reduce(means, heads(row), AX, ALU.add))
                step(dve.tensor_scalar(means, means, 1.0 / DH, None, ALU.mult))
                dve.tensor_tensor(heads(row), heads(row), wide(means), ALU.subtract).then_inc(s["centred"], 1)
                dve.wait_ge(s["squared"], 2 * ch + 1)
                dve.tensor_reduce(sums, heads(squares[:, ch]), AX, ALU.add).then_inc(s["summed"], 1)
                dve.wait_ge(s["squared"], 2 * ch + 2)
                step(dve.reciprocal(rstd, c.st[:, 16 + 8 * ch:24 + 8 * ch]))
                step(dve.tensor_tensor(heads(row), heads(row), wide(rstd), ALU.mult))
                dve.wait_ge(s["factors_ready"], ch + 1)
                step(dve.tensor_tensor(row, row, factor[:, ch], ALU.mult))
                dve.tensor_tensor(row, row, addend[:, ch], ALU.add).then_inc(s["y_done"], 1)
            for t in range(NT):
                dve.wait_ge(s["y_turned"], t + 1)
                dve.tensor_copy(c.y_rw[:, :, t * P:(t + 1) * P], bank4(2 + t)).then_inc(s["y_copied"], 1)

        @block.tensor
        def _(pe):
            for q in range(QUADS):
                for u in range(4 * q, 4 * q + 4):
                    ch, e, j = units[u]
                    rows, toks = rows_of(u), slice(ch * P, (ch + 1) * P)
                    keep_clock(pe, c, c.ps[4][:, 0:P], 2)
                    if u >= 2:
                        pe.wait_ge(s["kept"], u - 1)
                    pe.matmul(c.ps[u % 2][:, 0:S], rw3[rows, BH, j, toks], kr[rows, j, ch], start=True, stop=True)
                    pe.matmul(c.ps[u % 2][:, S:2 * S], rw3[rows, KH, j, toks], kr[rows, j, ch], start=True, stop=True
                              ).then_inc(s["scored"], 1)
                if q >= 2:
                    pe.wait_ge(s["kept_t"], q - 1)
                for i, u in enumerate(range(4 * q, 4 * q + 4)):
                    ch, e, j = units[u]
                    rows, toks = rows_of(u), slice(ch * P, (ch + 1) * P)
                    last = pe.matmul(c.ps[2 + q % 2][:, i * P:(i + 1) * P], kr[rows, j, ch, 0:P], rw3[rows, BH, j, toks],
                                     start=True, stop=True)
                last.then_inc(s["scored_t"], 1)

            TOTAL = (LEVELS - 1) * QUADS

            def n_updates(n):
                both = (LEVELS - 2) * QUADS
                return 2 * (n + 1) if n < both else 2 * both + (n + 1 - both)

            def inner_product(n):
                q = n % QUADS
                pe.wait_ge(s["low_ready"], n + 1)
                if n < QUADS:
                    pe.wait_ge(s["inverse0"], 2 * q + 2)
                else:
                    pe.wait_ge(s["updated"], n_updates(n - QUADS))
                pe.wait_ge(s["kept_t"], QUADS)
                if n >= 2:
                    pe.wait_ge(s["inner_copied"], n - 1)
                for i in range(4):
                    last = pe.matmul(c.ps[2 + n % 2][:, i * P:(i + 1) * P], low[:, n % 2, i * P:(i + 1) * P],
                                     z[:, 4 * q + i], start=True, stop=True)
                last.then_inc(s["inner_ready"], 1)

            def outer_product(n):
                q = n % QUADS
                pe.wait_ge(s["inner_copied"], n + 1)
                if n >= 2:
                    pe.wait_ge(s["updated"], n_updates(n - 2))
                for i in range(4):
                    last = pe.matmul(c.ps[4 + n % 2][:, i * P:(i + 1) * P], x[:, 4 * q + i],
                                     inner[:, n % 2, i * P:(i + 1) * P], start=True, stop=True)
                if n < (LEVELS - 2) * QUADS:
                    for i in range(4):
                        last = pe.matmul(c.ps[6 + n % 2][:, i * P:(i + 1) * P], inner[:, n % 2, i * P:(i + 1) * P],
                                         x[:, 4 * q + i], start=True, stop=True)
                last.then_inc(s["outer_ready"], 1)

            inner_product(0)
            for n in range(TOTAL):
                if n + 1 < TOTAL:
                    inner_product(n + 1)
                outer_product(n)

            pe.wait_ge(s["inner_copied"], TOTAL)
            for i, which in enumerate((BH, KH)):
                for j in range(PAIRS):
                    last = pe.transpose(c.ps[2 + i][:, j * P:(j + 1) * P], rw3[:, which, j, 0:P], c.ident)
                last.then_inc(s["b_turned"], 1)
            for ch in range(NT):
                us = range(ch * NH, (ch + 1) * NH)
                if ch == 0:
                    pe.wait_ge(s["kept"], UNITS)
                else:
                    pe.wait_ge(s["rhs_copied"], ch)
                    pe.wait_ge(s["state_copied"], 1)
                    for j in range(PAIRS):
                        pe.matmul(c.ps[0][:, j * P:(j + 1) * P], kr[:, j, ch, 0:P], state[:, j * P:(j + 1) * P],
                                  start=(j == 0), stop=False, skip_group_check=True)
                for u in us:
                    last = pe.matmul(c.ps[0][:, head_cols(u)], pairs_of[:, u, S:S + P], c.vt[:, ch, head_cols(u)],
                                     start=(ch == 0), stop=True, skip_group_check=True)
                last.then_inc(s["rhs_ready"], 1)
                pe.wait_ge(s["rhs_copied"], ch + 1)
                pe.wait_ge(s["updated"], n_updates(TOTAL - 1))
                if ch:
                    pe.wait_ge(s["w_copied"], ch)
                for u in us:
                    last = pe.matmul(c.ps[1][:, head_cols(u)], z[:, u], rhs[:, ch, head_cols(u)], start=True, stop=True)
                last.then_inc(s["w_ready"], 1)
                pe.wait_ge(s["w_copied"], ch + 1)
                if ch == 0:
                    pe.wait_ge(s["b_copied"], 2)
                    for j in range(PAIRS):
                        cols = slice(j * P, (j + 1) * P)
                        pe.matmul(c.ps[6][:, cols], b_rows[:, cols], w_rows[:, 0, cols], start=True, stop=False)
                        last = pe.matmul(c.ps[6][:, cols], h_rows[:, cols], c.vt[:, 0, cols], start=False, stop=True)
                    last.then_inc(s["state_ready"], 1)
                else:
                    for j in range(PAIRS):
                        pe.matmul(c.ps[4 + ch][:, j * P:(j + 1) * P], kr[:, j, ch, P:2 * P], state[:, j * P:(j + 1) * P],
                                  start=(j == 0), stop=False, skip_group_check=True)
                for u in us:
                    pe.matmul(c.ps[4 + ch][:, head_cols(u)], pairs_of[:, u, P:2 * P], w_rows[:, ch, head_cols(u)],
                              start=(ch == 0), stop=False, skip_group_check=True)
                    last = pe.matmul(c.ps[4 + ch][:, head_cols(u)], pairs_of[:, u, S + P:2 * S],
                                     c.vt[:, ch, head_cols(u)], start=False, stop=True, skip_group_check=True)
                last.then_inc(s["y_ready"], 1)
            for t in range(NT):
                pe.wait_ge(s["y_done"], t + 1)
                for j in range(PAIRS):
                    last = pe.transpose(c.ps[2 + t][:, j * P:(j + 1) * P], y[:, t, j * P:(j + 1) * P], c.ident)
                last.then_inc(s["y_turned"], 1)
    end_phase()
    ctx.close()


def mix_phase(nc, c, sg_ln_g, sg_ln_b, sg_w, sg_b, mix_w, w_out):
    s, end_phase = semaphores(nc, "mix", "rows_loaded ws_loaded scored decayed ret_used ret_squared "
                        "ret_done ws_turned ws_copied sg_step sg_squared sg_rooted sg_normed sg_ready sg_done y_turned "
                        "y_copied gated sig_ready multiplied dve_step merged_step merged_high y_high "
                        "out_ready residual_done" + RING_NAMES)
    STEPS = KT * N_BRANCH
    N_UNITS = STEPS + KT // 2
    ctx = ExitStack()

    def sb(name, shape, dtype=F32):
        return ctx.enter_context(nc.sbuf_tensor(name, shape, dtype))

    ring = Ring(nc, ctx, "mix", s, s["gated"], [n + 1 for n in range(N_UNITS)])
    y_parts = sb("branches_T", [P, 2, N_BRANCH, 4, S], F32R)
    merged_parts = sb("merged_parts", [P, 2, KT, S], F32R)
    sc = sb("ret_scores", [P, 2, 384])
    merged = c.h[:].rearrange("p t (f n) -> p (t f) n", n=S)
    sg = c.h[:].rearrange("p t (x n) -> p t x n", x=2)
    ws, wsT = sb("sg_rows", [P, 4, P])[:], sb("sg_rows_T", [P, 4, P])[:]
    ln = c.work[:, 0:2 * SG_W].rearrange("p (a n) -> p a n", a=2)
    sig = c.work[:, SG_W * 2:SG_W * 2 + 2 * 512].rearrange("p (b n) -> p b n", b=2)
    sq = c.vt[:]

    def width(n):
        return MIX_COLS if n < STEPS else 2 * D

    steps_of = [(f, b) for f in range(KT) for b in range(N_BRANCH)]

    with nc.Block() as block:
        @block.sync
        def _(sp):
            sp.dma_start(ws, sg_w.rearrange("g i j -> i g j")).then_inc(s["ws_loaded"], 16)
            for i, v in enumerate((sg_ln_g, sg_ln_b)):
                sp.dma_start(ln[:, i], v.unsqueeze(0).to_broadcast([P, SG_W])).then_inc(s["rows_loaded"], 16)
            sp.dma_start(c.st[:, 48:52], sg_b.rearrange("g i -> i g"), allow_slow_non_contiguous=True
                         ).then_inc(s["rows_loaded"], 16)
            for n in range(N_UNITS):
                ring.load(sp, n, mix_w[n * P:(n + 1) * P, :] if n < STEPS else w_out[(n - STEPS) * P:(n - STEPS + 1) * P, :])

        @block.scalar
        def _(act):
            for t in range(NT):
                act.wait_ge(s["sg_step"], t + 1)
                act.activation(sq[:, t], sg[:, t, 1], ACT.Square, accum_out=c.st[:, 8 + t:9 + t]).then_inc(s["sg_squared"], 1)
            act.wait_ge(s["sg_squared"], NT)
            act.activation(c.st[:, 12:14], c.st[:, 8:10], ACT.Sqrt, bias=c.eps, scale=1.0 / SG_W).then_inc(s["sg_rooted"], 1)
            for n in range(2):
                ring.high(act, n, width(n))
            act.activation(y_parts[:, 0, 0], c.y_rw, ACT.Copy).then_inc(s["y_high"], 1)
            for t in range(NT):
                act.wait_ge(s["ret_used"], RET_H)
                act.wait_ge(s["sg_rooted"], 1)
                act.activation(sq[:, t], c.ps[2 + t][:], ACT.Square).then_inc(s["ret_squared"], 1)
            act.wait_ge(s["ret_done"], 1)
            act.activation(c.st[:, 24:32], c.st[:, 16:24], ACT.Sqrt, bias=c.eps, scale=1.0 / RET_V).then_inc(s["ret_squared"], 1)
            for n in range(2, RING):
                ring.high(act, n, width(n))
            for i in range(2 * NT):
                t = i % NT
                act.wait_ge(s["y_turned"], i + 1)
                bank = c.ps[(2, 3, 6, 7)[i]][:].rearrange("p (k n) -> p k n", k=4)
                act.activation(y_parts[:, 0, 1 + i // NT, :, t * P:(t + 1) * P], bank, ACT.Copy).then_inc(s["y_high"], 1)
            for n in range(STEPS):
                act.wait_ge(s["gated"], n + 1)
                if n >= 2:
                    act.wait_ge(s["multiplied"], n - 1)
                act.activation(sig[:, n % 2, 0:S], c.ps[n % 2][:, 0:S], ACT.Sigmoid).then_inc(s["sig_ready"], 1)
                ring.high(act, n + RING, width(n + RING))
            for n in range(STEPS + RING, N_UNITS):
                ring.high(act, n, width(n))

        @block.gpsimd
        def _(pool):
            for n in range(RING):
                ring.low(pool, n, width(n))

        @block.vector
        def _(dve):
            steps = 0

            def step(ins):
                nonlocal steps
                steps += 1
                ins.then_inc(s["dve_step"], 1)
                dve.wait_ge(s["dve_step"], steps)

            v = sg[:, :, 1]
            step(dve.tensor_reduce(c.st[:, 0:NT], v, AX, ALU.add))
            step(dve.tensor_scalar(c.st[:, 0:NT], c.st[:, 0:NT], 1.0 / SG_W, None, ALU.mult))
            for t in range(NT):
                dve.tensor_scalar(v[:, t], v[:, t], c.st[:, t:t + 1], None, ALU.subtract).then_inc(s["sg_step"], 1)
            for h in range(RET_H):
                dve.wait_ge(s["scored"], h + 1)
                if h >= 2:
                    dve.wait_ge(s["ret_used"], h - 1)
                dve.tensor_tensor(sc[:, h % 2], c.ps[h % 2][:, 0:384], c.ret_decays[h], ALU.mult).then_inc(s["decayed"], 1)
            dve.wait_ge(s["sg_rooted"], 1)
            step(dve.reciprocal(c.st[:, 14:16], c.st[:, 12:14]))
            dve.wait_ge(s["rows_loaded"], 48)
            for t in range(NT):
                step(dve.scalar_tensor_tensor(v[:, t], v[:, t], c.st[:, 14 + t:15 + t], ln[:, 0], ALU.mult, ALU.mult))
            dve.tensor_tensor(v, v, ln[:, 1].unsqueeze(1).to_broadcast([P, NT, SG_W]), ALU.add).then_inc(s["sg_normed"], 1)
            dve.wait_ge(s["ws_turned"], 1)
            dve.tensor_tensor(wsT, c.ps[6][:].rearrange("p (g n) -> p g n", g=4),
                              c.rw_mask[:, P:2 * P].unsqueeze(1).to_broadcast([P, 4, P]), ALU.mult).then_inc(s["ws_copied"], 1)
            dve.wait_ge(s["ret_squared"], NT)
            dve.tensor_reduce(c.st[:, 16:24], sq.rearrange("p t (h d) -> p (t h) d", d=RET_V), AX, ALU.add
                              ).then_inc(s["ret_done"], 1)
            dve.wait_ge(s["ret_squared"], NT + 1)
            step(dve.reciprocal(c.st[:, 32:40], c.st[:, 24:32]))
            for t in range(NT):
                wide = c.st[:, 32 + 4 * t:36 + 4 * t].unsqueeze(2).to_broadcast([P, RET_H, RET_V])
                last = dve.tensor_tensor(sq[:, t].rearrange("p (h d) -> p h d", d=RET_V),
                                         c.ps[2 + t][:].rearrange("p (h d) -> p h d", d=RET_V), wide, ALU.mult)
            step(last)
            dve.tensor_tensor(c.ret_g[:], sq, c.ret_g[:], ALU.mult).then_inc(s["ret_done"], 1)
            for t in range(NT):
                dve.wait_ge(s["sg_ready"], t + 1)
                for g in range(4):
                    cols = slice(g * P, (g + 1) * P)
                    last = dve.scalar_tensor_tensor(c.ret_v[:, t, cols], c.ps[4 + t][:, cols], c.st[:, 48 + g:49 + g],
                                                    sg[:, t, 0, cols], ALU.add, ALU.mult)
                last.then_inc(s["sg_done"], 1)
            dve.wait_ge(s["y_high"], 1)
            dve.tensor_tensor(y_parts[:, 1, 0], c.y_rw, plain(y_parts[:, 0, 0]), ALU.subtract).then_inc(s["y_copied"], 1)
            for i in range(2 * NT):
                t = i % NT
                dve.wait_ge(s["y_high"], i + 2)
                bank = c.ps[(2, 3, 6, 7)[i]][:].rearrange("p (k n) -> p k n", k=4)
                high, low = both(y_parts, 1 + i // NT, slice(None), slice(t * P, (t + 1) * P))
                dve.tensor_tensor(low, bank, plain(high), ALU.subtract).then_inc(s["y_copied"], 1)
            for n, (f, b) in enumerate(steps_of):
                dve.wait_ge(s["sig_ready"], n + 1)
                if b == 0:
                    dve.tensor_tensor(merged[:, f], sig[:, n % 2, 0:S], c.ps[n % 2][:, S:2 * S], ALU.mult).then_inc(s["multiplied"], 1)
                else:
                    before = sum(j for _, j in steps_of[:n - 1])
                    if before:
                        dve.wait_ge(s["merged_step"], before)
                    dve.tensor_tensor(sig[:, n % 2, S:2 * S], sig[:, n % 2, 0:S], c.ps[n % 2][:, S:2 * S], ALU.mult
                                      ).then_inc(s["multiplied"], 1)
                    dve.wait_ge(s["multiplied"], n + 1)
                    if b == 2:
                        dve.wait_ge(s["merged_step"], 3 * f + 1)
                    dve.tensor_tensor(merged[:, f], merged[:, f], sig[:, n % 2, S:2 * S], ALU.add).then_inc(s["merged_step"], 1)
                if b == 2:
                    high, low = both(merged_parts, f)
                    dve.wait_ge(s["merged_step"], 3 * f + 2)
                    dve.tensor_copy(high, merged[:, f]).then_inc(s["merged_high"], 1)
                    dve.wait_ge(s["merged_high"], f + 1)
                    dve.tensor_tensor(low, merged[:, f], plain(high), ALU.subtract).then_inc(s["merged_step"], 1)
                if n == 0:
                    dve.wait_ge(s["unit_split"], RING)
                ring.low(dve, n + RING, width(n + RING))
            for n in range(STEPS + RING, N_UNITS):
                ring.low(dve, n, width(n))
            for b in range(2 * NT):
                t, half = b // 2, b % 2
                dve.wait_ge(s["out_ready"], b + 1)
                cols = slice(half * 512, half * 512 + 512)
                dve.tensor_tensor(c.x[:, t, cols], c.ps[4 + b][:], c.x[:, t, cols], ALU.add).then_inc(s["residual_done"], 1)

        @block.tensor
        def _(pe):
            def ret_sum(h):
                cols = slice(h * RET_V, (h + 1) * RET_V)
                pe.wait_ge(s["decayed"], h + 1)
                pe.matmul(c.ps[2][:, cols], sc[:, h % 2, 0:P], c.ret_v[:, 0, cols], start=True, stop=True)
                pe.matmul(c.ps[3][:, cols], sc[:, h % 2, P:S], c.ret_v[:, 0, cols], start=True, stop=False)
                last = pe.matmul(c.ps[3][:, cols], sc[:, h % 2, S:384], c.ret_v[:, 1, cols], start=False, stop=True)
                last.then_inc(s["ret_used"], 1)

            for h in range(RET_H):
                rows, tile = slice((h % 2) * DH, (h % 2 + 1) * DH), h // 2
                if h >= 2:
                    pe.wait_ge(s["decayed"], h - 1)
                bank = c.ps[h % 2]
                pe.matmul(bank[:, 0:S], c.ret_rot[rows, 2 + tile, 0:P], c.ret_rot[rows, tile, :], start=True, stop=True)
                pe.matmul(bank[:, S:S + P], c.ret_rot[rows, 2 + tile, P:S], c.ret_rot[rows, tile, P:S],
                          start=True, stop=True).then_inc(s["scored"], 1)
                if h >= 1:
                    ret_sum(h - 1)
            ret_sum(RET_H - 1)

            def gate_part(n):
                pe.wait_ge(s["unit_split"], n + 1)
                if n >= 2:
                    pe.wait_ge(s["multiplied"], n - 1)
                for k in range(KT):
                    matmul3(pe, c.ps[n % 2][:, 0:S], ring.operand(n, k * P, P), both(c.hT_parts, k), k == 0, k == KT - 1)

            def branch_part(n, b):
                for k in range(4):
                    last = matmul3(pe, c.ps[n % 2][:, S:2 * S], ring.operand(n, (KT + k) * P, P), both(y_parts, b, k),
                                   k == 0, k == 3)
                last.then_inc(s["gated"], 1)

            pe.wait_ge(s["ws_loaded"], 16)
            for g in range(4):
                last = pe.transpose(c.ps[6][:, g * P:(g + 1) * P], ws[:, g], c.ident)
            last.then_inc(s["ws_turned"], 1)
            pe.wait_ge(s["decayed"], RET_H)
            for n in range(2):
                gate_part(n)
            pe.wait_ge(s["ws_copied"], 1)
            pe.wait_ge(s["sg_normed"], 1)
            for t in range(NT):
                for g in range(4):
                    cols = slice(g * P, (g + 1) * P)
                    last = pe.matmul(c.ps[4 + t][:, cols], wsT[:, g], sg[:, t, 1, cols], start=True, stop=True)
                last.then_inc(s["sg_ready"], 1)
            for i in range(2 * NT):
                t = i % NT
                if i < NT:
                    pe.wait_ge(s["ret_done"], 2)
                else:
                    pe.wait_ge(s["sg_done"], t + 1)
                src = (c.ret_g, c.ret_v)[i // NT]
                for k in range(4):
                    last = pe.transpose(c.ps[(2, 3, 6, 7)[i]][:, k * P:(k + 1) * P], src[:, t, k * P:(k + 1) * P], c.ident)
                last.then_inc(s["y_turned"], 1)
            pe.wait_ge(s["y_copied"], 2 * NT + 1)
            for n, (f, b) in enumerate(steps_of):
                if n >= 2:
                    gate_part(n)
                branch_part(n, b)
            for n in range(STEPS, N_UNITS):
                f0 = 2 * (n - STEPS)
                pe.wait_ge(s["merged_step"], 3 * (f0 + 2))
                pe.wait_ge(s["unit_split"], n + 1)
                for b in range(2 * NT):
                    t, half = b // 2, b % 2
                    for k in range(2):
                        last = matmul3(pe, c.ps[4 + b][:], both(merged_parts, f0 + k, slice(t * P, (t + 1) * P)),
                                       ring.operand(n, k * D + half * 512, 512), f0 + k == 0, f0 + k == KT - 1)
                    if n == N_UNITS - 1:
                        last.then_inc(s["out_ready"], 1)
                if n < N_UNITS - 1:
                    last.then_inc(s["gated"], 1)
    end_phase()
    ctx.close()


def second_block(nc, c, ctx, a, out):
    t = load_tables(nc, c, ctx, "second", second_constants(), a["constants2"])
    c.ret_swap, c.ret_cos, c.ret_sin = t["ret_swap"], t["ret_cos"], t["ret_sin"]
    c.ret_decays = [t[f"ret_decay{h}"] for h in range(RET_H)]
    c.rw_mask, c.rw_mask_t, c.minus_level0_t = t["rw_mask"], t["rw_mask_t"], t["minus_level0_t"]
    c.levels = [t[f"level{n}"] for n in range(LEVELS)]
    c.same_head, c.head_pair, c.rw_eps, c.ones = t["same_head"], t["head_pair"], t["rw_eps"], t["ones"]

    with nc.Fori(0, DEPTH) as l:
        with ExitStack() as mixer:
            second_buffers(nc, mixer, c)
            with ExitStack() as recurrence:
                recurrence_buffers(nc, recurrence, c)
                rw_project_phase(nc, c, a["norm1_g_2"][l], a["w_in_2"][l], a["vectors"][l], a["rw_w_up_2"][l],
                                 a["rw_a_up_2"][l], a["rw_g_up_2"][l])
                rw_scan_phase(nc, c, a["rw_lnx_g_2"][l].rearrange("h d -> (h d)"),
                              a["rw_lnx_b_2"][l].rearrange("h d -> (h d)"))
            mix_phase(nc, c, a["sg_ln_g_2"][l], a["sg_ln_b_2"][l], a["sg_w_s_2"][l], a["sg_b_2"][l], a["mix_w"][l],
                      a["w_out_2"][l])
        ffn_phase(nc, c, "conv_ffn", a["norm2_g_2"][l], a["conv_ffn"][l], 1.0, a["conv"][l])
    final_norm_phase(nc, c, "final", a["final_g_2"], out)


def chunked(gate, up, down):
    gate, up = (x.reshape(DEPTH, KT, P, N_CHUNK, 1, FF_W).transpose(0, 3, 4, 2, 1, 5).reshape(DEPTH, N_CHUNK, 1, P, -1)
                for x in (gate, up))
    down = down.reshape(DEPTH, N_CHUNK, 1, FF_W // P, P, D).transpose(0, 1, 2, 4, 3, 5).reshape(DEPTH, N_CHUNK, 1, P, -1)
    return np.concatenate([gate, up, down], 2).reshape(DEPTH, N_CHUNK * 3 * P, -1)


def by_partition(w):
    return w.reshape(DEPTH, KT, P, -1).transpose(0, 2, 1, 3).reshape(DEPTH, P, -1)


def laid_out(a):
    a = {k: np.asarray(v) for k, v in a.items()}
    tables = constants()
    a["constants_shared"] = np.concatenate([tables.pop(k) for k in SHARED], 1)
    a["constants"] = np.concatenate(list(tables.values()), 1)
    a["constants2"] = np.concatenate(list(second_constants().values()), 1)
    w_in = a["w_in"][:, :, w_in_columns()]
    a["w_in"] = np.concatenate([by_partition(w_in[:, :, col:col + n]) for col, n in WI_UNITS], 2)
    for name in ("w_out", "w_out_2"):
        a[name] = a[name].reshape(DEPTH, KT // 2, 2, P, D).transpose(0, 1, 3, 2, 4).reshape(DEPTH, KT // 2 * P, -1)
    names = ("rw_mu_2", "rw_w0_2", "rw_a0_2", "rw_k_k_2", "rw_k_a_2", "rw_r_k_2")
    a["vectors"] = np.concatenate([a.pop(n).reshape(DEPTH, -1, P).transpose(0, 2, 1) for n in names], 2)
    gate = a["w_in_2"][:, :, GATE_OFF:].reshape(DEPTH, KT, P, N_BRANCH, KT, P).transpose(0, 4, 3, 2, 1, 5)
    branch = a.pop("w_branch_2").reshape(DEPTH, N_BRANCH, 4, P, KT, P).transpose(0, 4, 1, 3, 2, 5)
    units = DEPTH, KT * N_BRANCH * P, -1
    a["mix_w"] = np.concatenate([gate.reshape(units), branch.reshape(units)], 2)
    a["w_in_2"] = np.concatenate([by_partition(a["w_in_2"][:, :, col:col + 2 * P]) for col in PROJECT_COLS], 1)
    conv = np.concatenate([a.pop("ffn_conv_w_2"), a.pop("ffn_conv_b_2")[:, None]], 1)
    a["conv"] = conv.reshape(DEPTH, 4, 2, N_CHUNK, 2, P).transpose(0, 3, 5, 2, 4, 1).reshape(DEPTH, N_CHUNK * P, CONV_W)
    for name in ("ffn1", "ffn2"):
        a[name] = chunked(*(a.pop(f"w_{name}_{part}") for part in ("gate", "up", "down")))
    up = a.pop("ffn_w_up_2")
    a["conv_ffn"] = chunked(up[:, :, :D_FF], up[:, :, D_FF:], a.pop("ffn_w_down_2"))
    return {k: np.ascontiguousarray(v) for k, v in a.items()}


def kernel(**inputs):
    import concourse.bacc as bacc
    from concourse.bass_utils import run_bass_kernel_spmd

    nc = bacc.Bacc("TRN2", target_bir_lowering=False, num_devices=1)
    arrays, aps = {}, {}
    for name, value in laid_out(inputs).items():
        arrays[f"in_{name}"] = value
        aps[name] = nc.dram_tensor(f"in_{name}", value.shape, mybir.dt.from_np(value.dtype), kind="ExternalInput").ap()
    out = nc.dram_tensor("out", (1, S, D), F32, kind="ExternalOutput").ap()
    build(nc, aps, out)
    result = run_bass_kernel_spmd(nc, [arrays], core_ids=[0])
    return result.results[0]["out"]
```
